# Optimizing a Trainium2 kernel written in Bass

```python
import jax, jax.numpy as jnp
from jax import lax
import numpy as np
import math
import jax
import jax.numpy as jnp

D_MODEL = 1024
BATCH = 1
SEQ = 512
DEPTH = 2

N_EVEN = (DEPTH + 1) // 2
N_ODD = DEPTH // 2

MLA_HEADS = 8
MLA_Q_RANK = 384
MLA_KV_RANK = 256
MLA_NOPE = 64
MLA_ROPE = 32
MLA_V = 64
MLA_QK = MLA_NOPE + MLA_ROPE
Q_BLOCK = 128

RET_HEADS = 8
RET_DK = 64
RET_DV = 64
RET_CHUNK = 128
RET_DECAY_BASE = 5.0

GLA_HEADS = 4
GLA_DK = 128
GLA_DV = 256
GLA_GATE_RANK = 16
GLA_TAU = 16.0
GLA_CHUNK = 64

D_FF = 2816
CONV_W = 3

ROPE_THETA = 10000.0
EPS = 1e-6

EVEN_SPLIT = (MLA_Q_RANK, MLA_KV_RANK, MLA_ROPE,
              RET_HEADS * RET_DK, RET_HEADS * RET_DK, RET_HEADS * RET_DV, RET_HEADS * RET_DV)
EVEN_IN = MLA_Q_RANK + MLA_KV_RANK + MLA_ROPE + 2 * RET_HEADS * RET_DK + 2 * RET_HEADS * RET_DV
EVEN_OUT = MLA_HEADS * MLA_V + RET_HEADS * RET_DV
ODD_SPLIT = (GLA_HEADS * GLA_DK, GLA_HEADS * GLA_DK, GLA_HEADS * GLA_DV, GLA_HEADS * GLA_DV,
             GLA_GATE_RANK, GLA_GATE_RANK)
ODD_IN = 2 * GLA_HEADS * GLA_DK + 2 * GLA_HEADS * GLA_DV + 2 * GLA_GATE_RANK
ODD_OUT = GLA_HEADS * GLA_DV


def _split(p, sizes):
    outs, s = [], 0
    for n in sizes:
        outs.append(p[..., s:s + n])
        s += n
    return outs

def _rmsnorm(x, g):
    xf = x.astype(jnp.float32)
    y = xf * lax.rsqrt(jnp.mean(xf * xf, axis=-1, keepdims=True) + EPS)
    return (y * g.astype(jnp.float32)).astype(x.dtype)

def _rope(x, positions):
    half = x.shape[-1] // 2
    inv = ROPE_THETA ** (-jnp.arange(half, dtype=jnp.float32) / half)
    ang = positions.astype(jnp.float32)[:, :, None] * inv
    cos = jnp.cos(ang)[:, :, None, :]
    sin = jnp.sin(ang)[:, :, None, :]
    x1 = x[..., :half].astype(jnp.float32)
    x2 = x[..., half:].astype(jnp.float32)
    return jnp.concatenate([x1 * cos - x2 * sin, x2 * cos + x1 * sin], axis=-1).astype(x.dtype)

def _mla(cq, ckv, k_rope, positions, q_norm, kv_norm, w_uq, w_ukv, q_head_norm, k_head_norm):
    B, S, _ = cq.shape
    H = MLA_HEADS
    q = (_rmsnorm(cq, q_norm) @ w_uq).reshape(B, S, H, MLA_QK)
    kv = (_rmsnorm(ckv, kv_norm) @ w_ukv).reshape(B, S, H, MLA_NOPE + MLA_V)
    k_nope, v = kv[..., :MLA_NOPE], kv[..., MLA_NOPE:]
    k = jnp.concatenate([k_nope, jnp.broadcast_to(k_rope[:, :, None, :], (B, S, H, MLA_ROPE))], axis=-1)
    q = _rmsnorm(q, q_head_norm)
    k = _rmsnorm(k, k_head_norm)
    q = jnp.concatenate([q[..., :MLA_NOPE], _rope(q[..., MLA_NOPE:], positions)], axis=-1)
    k = jnp.concatenate([k[..., :MLA_NOPE], _rope(k[..., MLA_NOPE:], positions)], axis=-1)
    scale = MLA_QK ** -0.5
    nb = S // Q_BLOCK
    qb = q.reshape(B, nb, Q_BLOCK, H, MLA_QK).transpose(1, 0, 2, 3, 4)

    def block(qi):
        s = jnp.einsum('bqhd,bkhd->bhqk', qi, k).astype(jnp.float32) * scale
        p = jax.nn.softmax(s, axis=-1).astype(v.dtype)
        return jnp.einsum('bhqk,bkhe->bqhe', p, v)

    o = lax.map(block, qb)
    return o.transpose(1, 0, 2, 3, 4).reshape(B, S, H * MLA_V)

def _retention_dir(q, k, v, log_gamma, include_diag):
    B, S, H, dk = q.shape
    dv = v.shape[-1]
    C = RET_CHUNK
    n = S // C
    q = q.reshape(B, n, C, H, dk)
    k = k.reshape(B, n, C, H, dk)
    v = v.reshape(B, n, C, H, dv)
    lg = log_gamma.astype(jnp.float32)
    pos = jnp.arange(C, dtype=jnp.float32)
    rel = pos[:, None] - pos[None, :]
    mask = (rel >= 0) if include_diag else (rel > 0)
    decay = jnp.where(mask[None], jnp.exp(lg[:, None, None] * jnp.maximum(rel, 0.0)[None]), 0.0)
    scores = jnp.einsum('bnihd,bnjhd->bnhij', q, k) * decay
    intra = jnp.einsum('bnhij,bnjhe->bnihe', scores, v)
    zeta = jnp.exp(lg[:, None] * (C - 1 - pos)[None])
    chunk_state = jnp.einsum('bnjhd,bnjhe,hj->bnhde', k, v, zeta)
    chunk_decay = jnp.exp(lg * C)[None, :, None, None]

    def step(R, s):
        return chunk_decay * R + s, R

    R0 = jnp.zeros((B, H, dk, dv), chunk_state.dtype)
    _, R_prev = lax.scan(step, R0, jnp.moveaxis(chunk_state, 1, 0))
    R_prev = jnp.moveaxis(R_prev, 0, 1)
    xi = jnp.exp(lg[:, None] * (pos + 1.0)[None]).T
    cross = jnp.einsum('bnihd,bnhde->bnihe', q, R_prev) * xi[None, None, :, :, None]
    return (intra + cross).reshape(B, S, H, dv)

def _retention(rq, rk, rv, rg, positions, theta_fwd, theta_bwd, out_norm):
    B, S, _ = rq.shape
    H = RET_HEADS
    q = _rope(rq.reshape(B, S, H, RET_DK), positions)
    k = _rope(rk.reshape(B, S, H, RET_DK), positions) * (RET_DK ** -0.5)
    v = rv.reshape(B, S, H, RET_DV)
    lg_f = jnp.log1p(-jnp.exp2(-theta_fwd.astype(jnp.float32)))
    lg_b = jnp.log1p(-jnp.exp2(-theta_bwd.astype(jnp.float32)))
    o_f = _retention_dir(q, k, v, lg_f, True)
    o_b = jnp.flip(_retention_dir(jnp.flip(q, 1), jnp.flip(k, 1), jnp.flip(v, 1), lg_b, False), 1)
    o = _rmsnorm(o_f + o_b, out_norm)
    return jax.nn.silu(rg) * o.reshape(B, S, H * RET_DV)

def _gla_dir(q, k, v, log_a, include_diag):
    B, S, H, dk = q.shape
    dv = v.shape[-1]
    C = GLA_CHUNK
    n = S // C
    q = q.reshape(B, n, C, H, dk)
    k = k.reshape(B, n, C, H, dk)
    v = v.reshape(B, n, C, H, dv)
    b = jnp.cumsum(log_a.astype(jnp.float32).reshape(B, n, C, H, dk), axis=2)
    b_mid = b[:, :, C // 2:C // 2 + 1]
    b_last = b[:, :, -1]
    qc = q * jnp.exp(b - b_mid)
    kc = k * jnp.exp(b_mid - b)
    A = jnp.einsum('bnihd,bnjhd->bnhij', qc, kc)
    pos = jnp.arange(C)
    mask = (pos[:, None] >= pos[None, :]) if include_diag else (pos[:, None] > pos[None, :])
    A = jnp.where(mask, A, 0.0)
    intra = jnp.einsum('bnhij,bnjhe->bnihe', A, v)
    k_dec = k * jnp.exp(b_last[:, :, None] - b)
    chunk_state = jnp.einsum('bnjhd,bnjhe->bnhde', k_dec, v)
    chunk_decay = jnp.exp(b_last)

    def step(Sm, xs):
        dcy, st = xs
        return dcy[..., None] * Sm + st, Sm

    S0 = jnp.zeros((B, H, dk, dv), chunk_state.dtype)
    _, S_prev = lax.scan(step, S0, (jnp.moveaxis(chunk_decay, 1, 0), jnp.moveaxis(chunk_state, 1, 0)))
    S_prev = jnp.moveaxis(S_prev, 0, 1)
    inter = jnp.einsum('bnihd,bnhde->bnihe', q * jnp.exp(b), S_prev)
    return (intra + inter).reshape(B, S, H, dv)

def _gla(gq, gk, gv, gr, ga_f, ga_b, w_gate_fwd, b_gate_fwd, w_gate_bwd, b_gate_bwd, out_norm):
    B, S, _ = gq.shape
    H = GLA_HEADS
    q = gq.reshape(B, S, H, GLA_DK) * (GLA_DK ** -0.5)
    k = gk.reshape(B, S, H, GLA_DK)
    v = gv.reshape(B, S, H, GLA_DV)
    la_f = (jax.nn.log_sigmoid((ga_f @ w_gate_fwd + b_gate_fwd).astype(jnp.float32)) / GLA_TAU).reshape(B, S, H, GLA_DK)
    la_b = (jax.nn.log_sigmoid((ga_b @ w_gate_bwd + b_gate_bwd).astype(jnp.float32)) / GLA_TAU).reshape(B, S, H, GLA_DK)
    o_f = _gla_dir(q, k, v, la_f, True)
    o_b = jnp.flip(_gla_dir(jnp.flip(q, 1), jnp.flip(k, 1), jnp.flip(v, 1), jnp.flip(la_b, 1), False), 1)
    o = _rmsnorm(o_f + o_b, out_norm)
    return jax.nn.silu(gr) * o.reshape(B, S, H * GLA_DV)

def _conv_ffn(x, norm_g, w_up, conv_w, conv_b, w_down):
    h = _rmsnorm(x, norm_g)
    up = h @ w_up
    gate, val = up[..., :D_FF], up[..., D_FF:]
    gate = lax.conv_general_dilated(gate, conv_w[:, None, :].astype(gate.dtype), window_strides=(1,),
                                    padding='SAME', dimension_numbers=('NWC', 'WIO', 'NWC'),
                                    feature_group_count=D_FF) + conv_b
    return (jax.nn.silu(gate) * val) @ w_down

def first_inputs(seed: int = 0) -> dict:
    key = jax.random.key(seed)
    ks = iter(jax.random.split(key, 40))

    def dense(shape, fan_in):
        return jax.random.normal(next(ks), shape, jnp.float32) * (fan_in ** -0.5)

    def gain(shape):
        return 1.0 + 0.02 * jax.random.normal(next(ks), shape, jnp.float32)

    def small(shape, s):
        return s * jax.random.normal(next(ks), shape, jnp.float32)

    x = jax.random.normal(next(ks), (BATCH, SEQ, D_MODEL), jnp.float32)
    start = jax.random.randint(next(ks), (BATCH, 1), 0, 4096)
    positions = (start + jnp.arange(SEQ)[None, :]).astype(jnp.int32)
    ret_base = RET_DECAY_BASE + jnp.arange(RET_HEADS, dtype=jnp.float32)
    return {
        "x": x,
        "positions": positions,
        "mix_norm_even": gain((N_EVEN, D_MODEL)),
        "w_in_even": dense((N_EVEN, D_MODEL, EVEN_IN), D_MODEL),
        "mla_q_norm": gain((N_EVEN, MLA_Q_RANK)),
        "mla_kv_norm": gain((N_EVEN, MLA_KV_RANK)),
        "mla_w_uq": dense((N_EVEN, MLA_Q_RANK, MLA_HEADS * MLA_QK), MLA_Q_RANK),
        "mla_w_ukv": dense((N_EVEN, MLA_KV_RANK, MLA_HEADS * (MLA_NOPE + MLA_V)), MLA_KV_RANK),
        "mla_q_head_norm": gain((N_EVEN, MLA_QK)),
        "mla_k_head_norm": gain((N_EVEN, MLA_QK)),
        "ret_theta_fwd": ret_base + small((N_EVEN, RET_HEADS), 0.1),
        "ret_theta_bwd": ret_base + small((N_EVEN, RET_HEADS), 0.1),
        "ret_out_norm": gain((N_EVEN, RET_HEADS, RET_DV)),
        "w_out_even": dense((N_EVEN, EVEN_OUT, D_MODEL), EVEN_OUT),
        "mix_norm_odd": gain((N_ODD, D_MODEL)),
        "w_in_odd": dense((N_ODD, D_MODEL, ODD_IN), D_MODEL),
        "gla_w_gate_fwd": dense((N_ODD, GLA_GATE_RANK, GLA_HEADS * GLA_DK), GLA_GATE_RANK),
        "gla_b_gate_fwd": small((N_ODD, GLA_HEADS * GLA_DK), 0.1),
        "gla_w_gate_bwd": dense((N_ODD, GLA_GATE_RANK, GLA_HEADS * GLA_DK), GLA_GATE_RANK),
        "gla_b_gate_bwd": small((N_ODD, GLA_HEADS * GLA_DK), 0.1),
        "gla_out_norm": gain((N_ODD, GLA_HEADS, GLA_DV)),
        "w_out_odd": dense((N_ODD, ODD_OUT, D_MODEL), ODD_OUT),
        "ffn_norm": gain((DEPTH, D_MODEL)),
        "ffn_w_up": dense((DEPTH, D_MODEL, 2 * D_FF), D_MODEL),
        "ffn_conv_w": dense((DEPTH, CONV_W, D_FF), CONV_W),
        "ffn_conv_b": small((DEPTH, D_FF), 0.02),
        "ffn_w_down": dense((DEPTH, D_FF, D_MODEL), D_FF),
    }

def first_block(x, positions, mix_norm_even, w_in_even, mla_q_norm, mla_kv_norm, mla_w_uq, mla_w_ukv,
              mla_q_head_norm, mla_k_head_norm, ret_theta_fwd, ret_theta_bwd, ret_out_norm, w_out_even,
              mix_norm_odd, w_in_odd, gla_w_gate_fwd, gla_b_gate_fwd, gla_w_gate_bwd, gla_b_gate_bwd,
              gla_out_norm, w_out_odd, ffn_norm, ffn_w_up, ffn_conv_w, ffn_conv_b, ffn_w_down):
    for layer in range(DEPTH):
        i = layer // 2
        if layer % 2 == 0:
            h = _rmsnorm(x, mix_norm_even[i])
            cq, ckv, k_rope, rq, rk, rv, rg = _split(h @ w_in_even[i], EVEN_SPLIT)
            a = _mla(cq, ckv, k_rope, positions, mla_q_norm[i], mla_kv_norm[i], mla_w_uq[i], mla_w_ukv[i],
                     mla_q_head_norm[i], mla_k_head_norm[i])
            r = _retention(rq, rk, rv, rg, positions, ret_theta_fwd[i], ret_theta_bwd[i], ret_out_norm[i])
            x = x + jnp.concatenate([a, r], axis=-1) @ w_out_even[i]
        else:
            h = _rmsnorm(x, mix_norm_odd[i])
            gq, gk, gv, gr, ga_f, ga_b = _split(h @ w_in_odd[i], ODD_SPLIT)
            g = _gla(gq, gk, gv, gr, ga_f, ga_b, gla_w_gate_fwd[i], gla_b_gate_fwd[i],
                     gla_w_gate_bwd[i], gla_b_gate_bwd[i], gla_out_norm[i])
            x = x + g @ w_out_odd[i]
        x = x + _conv_ffn(x, ffn_norm[layer], ffn_w_up[layer], ffn_conv_w[layer], ffn_conv_b[layer],
                          ffn_w_down[layer])
    return x


D_MIX = D_MODEL
FOX_HEADS = 8
FOX_HEAD_DIM = 64
FOX_WIDTH = FOX_HEADS * FOX_HEAD_DIM
S5_WIDTH = D_MIX - FOX_WIDTH
S5_GROUP = 16
S5_GROUPS = S5_WIDTH // S5_GROUP
S5_STATE = 64
EVEN_IN_2 = 3 * FOX_WIDTH + FOX_HEADS + S5_WIDTH
MLSTM_HEADS = 8
MLSTM_HEAD_DIM = D_MIX // MLSTM_HEADS
MLSTM_CHUNK = 64
CONV_WIDTH = 4
ODD_IN_2 = 4 * D_MIX + 2 * MLSTM_HEADS
N_GROUPS = 4
EXPERTS_PER_GROUP = 4
N_EXPERTS = N_GROUPS * EXPERTS_PER_GROUP
EXPERT_TOP_K = 2
D_EXPERT = 256
DN_ALPHA = (2 * DEPTH) ** 0.25
DN_BETA = (8 * DEPTH) ** -0.25
N_EVEN_2 = (DEPTH + 1) // 2
N_ODD_2 = DEPTH // 2
LN_EPS = 1e-5


def layer_norm(x, g, b):
    xf = x.astype(jnp.float32)
    mu = jnp.mean(xf, axis=-1, keepdims=True)
    var = jnp.mean(jnp.square(xf - mu), axis=-1, keepdims=True)
    y = (xf - mu) * lax.rsqrt(var + LN_EPS) * g.astype(jnp.float32) + b.astype(jnp.float32)
    return y.astype(x.dtype)

def forgetting_attention(q, k, v, f_logit):
    B, S, H, Dh = q.shape
    nb = S // Q_BLOCK
    c = jnp.cumsum(jax.nn.log_sigmoid(f_logit.astype(jnp.float32)), axis=1).transpose(0, 2, 1)
    qh = q.transpose(0, 2, 1, 3)
    kh = k.transpose(0, 2, 1, 3)
    vh = v.transpose(0, 2, 1, 3)
    q_blocks = qh.reshape(B, H, nb, Q_BLOCK, Dh).transpose(2, 0, 1, 3, 4)
    c_blocks = c.reshape(B, H, nb, Q_BLOCK).transpose(2, 0, 1, 3)
    pos_k = jnp.arange(S)
    scale = Dh ** -0.5

    def one_block(args):
        qb, cb, i = args
        s = jnp.einsum('bhqd,bhkd->bhqk', qb, kh).astype(jnp.float32) * scale
        s = s + cb[..., :, None] - c[..., None, :]
        pos_q = i * Q_BLOCK + jnp.arange(Q_BLOCK)
        mask = pos_k[None, :] <= pos_q[:, None]
        s = jnp.where(mask, s, -jnp.inf)
        p = jax.nn.softmax(s, axis=-1).astype(vh.dtype)
        return jnp.einsum('bhqk,bhkd->bhqd', p, vh)

    out = lax.map(one_block, (q_blocks, c_blocks, jnp.arange(nb)))
    return out.transpose(1, 0, 3, 2, 4).reshape(B, S, H, Dh)

def s5_scan(u, a_re, a_im, log_dt, b_re, b_im, c_re, c_im, d_skip):
    dt = jnp.exp(log_dt)[:, None]
    mag = jnp.exp(a_re * dt)
    lb_re = mag * jnp.cos(a_im * dt)
    lb_im = mag * jnp.sin(a_im * dt)
    num_re = lb_re - 1.0
    num_im = lb_im
    den = a_re * a_re + a_im * a_im
    z_re = (num_re * a_re + num_im * a_im) / den
    z_im = (num_im * a_re - num_re * a_im) / den
    bb_re = z_re[..., None] * b_re - z_im[..., None] * b_im
    bb_im = z_re[..., None] * b_im + z_im[..., None] * b_re
    bu_re = jnp.einsum('bsgc,gpc->bsgp', u, bb_re)
    bu_im = jnp.einsum('bsgc,gpc->bsgp', u, bb_im)
    a_re_t = jnp.broadcast_to(lb_re, bu_re.shape)
    a_im_t = jnp.broadcast_to(lb_im, bu_im.shape)

    def combine(e1, e2):
        a1r, a1i, b1r, b1i = e1
        a2r, a2i, b2r, b2i = e2
        return (a2r * a1r - a2i * a1i,
                a2r * a1i + a2i * a1r,
                a2r * b1r - a2i * b1i + b2r,
                a2r * b1i + a2i * b1r + b2i)

    _, _, h_re, h_im = lax.associative_scan(combine, (a_re_t, a_im_t, bu_re, bu_im), axis=1)
    y = jnp.einsum('bsgp,gcp->bsgc', h_re, c_re) - jnp.einsum('bsgp,gcp->bsgc', h_im, c_im)
    return y + d_skip * u

def causal_dwconv(x, w, b):
    C = x.shape[-1]
    y = lax.conv_general_dilated(x, w[:, None, :], window_strides=(1,), padding=[(CONV_WIDTH - 1, 0)],
                                 dimension_numbers=('NWC', 'WIO', 'NWC'), feature_group_count=C)
    return y + b

def mlstm_chunkwise(q, k, v, i_pre, f_pre):
    B, S, H, Dh = q.shape
    L = MLSTM_CHUNK
    NC = S // L
    f32 = jnp.float32

    def to_chunks(t):
        return t.reshape(B, NC, L, H, Dh).transpose(0, 3, 1, 2, 4)

    qc = to_chunks(q)
    kc = to_chunks(k * (Dh ** -0.5))
    vc = to_chunks(v)
    log_i = i_pre.astype(f32).reshape(B, NC, L, H).transpose(0, 3, 1, 2)
    log_f = jax.nn.log_sigmoid(f_pre.astype(f32)).reshape(B, NC, L, H).transpose(0, 3, 1, 2)
    bcum = jnp.cumsum(log_f, axis=-1)
    b_last = bcum[..., -1]
    g = b_last[..., None] - bcum + log_i
    m_loc = jnp.max(g, axis=-1)

    def step(carry, inp):
        Cm, nv, m = carry
        k_n, v_n, g_n, bl_n, ml_n = inp
        m_new = jnp.maximum(bl_n + m, ml_n)
        decay = jnp.exp(bl_n + m - m_new)
        w = jnp.exp(g_n - m_new[..., None])
        C_new = decay[..., None, None] * Cm + jnp.einsum('bhld,bhle->bhde', v_n * w[..., None], k_n)
        n_new = decay[..., None] * nv + jnp.einsum('bhl,bhle->bhe', w, k_n)
        return (C_new, n_new, m_new), (Cm, nv, m)

    init = (jnp.zeros((B, H, Dh, Dh), f32), jnp.zeros((B, H, Dh), f32), jnp.zeros((B, H), f32))
    xs = (kc.transpose(2, 0, 1, 3, 4), vc.transpose(2, 0, 1, 3, 4), g.transpose(2, 0, 1, 3),
          b_last.transpose(2, 0, 1), m_loc.transpose(2, 0, 1))
    _, (C_prev, n_prev, m_prev) = lax.scan(step, init, xs)
    C_prev = C_prev.transpose(1, 2, 0, 3, 4)
    n_prev = n_prev.transpose(1, 2, 0, 3)
    m_prev = m_prev.transpose(1, 2, 0)

    causal = jnp.tril(jnp.ones((L, L), dtype=bool))
    log_D = bcum[..., :, None] - bcum[..., None, :] + log_i[..., None, :]
    log_D = jnp.where(causal, log_D, -jnp.inf)
    m_inter = bcum + m_prev[..., None]
    m_t = jnp.maximum(m_inter, jnp.max(log_D, axis=-1))
    Dmat = jnp.exp(log_D - m_t[..., None])
    s = jnp.einsum('bhnld,bhnjd->bhnlj', qc, kc) * Dmat
    inter_scale = jnp.exp(m_inter - m_t)
    num = jnp.einsum('bhnlj,bhnjd->bhnld', s, vc) + inter_scale[..., None] * jnp.einsum('bhnvk,bhnlk->bhnlv', C_prev, qc)
    den = jnp.sum(s, axis=-1) + inter_scale * jnp.einsum('bhnk,bhnlk->bhnl', n_prev, qc)
    h = num / jnp.maximum(jnp.abs(den), jnp.exp(-m_t))[..., None]
    return h.transpose(0, 2, 3, 1, 4).reshape(B, S, H, Dh).astype(v.dtype)

def fox_s5_mixer(x, w_in, f_bias, a_re, a_im, log_dt, b_re, b_im, c_re, c_im, d_skip, w_glu, b_glu, w_out):
    B, S, _ = x.shape
    z = x @ w_in
    q, k, v, f_logit, u = jnp.split(z, [FOX_WIDTH, 2 * FOX_WIDTH, 3 * FOX_WIDTH, 3 * FOX_WIDTH + FOX_HEADS], axis=-1)
    shp = (B, S, FOX_HEADS, FOX_HEAD_DIM)
    att = forgetting_attention(q.reshape(shp), k.reshape(shp), v.reshape(shp), f_logit + f_bias)
    att = att.reshape(B, S, FOX_WIDTH)
    y = s5_scan(u.reshape(B, S, S5_GROUPS, S5_GROUP), a_re, a_im, log_dt, b_re, b_im, c_re, c_im, d_skip)
    y = jax.nn.gelu(y.reshape(B, S, S5_WIDTH))
    y = y * jax.nn.sigmoid(y @ w_glu + b_glu)
    return jnp.concatenate([att, y], axis=-1) @ w_out

def mlstm_mixer(x, w_in, conv_w, conv_b, i_bias, f_bias, w_out):
    B, S, _ = x.shape
    z = x @ w_in
    qk, v, o, i_pre, f_pre = jnp.split(z, [2 * D_MIX, 3 * D_MIX, 4 * D_MIX, 4 * D_MIX + MLSTM_HEADS], axis=-1)
    qk = jax.nn.silu(causal_dwconv(qk, conv_w, conv_b))
    q, k = jnp.split(qk, 2, axis=-1)
    shp = (B, S, MLSTM_HEADS, MLSTM_HEAD_DIM)
    h = mlstm_chunkwise(q.reshape(shp), k.reshape(shp), v.reshape(shp), i_pre + i_bias, f_pre + f_bias)
    h = h.reshape(B, S, D_MIX) * jax.nn.sigmoid(o)
    return h @ w_out

def hier_moe(x, w_group, b_group, w_expert, b_expert, w_gate, w_up, w_down):
    B, S, D = x.shape
    t = x.reshape(B * S, D)
    g_prob = jax.nn.softmax((t @ w_group + b_group).astype(jnp.float32), axis=-1)
    g_val, g_idx = lax.top_k(g_prob, 1)
    e_all = jnp.einsum('td,gde->tge', t, w_expert) + b_expert
    e_logits = jnp.take_along_axis(e_all, g_idx[:, :, None], axis=1)[:, 0]
    e_prob = jax.nn.softmax(e_logits.astype(jnp.float32), axis=-1)
    e_val, e_idx = lax.top_k(e_prob, EXPERT_TOP_K)
    e_val = e_val / jnp.sum(e_val, axis=-1, keepdims=True)
    weights = g_val * e_val
    expert_id = g_idx * EXPERTS_PER_GROUP + e_idx
    combine = jnp.einsum('tk,tke->te', weights, jax.nn.one_hot(expert_id, N_EXPERTS, dtype=jnp.float32))
    hid = jax.nn.silu(jnp.einsum('td,edf->tef', t, w_gate)) * jnp.einsum('td,edf->tef', t, w_up)
    hid = hid * combine.astype(hid.dtype)[:, :, None]
    out = jnp.einsum('tef,efd->td', hid, w_down)
    return out.reshape(B, S, D)

def second_inputs(seed: int = 0) -> dict:
    key = jax.random.key(seed)
    ks = iter(jax.random.split(key, 48))
    f32 = jnp.float32

    def nrm(shape, scale):
        return jax.random.normal(next(ks), shape, f32) * scale

    x = nrm((BATCH, SEQ, D_MODEL), 1.0)
    ln_g = 1.0 + nrm((DEPTH, 2, D_MODEL), 0.01)
    ln_b = nrm((DEPTH, 2, D_MODEL), 0.01)
    even_w_in = nrm((N_EVEN_2, D_MODEL, EVEN_IN_2), D_MODEL ** -0.5)
    fox_f_bias = jnp.linspace(2.0, 5.0, FOX_HEADS, dtype=f32)[None, :] + nrm((N_EVEN_2, FOX_HEADS), 0.1)
    s5_a_re = -0.5 + nrm((N_EVEN_2, S5_GROUPS, S5_STATE), 0.01)
    s5_a_im = jnp.pi * jnp.arange(S5_STATE, dtype=f32)[None, None, :] + nrm((N_EVEN_2, S5_GROUPS, S5_STATE), 0.01)
    s5_log_dt = jax.random.uniform(next(ks), (N_EVEN_2, S5_GROUPS), f32, minval=math.log(1e-3), maxval=math.log(1e-1))
    s5_b_re = nrm((N_EVEN_2, S5_GROUPS, S5_STATE, S5_GROUP), (2 * S5_GROUP) ** -0.5)
    s5_b_im = nrm((N_EVEN_2, S5_GROUPS, S5_STATE, S5_GROUP), (2 * S5_GROUP) ** -0.5)
    s5_c_re = nrm((N_EVEN_2, S5_GROUPS, S5_GROUP, S5_STATE), S5_STATE ** -0.5)
    s5_c_im = nrm((N_EVEN_2, S5_GROUPS, S5_GROUP, S5_STATE), S5_STATE ** -0.5)
    s5_d = nrm((N_EVEN_2, S5_GROUPS, S5_GROUP), 1.0)
    s5_w_glu = nrm((N_EVEN_2, S5_WIDTH, S5_WIDTH), S5_WIDTH ** -0.5)
    s5_b_glu = nrm((N_EVEN_2, S5_WIDTH), 0.01)
    even_w_out = nrm((N_EVEN_2, D_MIX, D_MODEL), D_MIX ** -0.5 * DN_BETA)
    odd_w_in = nrm((N_ODD_2, D_MODEL, ODD_IN_2), D_MODEL ** -0.5)
    mlstm_conv_w = nrm((N_ODD_2, CONV_WIDTH, 2 * D_MIX), CONV_WIDTH ** -0.5)
    mlstm_conv_b = nrm((N_ODD_2, 2 * D_MIX), 0.01)
    mlstm_i_bias = nrm((N_ODD_2, MLSTM_HEADS), 0.1)
    mlstm_f_bias = jnp.linspace(3.0, 6.0, MLSTM_HEADS, dtype=f32)[None, :] + nrm((N_ODD_2, MLSTM_HEADS), 0.01)
    odd_w_out = nrm((N_ODD_2, D_MIX, D_MODEL), D_MIX ** -0.5 * DN_BETA)
    moe_w_group = nrm((DEPTH, D_MODEL, N_GROUPS), D_MODEL ** -0.5)
    moe_b_group = nrm((DEPTH, N_GROUPS), 0.01)
    moe_w_expert = nrm((DEPTH, N_GROUPS, D_MODEL, EXPERTS_PER_GROUP), D_MODEL ** -0.5)
    moe_b_expert = nrm((DEPTH, N_GROUPS, EXPERTS_PER_GROUP), 0.01)
    moe_w_gate = nrm((DEPTH, N_EXPERTS, D_MODEL, D_EXPERT), D_MODEL ** -0.5)
    moe_w_up = nrm((DEPTH, N_EXPERTS, D_MODEL, D_EXPERT), D_MODEL ** -0.5)
    moe_w_down = nrm((DEPTH, N_EXPERTS, D_EXPERT, D_MODEL), D_EXPERT ** -0.5 * DN_BETA)
    return {'x': x, 'ln_g': ln_g, 'ln_b': ln_b,
            'even_w_in': even_w_in, 'fox_f_bias': fox_f_bias,
            's5_a_re': s5_a_re, 's5_a_im': s5_a_im, 's5_log_dt': s5_log_dt,
            's5_b_re': s5_b_re, 's5_b_im': s5_b_im, 's5_c_re': s5_c_re, 's5_c_im': s5_c_im,
            's5_d': s5_d, 's5_w_glu': s5_w_glu, 's5_b_glu': s5_b_glu, 'even_w_out': even_w_out,
            'odd_w_in': odd_w_in, 'mlstm_conv_w': mlstm_conv_w, 'mlstm_conv_b': mlstm_conv_b,
            'mlstm_i_bias': mlstm_i_bias, 'mlstm_f_bias': mlstm_f_bias, 'odd_w_out': odd_w_out,
            'moe_w_group': moe_w_group, 'moe_b_group': moe_b_group,
            'moe_w_expert': moe_w_expert, 'moe_b_expert': moe_b_expert,
            'moe_w_gate': moe_w_gate, 'moe_w_up': moe_w_up, 'moe_w_down': moe_w_down}

def second_block(x, ln_g, ln_b, even_w_in, fox_f_bias, s5_a_re, s5_a_im, s5_log_dt, s5_b_re, s5_b_im,
              s5_c_re, s5_c_im, s5_d, s5_w_glu, s5_b_glu, even_w_out, odd_w_in, mlstm_conv_w,
              mlstm_conv_b, mlstm_i_bias, mlstm_f_bias, odd_w_out, moe_w_group, moe_b_group,
              moe_w_expert, moe_b_expert, moe_w_gate, moe_w_up, moe_w_down):
    h = x
    for layer in range(DEPTH):
        j = layer // 2
        if layer % 2 == 0:
            mix = fox_s5_mixer(h, even_w_in[j], fox_f_bias[j], s5_a_re[j], s5_a_im[j], s5_log_dt[j],
                               s5_b_re[j], s5_b_im[j], s5_c_re[j], s5_c_im[j], s5_d[j],
                               s5_w_glu[j], s5_b_glu[j], even_w_out[j])
        else:
            mix = mlstm_mixer(h, odd_w_in[j], mlstm_conv_w[j], mlstm_conv_b[j], mlstm_i_bias[j],
                              mlstm_f_bias[j], odd_w_out[j])
        h = layer_norm(DN_ALPHA * h + mix, ln_g[layer, 0], ln_b[layer, 0])
        ffn = hier_moe(h, moe_w_group[layer], moe_b_group[layer], moe_w_expert[layer], moe_b_expert[layer],
                       moe_w_gate[layer], moe_w_up[layer], moe_w_down[layer])
        h = layer_norm(DN_ALPHA * h + ffn, ln_g[layer, 1], ln_b[layer, 1])
    return h


def setup_inputs(seed=0):
    out = dict(first_inputs(seed))
    for name, value in second_inputs(seed + 1).items():
        if name != "x":
            out[name + "_2"] = value
    return out


def reference(
    x, positions, mix_norm_even, w_in_even, mla_q_norm, mla_kv_norm, mla_w_uq, mla_w_ukv,
    mla_q_head_norm, mla_k_head_norm, ret_theta_fwd, ret_theta_bwd, ret_out_norm, w_out_even,
    mix_norm_odd, w_in_odd, gla_w_gate_fwd, gla_b_gate_fwd, gla_w_gate_bwd, gla_b_gate_bwd,
    gla_out_norm, w_out_odd, ffn_norm, ffn_w_up, ffn_conv_w, ffn_conv_b, ffn_w_down, ln_g_2,
    ln_b_2, even_w_in_2, fox_f_bias_2, s5_a_re_2, s5_a_im_2, s5_log_dt_2, s5_b_re_2, s5_b_im_2,
    s5_c_re_2, s5_c_im_2, s5_d_2, s5_w_glu_2, s5_b_glu_2, even_w_out_2, odd_w_in_2,
    mlstm_conv_w_2, mlstm_conv_b_2, mlstm_i_bias_2, mlstm_f_bias_2, odd_w_out_2, moe_w_group_2,
    moe_b_group_2, moe_w_expert_2, moe_b_expert_2, moe_w_gate_2, moe_w_up_2, moe_w_down_2,
):
    x = first_block(
        x, positions, mix_norm_even, w_in_even, mla_q_norm, mla_kv_norm, mla_w_uq, mla_w_ukv,
        mla_q_head_norm, mla_k_head_norm, ret_theta_fwd, ret_theta_bwd, ret_out_norm,
        w_out_even, mix_norm_odd, w_in_odd, gla_w_gate_fwd, gla_b_gate_fwd, gla_w_gate_bwd,
        gla_b_gate_bwd, gla_out_norm, w_out_odd, ffn_norm, ffn_w_up, ffn_conv_w, ffn_conv_b,
        ffn_w_down,
    )
    return second_block(
        x, ln_g_2, ln_b_2, even_w_in_2, fox_f_bias_2, s5_a_re_2, s5_a_im_2, s5_log_dt_2,
        s5_b_re_2, s5_b_im_2, s5_c_re_2, s5_c_im_2, s5_d_2, s5_w_glu_2, s5_b_glu_2,
        even_w_out_2, odd_w_in_2, mlstm_conv_w_2, mlstm_conv_b_2, mlstm_i_bias_2,
        mlstm_f_bias_2, odd_w_out_2, moe_w_group_2, moe_b_group_2, moe_w_expert_2,
        moe_b_expert_2, moe_w_gate_2, moe_w_up_2, moe_w_down_2,
    )


_drawn_inputs = setup_inputs


def setup_inputs(seed=0):
    import zlib

    import numpy as np

    out = dict(_drawn_inputs(seed))
    spreads = {}
    factors = {'mla_q_norm': 8.0,
     'mla_kv_norm': 8.0,
     'mla_q_head_norm': 8.0,
     'mla_k_head_norm': 8.0,
     'ret_out_norm': 13.175,
     'gla_b_gate_fwd': 2.996,
     'gla_b_gate_bwd': 3.142,
     'gla_out_norm': 12.255,
     'ffn_conv_b': 2.75,
     's5_a_re_2': 64.0,
     's5_a_im_2': 31.928,
     's5_log_dt_2': 36.304,
     's5_b_re_2': 45.888,
     's5_b_im_2': 49.872,
     's5_c_re_2': 48.296,
     's5_c_im_2': 51.496,
     's5_b_glu_2': 200.0,
     'mlstm_conv_b_2': 48.455,
     'mlstm_i_bias_2': 64.0,
     'moe_b_group_2': 27.109,
     'moe_b_expert_2': 27.149,
     'ffn_norm': 4.205}
    for name, (base, spread) in spreads.items():
        noise = np.random.default_rng([zlib.crc32(name.encode()), seed]).standard_normal(out[name].shape)
        drawn = base * np.exp(spread * noise) if base else spread * noise
        out[name] = jnp.asarray(drawn.astype(out[name].dtype))
    for name, factor in factors.items():
        out[name] = (out[name] * factor).astype(out[name].dtype)
    return out
```

```python
from contextlib import ExitStack

import numpy as np

import concourse.bass as bass
from concourse import mybir

ALU = mybir.AluOpType
ACT = mybir.ActivationFunctionType
F32 = mybir.dt.float32
U32 = mybir.dt.uint32
I32 = mybir.dt.int32
AX = mybir.AxisListType.X

S = 512
D = 1024
KT = 8
FF = 22
NSLOT = 4
SLOT = 4096
NWK = 42
MAGIC = 12582912.0
TWO_PI = 6.283185307179586
C1 = 6.28125
C2 = 0.0019350051879882812
C3 = TWO_PI - C1 - C2
PI_IN = 3.1415925
ALPHA = 4.0 ** 0.25

COL = {}
_n = 0
for _name, _w in (
    ("mix_even", 8), ("q_norm", 3), ("kv_norm", 2), ("qhn", 1), ("khn", 1), ("ret_norm", 4),
    ("th_f", 8), ("th_b", 8), ("mix_odd", 8), ("gb_f", 4), ("gb_b", 4), ("gla_norm", 8),
    ("ffn0", 8), ("ffn1", 8), ("cw0", 66), ("cw1", 66), ("cb0", 22), ("cb1", 22),
    ("lng", 32), ("lnb", 32), ("fox_fb", 1), ("a_re", 16), ("a_im", 16), ("log_dt", 16),
    ("s5_d", 4), ("b_glu", 4), ("mcw", 64), ("mcb", 16), ("ib", 1), ("fb", 1),
    ("mb0", 20), ("mb1", 20), ("inv64", 1), ("inv96", 1), ("eps6", 1), ("eps5", 1),
    ("halfpi", 1), ("one", 1),
):
    COL[_name] = (_n, _w)
    _n += _w
NCOL = _n

CST = {}
_n = 0
for _name, _w in (
    ("ident", 128), ("nident", 128), ("ones", 128), ("bd64", 128), ("rot64", 128), ("rot96", 128),
    ("maskn", 128), ("maskt", 128), ("mf", 128), ("mb", 128), ("causal", 128),
    ("sel", 16 * 128), ("foxsel", 8 * 128), ("oh", 64),
):
    CST[_name] = (_n, _w)
    _n += _w
NCST = _n


class Queues:

    def __init__(self, sem):
        self.make = sem
        self.q = {k: [] for k in ("pe", "act", "dve", "pool", "sp")}
        self.waited = {k: {} for k in self.q}
        self.last = {k: None for k in self.q}
        self.stage = 0
        self.fresh()

    def fresh(self):
        self.sem = {k: self.make(f"s_{k}{self.stage}") for k in ("pe", "act", "dve", "pool")}
        self.count = {k: 0 for k in self.sem}
        self.stage += 1

    def put(self, k, fn, after, sig=True):
        waits = []
        if k in ("act", "dve", "pool"):
            after = [*after, self.last[k]]
        for t in after:
            if t is None:
                continue
            s, v = t
            if self.waited[k].get(id(s), 0) < v:
                self.waited[k][id(s)] = v
                waits = [w for w in waits if w[0] is not s] + [t]
        tok = None
        if sig:
            self.count[k] += 1
            tok = (self.sem[k], self.count[k])
            self.last[k] = tok
        self.q[k].append((waits, fn, (tok[0], 1) if sig else None))
        return tok

    def dma(self, k, out, in_, sem, value, after=()):
        waits = []
        for t in after:
            if t is not None and self.waited[k].get(id(t[0]), 0) < t[1]:
                self.waited[k][id(t[0])] = t[1]
                waits.append(t)
        self.q[k].append((waits, lambda e: e.dma_start(out, in_), (sem, 16)))
        return (sem, value)

    def wait_all(self, k, after):
        self.q[k].append((list(after), None, None))

    def run(self, k, e):
        for waits, fn, inc in self.q[k]:
            for s, v in waits:
                e.wait_ge(s, v)
            if fn is not None:
                ins = fn(e)
                if inc is not None:
                    ins.then_inc(*inc)

    def tt(self, out, a, b, op, *after, eng="dve"):
        return self.put(eng, lambda e: e.tensor_tensor(out, a, b, op), after)

    def ts(self, out, a, s1, s2, op0, op1, *after, eng="dve"):
        if s2 is None:
            return self.put(eng, lambda e: e.tensor_scalar(out, a, s1, None, op0), after)
        return self.put(eng, lambda e: e.tensor_scalar(out, a, s1, s2, op0, op1), after)

    def stt(self, out, a, s, b, op0, op1, *after):
        return self.put("dve", lambda e: e.scalar_tensor_tensor(out, a, s, b, op0, op1), after)

    def scan(self, out, d0, d1, init, op0, op1, *after):
        return self.put("dve", lambda e: e.tensor_tensor_scan(out, d0, d1, init, op0, op1), after)

    def rmax(self, out, a, *after):
        return self.put("dve", lambda e: e.tensor_reduce(out, a, AX, ALU.max), after)

    def rsum(self, out, a, *after):
        return self.put("dve", lambda e: e.tensor_reduce(out, a, AX, ALU.add), after)

    def recip(self, out, a, *after):
        return self.put("dve", lambda e: e.reciprocal(out, a), after)

    def cp(self, out, a, *after, eng="dve"):
        return self.put(eng, lambda e: e.tensor_copy(out, a), after)

    def cpred(self, out, mask, a, *after):
        return self.put("dve", lambda e: e.copy_predicated(out, mask, a), after)

    def memset(self, out, v, *after, eng="pool"):
        return self.put(eng, lambda e: e.memset(out, v), after)

    def act(self, out, a, f, *after, scale=1.0, bias=0.0):
        return self.put("act", lambda e: e.activation(out, a, f, bias=bias, scale=scale), after)

    def mm(self, out, lhsT, rhs, start, stop, *after, sig=False, loose=False):
        return self.put("pe", lambda e: e.matmul(out, lhsT, rhs, start=start, stop=stop,
                                                 skip_group_check=loose), after, sig)

    def tr(self, out, a, ident, *after, sig=False):
        return self.put("pe", lambda e: e.transpose(out, a, ident), after, sig)

    def group(self, out, pairs, *after, start=True, stop=True, loose=False, each=None):
        t = None
        for i, (w, r) in enumerate(pairs):
            last = i == len(pairs) - 1
            own = after if i == 0 else ()
            if each is not None:
                own = (*own, each[i])
            t = self.mm(out, w, r, start and i == 0, stop and last, *own, sig=last, loose=loose)
        return t


class Build:
    def __init__(self, nc, ins, out):
        self.nc, self.ins, self.out = nc, ins, out
        self.ctx = ExitStack()

    def sb(self, name, shape, dt=F32):
        return self.ctx.enter_context(self.nc.sbuf_tensor(name, shape, dt))

    def sem(self, name):
        return self.ctx.enter_context(self.nc.semaphore(name))

    def col(self, name, i=0, p0=0, p1=128, n=1):
        a = COL[name][0] + i
        return self.cols[p0:p1, a:a + n]

    def cst(self, name, p=128, a=0, n=None):
        c, w = CST[name]
        n = w if n is None else n
        return self.csts[0:p, c + a:c + a + n]

    def setup(self):
        nc = self.nc
        self.X = self.sb("X", [128, KT, S])
        self.H = self.sb("H", [128, KT, S])
        self.ring = self.sb("ring", [128, NSLOT, SLOT])
        self.WK = self.sb("WK", [128, NWK, S])
        self.cols = self.sb("cols", [128, NCOL])
        self.csts = self.sb("csts", [128, NCST])
        self.small = self.sb("small", [128, 640])
        self.PB = [self.ctx.enter_context(nc.psum_tensor(f"PB{i}", [128, S], F32)) for i in range(8)]
        self.p = Queues(self.sem)
        self.slot_sem = [self.sem(f"ds{i}") for i in range(NSLOT)]
        self.slot_use = [0] * NSLOT
        self.slot_free = [()] * NSLOT
        self.next_slot = 0
        s0 = [self.sem(f"di{i}") for i in range(3)]
        p = self.p
        self.t_csts = p.dma("sp", self.csts[:, :], self.ins["csts"], s0[1], 16)
        self.t_cols = p.dma("sp", self.cols[:, :], self.ins["cols"], s0[2], 16)
        self.t_x = p.dma("sp", self.X[:, :, :], self.ins["xT"].rearrange("(t p) s -> p t s", p=128), s0[0], 16)
        self.fr = [()] * 8
        for k in ("pe", "act", "dve", "pool"):
            p.wait_all(k, [self.t_csts, self.t_cols, self.t_x])

    def load(self, src, shape):
        s = self.next_slot
        self.next_slot = (s + 1) % NSLOT
        self.slot_use[s] += 1
        n = int(np.prod(shape[1:]))
        flat = self.ring[0:shape[0], s, 0:n]
        if len(shape) == 3:
            view = flat.rearrange("p (a b) -> p a b", a=shape[1])
        elif len(shape) == 4:
            view = flat.rearrange("p (a b c) -> p a b c", a=shape[1], b=shape[2])
        else:
            view = flat
        if len(src.shape) == 4:
            src = src.rearrange("t p k c -> p t (k c)")
            flat = flat.rearrange("p (t n) -> p t n", t=shape[1])
        t = self.p.dma("sp", flat, src, self.slot_sem[s], 16 * self.slot_use[s], self.slot_free[s])
        return view, t, s

    def tiles(self, name, a, b, kt):
        return self.load(self.ins[name][a:b], [128, b - a, kt, 128])

    def barrier(self):
        p = self.p
        now = [p.last[k] for k in ("pe", "act", "dve", "pool") if p.last[k] is not None]
        for k in ("pe", "act", "dve", "pool"):
            p.wait_all(k, now)
        p.fresh()
        self.fr = [()] * 8

    def rstd(self, out, bank, n, eps, rows, *after):
        p = self.p
        t = p.act(out, bank, ACT.Ln, *after, scale=1.0 / n, bias=eps)
        return p.act(out, out, ACT.Exp, t, scale=-0.5)

    def rmsnorm(self, src, gain, dst, n, bank, tmp, ready):
        p = self.p
        used = [(), ()]
        for i, a in enumerate(src):
            sq = tmp[i % 2]
            t = p.act(sq, a, ACT.Square, ready, *used[i % 2])
            m = p.mm(self.PB[bank][:, :], self.cst("ones"), sq, i == 0, i == len(src) - 1, t,
                     *(self.fr[bank] if i == 0 else ()), sig=True)
            used[i % 2] = (m,)
        t = self.rstd(tmp[2], self.PB[bank][:, :], n, self.col("eps6"), 128, m)
        self.fr[bank] = (t,)
        return [p.stt(d, a, g, tmp[2], ALU.mult, ALU.mult, t) for d, a, g in zip(dst, src, gain)]

    def layernorm(self, row):
        p, X, PB = self.p, self.X, self.PB
        tmp = [self.WK[:, 36 + i, :] for i in range(4)]
        now = p.last["dve"]
        m = p.group(PB[0][:, :], [(self.cst("ones"), X[:, i, :]) for i in range(KT)], now, *self.fr[0])
        mu = p.act(tmp[3], PB[0][:, :], ACT.Copy, m, scale=1.0 / D)
        self.fr[0] = (mu,)
        used = [(), ()]
        for i in range(KT):
            c = p.tt(X[:, i, :], X[:, i, :], tmp[3], ALU.subtract, mu)
            t = p.act(tmp[i % 2], X[:, i, :], ACT.Square, c, *used[i % 2])
            m = p.mm(PB[1][:, :], self.cst("ones"), tmp[i % 2], i == 0, i == KT - 1, t,
                     *(self.fr[1] if i == 0 else ()), sig=True)
            used[i % 2] = (m,)
        t = self.rstd(tmp[2], PB[1][:, :], D, self.col("eps5"), 128, m)
        self.fr[1] = (t,)
        for i in range(KT):
            c = p.stt(X[:, i, :], X[:, i, :], self.col("lng", 8 * row + i), tmp[2], ALU.mult, ALU.mult, t)
            p.act(X[:, i, :], X[:, i, :], ACT.Identity, c, bias=self.col("lnb", 8 * row + i))
        self.barrier()

    def project(self, name, n_tiles, kt, rhs, ready, banks, use, first=0):
        p = self.p
        per = max(1, min(4, SLOT // (kt * 128)))
        t0 = first
        n = 0
        while t0 < first + n_tiles:
            t1 = min(t0 + per, first + n_tiles)
            w, tw, slot = self.tiles(name, t0, t1, kt)
            for t in range(t0, t1):
                b = banks[n % len(banks)]
                n += 1
                m = p.group(self.PB[b][:, :], [(w[:, t - t0, k, :], rhs[k]) for k in range(kt)],
                            tw, *self.fr[b], each=ready)
                self.fr[b] = use(t, b, m)
            self.slot_free[slot] = (m,)
            t0 = t1

    def project_rows(self, name, first, n_tiles, lhs, ready, banks, use):
        p = self.p
        n = 0
        for t0 in range(first, first + n_tiles, 4):
            w, tw, slot = self.tiles(name, t0, t0 + 4, KT)
            for q in range(4):
                b = banks[n % len(banks)]
                n += 1
                m = p.group(self.PB[b][:, :].rearrange("p (a c) -> p a c", a=4),
                            [(lhs[k][:, 128 * q:128 * q + 128], w[:, :, k, :]) for k in range(KT)],
                            tw, *self.fr[b], each=ready)
                self.fr[b] = use((t0 - first) // 4, q, b, m)
            self.slot_free[slot] = (m,)

    def add_out(self, name, rhs, ready, scale, kt=KT, banks=(4, 5, 6, 7)):
        p, X = self.p, self.X

        def use(t, b, m):
            if scale is None:
                return (p.tt(X[:, t, :], X[:, t, :], self.PB[b][:, :], ALU.add, m),)
            return (p.stt(X[:, t, :], X[:, t, :], scale, self.PB[b][:, :], ALU.mult, ALU.add, m),)

        self.project(name, 8, kt, rhs, ready, banks, use)

    def log_sigmoid(self, z, dst, t1, t2, after):
        p = self.p
        a = p.act(t1, z, ACT.Abs, *after)
        a = p.act(t1, t1, ACT.Exp, a, scale=-1.0)
        a = p.act(t1, t1, ACT.Ln, a, bias=1.0)
        b = p.ts(t2, z, 0.0, None, ALU.min, None, *after)
        return p.tt(dst, t2, t1, ALU.subtract, a, b)

    def rope_tables(self, inv, posf, cos, sin, tmp, after):
        p = self.p
        t = p.ts(sin, posf, inv, None, ALU.mult, None, after)
        t = p.ts(tmp, sin, 1.0 / TWO_PI, MAGIC, ALU.mult, ALU.add, t)
        t = p.ts(tmp, tmp, MAGIC, None, ALU.subtract, None, t)
        for c in (C1, C2, C3):
            t = p.stt(sin, tmp, -c, sin, ALU.mult, ALU.add, t)
        t = p.ts(sin, sin, PI_IN, -PI_IN, ALU.min, ALU.max, t)
        a = p.act(cos, sin, ACT.Abs, t)
        a = p.act(cos, cos, ACT.Sin, a, scale=-1.0, bias=self.col("halfpi"))
        return p.act(sin, sin, ACT.Sin, a)

    def even0(self):
        p, X, H, WK, PB = self.p, self.X, self.H, self.WK, self.PB
        rq = [WK[:, i, :] for i in range(0, 4)]
        rk = [WK[:, i, :] for i in range(4, 8)]
        rv = [WK[:, i, :] for i in range(8, 12)]
        rg = [WK[:, i, :] for i in range(12, 16)]
        cq = [WK[:, i, :] for i in range(16, 19)]
        kro = WK[:, 19, :]
        ckv = [WK[:, i, :] for i in range(20, 22)]
        tmp = [WK[:, i, :] for i in range(22, 30)]
        c64, s64, c96, s96 = (WK[:, i, :] for i in range(30, 34))
        hs = [H[:, i, :] for i in range(KT)]
        xs = [X[:, i, :] for i in range(KT)]

        posi = tmp[4].bitcast(I32)
        tp = p.dma("sp", posi, self.ins["posb"], self.sem("dpos"), 16)
        th = self.rmsnorm(xs, [self.col("mix_even", i) for i in range(KT)], hs, D, 7, tmp[0:3], None)
        t = p.cp(tmp[5], posi, tp)
        self.rope_tables(self.col("inv64"), tmp[5], c64, s64, tmp[6], t)
        t_rope = self.rope_tables(self.col("inv96"), tmp[5], c96, s96, tmp[6], p.last["dve"])

        roped = {}

        def rope_tile(dst, raw_tile):
            def use(i, b, m):
                j = i % 4
                raw = raw_tile[i % 2]
                c = p.act(raw, PB[b][:, :], ACT.Copy, m, *roped.get(raw_tile[i % 2].offset, ()))
                rb = 6 + i % 2
                r = p.mm(PB[rb][:, :], self.cst("rot64"), raw, True, True, c, *self.fr[rb], sig=True)
                a = p.tt(dst[j], raw, c64, ALU.mult, c, t_rope)
                s = p.tt(tmp[4], PB[rb][:, :], s64, ALU.mult, r)
                self.fr[rb] = (s,)
                roped[raw_tile[i % 2].offset] = (a, r)
                p.tt(dst[j], dst[j], tmp[4], ALU.add, a, s)
                return (c,)
            return use

        self.project("w_in_even", 4, KT, hs, th, (0, 1, 2, 3), rope_tile(rq, tmp[6:8]), 0)
        self.project("w_in_even", 4, KT, hs, None, (0, 1, 2, 3), rope_tile(rk, tmp[6:8]), 4)
        self.project_rows("w_in_even", 8, 4, hs, None, (0, 1, 2, 3),
                          lambda n, q, b, m: (p.act(rv[q], PB[b][:, :], ACT.Copy, m),))
        t_rkv = p.last["act"]
        t_rqk = p.last["dve"]
        self.project("w_in_even", 4, KT, hs, None, (0, 1, 2, 3),
                     lambda i, b, m: (p.act(rg[i - 12], PB[b][:, :], ACT.Silu, m),), 12)
        self.project("w_in_even", 6, KT, hs, None, (0, 1, 2, 3),
                     lambda i, b, m: (p.act(WK[:, i, :], PB[b][:, :], ACT.Copy, m),), 16)
        t_c = p.last["act"]

        tq = self.rmsnorm(cq, [self.col("q_norm", i) for i in range(3)], cq, 384, 4, tmp[0:3], t_c)
        tkv = self.rmsnorm(ckv, [self.col("kv_norm", i) for i in range(2)], ckv, 256, 5, tmp[0:3], tq[-1])
        self.barrier()

        self.retention(rq, rk, rv, rg, [tmp[i] for i in range(8)] + [WK[:, i, :] for i in range(34, 42)])
        self.barrier()
        self.mla(cq, ckv, kro, c96, s96)
        self.barrier()
        self.add_out("w_out_even", hs, None, None)
        self.barrier()

    def retention(self, rq, rk, rv, rg, w):
        p, H, PB, sm = self.p, self.H, self.PB, self.small
        y, u, lg, e = (sm[:, 16 * i:16 * i + 16] for i in range(4))
        th = self.col("th_f", n=16)
        t = p.act(y, th, ACT.Exp, scale=-0.6931471805599453)
        t = p.ts(u, y, -1.0, 1.0, ALU.mult, ALU.add, t)
        a = p.act(lg, u, ACT.Ln, t)
        t = p.ts(e, u, -1.0, None, ALU.add, None, t)
        t = p.tt(e, e, y, ALU.add, t)
        t2 = p.recip(y, u, t)
        t = p.tt(e, e, y, ALU.mult, t2)
        t_lg = p.tt(lg, lg, e, ALU.subtract, t, a)
        R = w[0][:, :]
        flat = self.WK[:, 22:24, :].rearrange("p a b -> p (a b)")[:, 0:896]
        flatn = self.WK[:, 24:26, :].rearrange("p a b -> p (a b)")[:, 0:896]
        ri = self.WK[:, 26:28, :].rearrange("p a b -> p (a b)")[:, 0:896].bitcast(I32)
        t = p.put("pool", lambda e_: e_.iota(ri, [[1, 896]], base=-384, channel_multiplier=-1), ())
        t = p.cp(flat, ri, t)
        t = p.ts(flatn, flat, -1.0, 0.0, ALU.mult, ALU.max, t)
        t_r = p.ts(flat, flat, 0.0, None, ALU.max, None, t)
        dtab = [self.WK[:, 26:28, :].rearrange("p a b -> p (a b)")[:, 0:896],
                self.WK[:, 28:30, :].rearrange("p a b -> p (a b)")[:, 0:896]]
        st = [w[i] for i in range(8, 12)]
        sq, r, nrm = w[12], w[13], w[14]
        read = [(), ()]
        st_read = [()] * 4
        tail = ()
        for h in range(8):
            d = dtab[h % 2]
            t = p.ts(d, flat, lg[:, h:h + 1], None, ALU.mult, None, t_lg, t_r, *read[h % 2])
            t = p.stt(d, flatn, lg[:, 8 + h:9 + h], d, ALU.mult, ALU.add, t)
            t_d = p.act(d, d, ACT.Exp, t)
            r0 = 64 * (h % 2)
            ob = 4 + (h // 2) % 2
            for j in range(4):
                b = j
                m = p.mm(PB[b][:, :], rk[h // 2][r0:r0 + 64, 128 * j:128 * j + 128], rq[h // 2][r0:r0 + 64, :],
                         True, True, *self.fr[b], sig=True)
                t = p.stt(st[j], PB[b][:, :], 0.125, d[:, 384 - 128 * j:896 - 128 * j], ALU.mult, ALU.mult,
                          m, t_d, *st_read[j])
                self.fr[b] = (t,)
                m = p.mm(PB[ob][r0:r0 + 64, :], rv[j][:, 64 * h:64 * h + 64], st[j], j == 0, j == 3, t,
                         *(self.fr[ob] if j == 0 else ()), sig=True)
                st_read[j] = (m,)
            read[h % 2] = (t,)
            if h % 2 == 1:
                i = h // 2
                t = p.act(sq, PB[ob][:, :], ACT.Square, m, *tail)
                m2 = p.mm(PB[6][:, :], self.cst("bd64"), sq, True, True, t, *self.fr[6], sig=True)
                t = self.rstd(r, PB[6][:, :], 64, self.col("eps6"), 128, m2)
                self.fr[6] = (t,)
                t = p.stt(nrm, PB[ob][:, :], self.col("ret_norm", i), r, ALU.mult, ALU.mult, t)
                self.fr[ob] = (t,)
                t = p.tt(H[:, 4 + i, :], nrm, rg[i], ALU.mult, t)
                tail = (t,)

    def mla(self, cq, ckv, kro, c96, s96):
        p, H, WK, PB, sm = self.p, self.H, self.WK, self.PB, self.small
        wq, tw, sq_slot = self.load(self.ins["w_uq"], [128, 8, 3, 96])
        wkv, twk, skv = self.load(self.ins["w_ukv"], [128, 4, 512])
        vaug = WK[:, 0:8, :].rearrange("p a b -> p (a b)").rearrange("p (k h e) -> p k h e", k=4, h=8)
        qT = [WK[:, 8, :], WK[:, 9, :]]
        kT = [WK[:, 10, :], WK[:, 11, :]]
        pT = [WK[:, i, :] for i in range(12, 16)]
        sq, rs, qn, tr, raw, rc = (WK[:, i, :] for i in range(22, 28))
        mcol = [sm[:, 64:68], sm[:, 68:72]]
        t_one = [p.memset(kT[i][96:97, :], 1.0) for i in range(2)][-1]
        t_v1 = p.memset(vaug, 1.0)
        for k in range(4):
            b = k % 2
            m = p.group(PB[b][:, :], [(ckv[c][:, 128 * k:128 * k + 128], wkv[:, 2 + c, :]) for c in range(2)],
                        twk, *self.fr[b])
            v = PB[b][:, :].rearrange("p (h e) -> p h e", h=8)
            t = p.act(vaug[:, k, 0:8:2, 0:64], v[:, 0:8:2, :], ACT.Copy, m, t_v1)
            t = p.act(vaug[:, k, 1:8:2, 64:128], v[:, 1:8:2, :], ACT.Copy, m, t_v1)
            self.fr[b] = (t,)
        t_v = t
        scale = 96.0 ** -0.5
        used_q = [(), ()]
        used_k = [(), ()]
        pt_read = [()] * 4
        side = [()]

        def normed(src, sq_in_ready, gain, dst, free):
            t = p.act(sq[0:96, :], src, ACT.Square, *sq_in_ready, *side[0])
            m = p.mm(PB[7][0:96, :], self.cst("ones", 96, 0, 96), sq[0:96, :], True, True, t, *self.fr[7], sig=True)
            t = self.rstd(rs[0:96, :], PB[7][0:96, :], 96, self.col("eps6", 0, 0, 96), 96, m)
            n = p.stt(qn[0:96, :], src, gain, rs[0:96, :], ALU.mult, ALU.mult, t)
            m = p.mm(PB[7][0:96, :], self.cst("rot96", 96, 0, 96), qn[0:96, :], True, True, n, sig=True)
            a = p.tt(dst[0:96, :], qn[0:96, :], c96[0:96, :], ALU.mult, n, *free)
            s = p.tt(tr[64:96, :], PB[7][64:96, :], s96[64:96, :], ALU.mult, m)
            self.fr[7] = (s,)
            side[0] = (m, s)
            return n, p.tt(dst[64:96, :], dst[64:96, :], tr[64:96, :], ALU.add, a, s)

        def make(h):
            m = p.group(PB[6][0:96, :], [(wq[:, h, c, :], cq[c]) for c in range(3)], tw, *self.fr[6])
            n, tq = normed(PB[6][0:96, :], (m,), self.col("qhn", 0, 0, 96), qT[h % 2], used_q[h % 2])
            self.fr[6] = (n,)
            m = p.group(PB[6][0:64, :], [(wkv[:, c, 64 * h:64 * h + 64], ckv[c]) for c in range(2)], twk,
                        *self.fr[6])
            t = p.act(raw[0:64, :], PB[6][0:64, :], ACT.Copy, m)
            self.fr[6] = (t,)
            t = p.act(raw[64:96, :], kro[0:32, :], ACT.Copy, t)
            n, tk = normed(raw[0:96, :], (t,), self.col("khn", 0, 0, 96), kT[h % 2], (*used_k[h % 2], t_one))
            return tq, tk

        ready = make(0)
        for h in range(8):
            tq, tk = ready
            q, k = qT[h % 2], kT[h % 2]
            mc = mcol[h % 2]
            for i in range(4):
                b = i % 2
                m = p.mm(PB[b][:, :], q[0:96, 128 * i:128 * i + 128], k[0:96, :], True, True, tq, tk, *self.fr[b],
                         sig=True)
                t = p.rmax(mc[:, i:i + 1], PB[b][:, :], m)
                self.fr[b] = (t,)
            if h < 7:
                ready = make(h + 1)
            for i in range(4):
                m = p.mm(PB[4][96:97, 128 * i:128 * i + 128], mc[:, i:i + 1], self.cst("nident"), i == 0, i == 3, t,
                         *(self.fr[4] if i == 0 else ()), sig=i == 3, loose=True)
            t_m = p.act(q[96:97, :], PB[4][96:97, :], ACT.Copy, m)
            self.fr[4] = (t_m,)
            for i in range(4):
                b = 2 + i % 2
                m = p.mm(PB[b][:, :], k[0:97, 128 * i:128 * i + 128], q[0:97, :], True, True, t_m, *self.fr[b],
                         sig=True)
                t = p.act(pT[i], PB[b][:, :], ACT.Exp, m, *pt_read[i], scale=scale)
                self.fr[b] = (t,)
                used_q[h % 2] = used_k[h % 2] = (m,)
                m = p.mm(PB[5][:, :], vaug[:, i, h, :], pT[i], i == 0, i == 3, t, t_v,
                         *(self.fr[5] if i == 0 else ()), sig=True)
                pt_read[i] = (m,)
            o, s = (slice(0, 64), slice(64, 128)) if h % 2 == 0 else (slice(64, 128), slice(0, 64))
            t = p.recip(rc[o, :], PB[5][s, :], m)
            t = p.tt(H[o, h // 2, :], PB[5][o, :], rc[o, :], ALU.mult, t)
            self.fr[5] = (t,)
        self.slot_free[sq_slot] = (p.last["pe"],)
        self.slot_free[skv] = (p.last["pe"],)

    def ffn(self, layer):
        p, X, H, WK, PB = self.p, self.X, self.H, self.WK, self.PB
        hs = [H[:, i, :] for i in range(KT)]
        th = self.rmsnorm([X[:, i, :] for i in range(KT)], [self.col(f"ffn{layer}", i) for i in range(KT)], hs, D, 7,
                          [WK[:, 36 + i, :] for i in range(3)], None)
        hid = [WK[:, i, :] for i in range(FF)]
        cv = [WK[:, 24 + i, :] for i in range(3)]
        done = []
        gate = {}

        def use(t, b, m):
            i = t // 2
            ps = PB[b]
            if t % 2 == 0:
                c = cv[i % 3]
                w = [self.col(f"cw{layer}", FF * j + i) for j in range(3)]
                a = p.act(c, ps[:, :], ACT.Identity, m, *(done[i - 3:i - 2] if i >= 3 else ()), scale=w[1],
                          bias=self.col(f"cb{layer}", i))
                a = p.stt(c[:, 1:S], ps[:, 0:S - 1], w[0], c[:, 1:S], ALU.mult, ALU.add, a)
                a = p.stt(c[:, 0:S - 1], ps[:, 1:S], w[2], c[:, 0:S - 1], ALU.mult, ALU.add, a)
                gate[i] = p.act(c, c, ACT.Silu, a)
                return (a,)
            d = p.tt(hid[i], cv[i % 3], ps[:, :], ALU.mult, m, gate[i])
            done.append(d)
            return (d,)

        self.project(f"w_up{layer}", 2 * FF, KT, hs, th, (0, 1, 2, 3), use)
        self.add_out(f"w_down{layer}", hid, done, None, FF)
        self.barrier()

    def odd0(self):
        p, X, H, WK, PB, sm = self.p, self.X, self.H, self.WK, self.PB, self.small
        hs = [H[:, i, :] for i in range(KT)]
        th = self.rmsnorm([X[:, i, :] for i in range(KT)], [self.col("mix_odd", i) for i in range(KT)], hs, D, 7,
                          [WK[:, 36 + i, :] for i in range(3)], None)
        gq = [WK[:, i, :] for i in range(0, 4)]
        gk = [WK[:, i, :] for i in range(4, 8)]
        gv = WK[:, 8:16, :].rearrange("p (q a) b -> p q (a b)", q=4)
        gr = [WK[:, i, :] for i in range(16, 24)]
        ga = WK[:, 24, :]
        sc = 128.0 ** -0.5
        self.project("w_in_odd", 4, KT, hs, th, (0, 1, 2, 3),
                     lambda i, b, m: (p.act(gq[i], PB[b][:, :], ACT.Copy, m, scale=sc),), 0)
        self.project("w_in_odd", 4, KT, hs, None, (0, 1, 2, 3),
                     lambda i, b, m: (p.act(gk[i - 4], PB[b][:, :], ACT.Copy, m),), 4)
        self.project_rows("w_in_odd", 8, 8, hs, None, (0, 1, 2, 3),
                          lambda n, q, b, m: (p.act(gv[:, q, 512 * n:512 * n + 512], PB[b][:, :], ACT.Copy, m),))
        self.project("w_in_odd", 8, KT, hs, None, (0, 1, 2, 3),
                     lambda i, b, m: (p.act(gr[i - 16], PB[b][:, :], ACT.Silu, m),), 16)
        self.project("w_in_odd", 1, KT, hs, None, (0,),
                     lambda i, b, m: (p.act(ga, PB[b][:, :], ACT.Copy, m),), 24)
        wg, tw, slot = self.load(self.ins["w_gate"], [32, 2, 512])
        self.barrier()

        T = [WK[:, i, :] for i in range(25, 42)]
        at = T[0:2]
        chunk = T[2:4]
        for d in range(2):
            p.memset(at[d], 0.0)
            t = p.memset(chunk[d], 1.0)
            edge = 0 if d == 0 else 63
            t_c = p.memset(chunk[d][:, edge:S:64], 0.0, t)
        ax, bb = T[4], T[5]
        qc, kc, kd, qb = T[6], T[7], T[8], T[9:11]
        kdn = T[11:13]
        sst = [[T[13 + d][:, 256 * i:256 * i + 256] for i in range(2)] for d in range(2)]
        sq, rr = T[15], T[16]
        dec = [sm[:, 8 * d:8 * d + 8] for d in range(2)]
        mask = [self.cst("mf").bitcast(U32), self.cst("mb").bitcast(U32)]
        v3 = lambda a: a.rearrange("p (c t) -> p c t", t=64)
        tail = ()
        at_read = [(), ()]
        kdn_read = [(), ()]
        qb_read = [(), ()]
        s_read = [(), ()]
        kc_read = ()
        kd_read = ()
        for h in range(4):
            heads = []
            for d in range(2):
                m = p.mm(PB[0][:, :], wg[:, d, 128 * h:128 * h + 128], ga[0:32, :], True, True, tw, *self.fr[0],
                         sig=True)
                bias = self.col("gb_f" if d == 0 else "gb_b", h)
                z = p.ts(bb, PB[0][:, :], bias, None, ALU.add, None, m)
                self.fr[0] = (z,)
                t = self.log_sigmoid(bb, bb, ax, qc, (z, *kc_read))
                if d == 0:
                    t = p.scan(ax, chunk[0], bb, 0.0, ALU.mult, ALU.add, t, t_c)
                else:
                    t = p.scan(ax[:, ::-1], chunk[1][:, ::-1], bb[:, ::-1], 0.0, ALU.mult, ALU.add, t, t_c)
                b3 = v3(ax)
                mid, last = (32, 63) if d == 0 else (31, 0)
                t_b = t
                t = p.tt(v3(bb), b3, b3[:, :, mid:mid + 1].to_broadcast([128, 8, 64]), ALU.subtract, t_b)
                a = p.act(qc, bb, ACT.Exp, t, scale=1.0 / 16)
                a2 = p.act(kc, bb, ACT.Exp, t, scale=-1.0 / 16, *())
                t_q = p.tt(qc, qc, gq[h], ALU.mult, a)
                t_k = p.tt(kc, kc, gk[h], ALU.mult, a2)
                a = p.act(qb[d], ax, ACT.Exp, t_b, *qb_read[d], scale=1.0 / 16)
                t_qb = p.tt(qb[d], qb[d], gq[h], ALU.mult, a)
                t = p.tt(v3(bb), b3[:, :, last:last + 1].to_broadcast([128, 8, 64]), b3, ALU.subtract, a2)
                a = p.act(kd, bb, ACT.Exp, t, *kd_read, scale=1.0 / 16)
                t_kd = p.tt(kd, kd, gk[h], ALU.mult, a)
                t_dec = p.act(dec[d], b3[:, :, last:last + 1].rearrange("p c o -> p (c o)"), ACT.Exp, t_b, *s_read[d],
                              scale=1.0 / 16)
                for q in range(4):
                    c = slice(128 * q, 128 * q + 128)
                    m = p.mm(PB[1][:, c], kc[:, c], qc[:, c], True, True, t_q, t_k, *(self.fr[1] if q == 0 else ()),
                             sig=q == 3)
                kc_read = (m,)
                t_at = p.cpred(at[d].rearrange("p (q j) -> p q j", q=4),
                               mask[d].unsqueeze(1).to_broadcast([128, 4, 128]),
                               PB[1][:, :].rearrange("p (q j) -> p q j", q=4), m, *at_read[d])
                self.fr[1] = (t_at,)
                for q in range(4):
                    c = slice(128 * q, 128 * q + 128)
                    m = p.tr(PB[2][:, c], kd[:, c], self.cst("ident"), t_kd, *(self.fr[2] if q == 0 else ()),
                             sig=q == 3)
                kd_read = (m,)
                t_kn = p.act(kdn[d], PB[2][:, :], ACT.Copy, m, *kdn_read[d])
                self.fr[2] = (t_kn,)
                heads.append((t_qb, t_dec, t_at, t_kn))
            first = [True, True]

            def out(e, cols, w, r, *after, sig=False):
                m = p.mm(PB[3 + e][:, cols], w, r, first[e], False, *after, *(self.fr[3 + e] if first[e] else ()),
                         sig=sig, loose=True)
                first[e] = False
                return m

            for d in range(2):
                for q in range(4):
                    for e in range(2):
                        c = slice(128 * q, 128 * q + 128)
                        m = out(e, c, gv[:, q, 256 * h + 128 * e:256 * h + 128 * e + 128], at[d][:, c], heads[d][2],
                                sig=True)
                at_read[d] = (m,)
            t_s = [None, None]
            m_in = [None, None]
            for n in range(8):
                for d in range(2):
                    t_qb, t_dec, t_at, t_kn = heads[d]
                    c = n if d == 0 else 7 - n
                    cc = slice(64 * c, 64 * c + 64)
                    prev, new = sst[d][(n + 1) % 2], sst[d][n % 2]
                    if n > 0:
                        for e in range(2):
                            m_in[d] = out(e, cc, prev[:, 128 * e:128 * e + 128], qb[d][:, cc], t_s[d], t_qb, sig=True)
                    if n < 7:
                        r0 = 64 * (c % 2)
                        q = c // 2
                        b = 5 + d
                        m = p.mm(PB[b][:, 0:256], kdn[d][r0:r0 + 64, 128 * q:128 * q + 128],
                                 gv[r0:r0 + 64, q, 256 * h:256 * h + 256], True, True, t_kn, *self.fr[b], sig=True)
                        kdn_read[d] = (m,)
                        if n == 0:
                            t_s[d] = p.cp(new, PB[b][:, 0:256], m, *qb_read[d])
                        else:
                            t_s[d] = p.stt(new, prev, dec[d][:, c:c + 1], PB[b][:, 0:256], ALU.mult, ALU.add, m, t_dec,
                                           t_s[d])
                            s_read[d] = (t_s[d],)
                        self.fr[b] = (t_s[d],)
            qb_read = [(m_in[0],), (m_in[1],)]
            last = m_in[1]
            for e in range(2):
                t = p.act(sq, PB[3 + e][:, :], ACT.Square, last, *tail)
                m2 = p.mm(PB[7][:, :], self.cst("ones"), sq, e == 0, e == 1, t, *(self.fr[7] if e == 0 else ()),
                          sig=True)
                tail = (m2,)
            t = self.rstd(rr, PB[7][:, :], 256, self.col("eps6"), 128, m2)
            self.fr[7] = (t,)
            for e in range(2):
                i = 2 * h + e
                x = p.stt(H[:, i, :], PB[3 + e][:, :], self.col("gla_norm", i), rr, ALU.mult, ALU.mult, t)
                self.fr[3 + e] = (x,)
                p.tt(H[:, i, :], H[:, i, :], gr[i], ALU.mult, x)
        self.slot_free[slot] = (p.last["pe"],)
        self.barrier()
        self.add_out("w_out_odd", hs, None, None)
        self.barrier()

    def even1(self):
        p, X, H, WK, PB, sm = self.p, self.X, self.H, self.WK, self.PB, self.small
        xs = [X[:, i, :] for i in range(KT)]
        fq = [WK[:, i, :] for i in range(0, 4)]
        fk = [WK[:, i, :] for i in range(4, 8)]
        vaug = WK[:, 8:16, :].rearrange("p a b -> p (a b)").rearrange("p (k h e) -> p k h e", k=4, h=8)
        u = [WK[:, i, :] for i in range(16, 20)]
        c = WK[0:8, 20, :]
        t1, t2, one = WK[0:8, 21, :], WK[0:8, 22, :], WK[0:8, 23, :]
        t_v1 = p.memset(vaug, 1.0)
        t_one = p.memset(one, 1.0)
        self.project("w_in_even_2", 4, KT, xs, None, (0, 1, 2, 3),
                     lambda i, b, m: (p.act(fq[i], PB[b][:, :], ACT.Copy, m, scale=0.125),), 0)
        self.project("w_in_even_2", 4, KT, xs, None, (0, 1, 2, 3),
                     lambda i, b, m: (p.act(fk[i - 4], PB[b][:, :], ACT.Copy, m),), 4)

        def use_v(n, k, b, m):
            v = PB[b][:, :].rearrange("p (h e) -> p h e", h=8)
            t = p.act(vaug[:, k, 0:8:2, 0:64], v[:, 0:8:2, :], ACT.Copy, m, t_v1)
            return (p.act(vaug[:, k, 1:8:2, 64:128], v[:, 1:8:2, :], ACT.Copy, m, t_v1),)

        self.project_rows("w_in_even_2", 8, 4, xs, None, (0, 1, 2, 3), use_v)
        self.project("w_in_even_2", 4, KT, xs, None, (0, 1, 2, 3),
                     lambda i, b, m: (p.act(u[i - 12], PB[b][:, :], ACT.Copy, m),), 12)
        wf, tw, slot = self.load(self.ins["w_fox_f"], [128, 8, 8])
        m = p.group(PB[4][0:8, :], [(wf[:, k, :], xs[k]) for k in range(KT)], tw, *self.fr[4])
        self.slot_free[slot] = (m,)
        t = p.ts(c, PB[4][0:8, :], self.col("fox_fb", 0, 0, 8), None, ALU.add, None, m)
        self.fr[4] = (t,)
        t = self.log_sigmoid(c, c, t1, t2, (t,))
        t = p.scan(t1, one, c, 0.0, ALU.mult, ALU.add, t, t_one)
        cum = t1
        self.barrier()
        self.fox(fq, fk, vaug, cum)
        self.barrier()
        self.s5(u)
        self.barrier()
        self.add_out("w_out_even_2", [H[:, i, :] for i in range(KT)], None, ALPHA)
        self.barrier()
        self.layernorm(0)

    def fox(self, fq, fk, vaug, cum):
        p, H, WK, PB, sm = self.p, self.H, self.WK, self.PB, self.small
        qT = [WK[:, 24, :], WK[:, 25, :]]
        kT = [WK[:, 26, :], WK[:, 27, :]]
        pT = [WK[:, i, :] for i in range(28, 32)]
        rc = WK[:, 32, :]
        mcol = [sm[:, 64:68], sm[:, 68:72]]
        for i in range(2):
            p.memset(qT[i][64:96, :], 0.0)
            p.memset(kT[i][64:96, :], 0.0)
            p.memset(qT[i][96:97, :], 1.0)
            t_one = p.memset(kT[i][64:65, :], 1.0)
        used = [(), ()]
        pt_read = [()] * 4

        def make(h):
            r0 = 64 * (h % 2)
            j = h % 2
            cb = 6 + j
            a = p.act(qT[j][0:64, :], fq[h // 2][r0:r0 + 64, :], ACT.Copy, *used[j])
            b = p.cp(kT[j][0:64, :], fk[h // 2][r0:r0 + 64, :], *used[j])
            m = p.mm(PB[cb][:, :], self.cst("foxsel", 8, 128 * h, 128), cum, True, False, *self.fr[cb], sig=True,
                     loose=True)
            a = p.act(qT[j][64:65, :], PB[cb][64:65, :], ACT.Copy, m, t_one)
            b = p.cp(kT[j][96:97, :], PB[cb][96:97, :], m)
            return a, b

        ready = make(0)
        for h in range(8):
            tq, tk = ready
            j = h % 2
            cb = 6 + j
            q, k = qT[j], kT[j]
            mc = mcol[j]
            for i in range(4):
                b = i % 2
                n = 128 * i + 128
                p.mm(PB[b][:, 0:n], q[0:97, 128 * i:n], k[0:97, 0:n], True, False, tq, tk, *self.fr[b], loose=True)
                m = p.mm(PB[b][:, 128 * i:n], self.cst("ident"), self.cst("maskn"), False, True, sig=True, loose=True)
                t = p.rmax(mc[:, i:i + 1], PB[b][:, 0:n], m)
                self.fr[b] = (t,)
            for i in range(4):
                m = p.mm(PB[cb][64:65, 128 * i:128 * i + 128], mc[:, i:i + 1], self.cst("nident"), False, i == 3, t, tk,
                         sig=i == 3, loose=True)
            t_m = p.act(q[64:65, :], PB[cb][64:65, :], ACT.Copy, m)
            self.fr[cb] = (t_m, tk)
            if h < 7:
                ready = make(h + 1)
            for i in range(4):
                b = 2 + i % 2
                lo = 128 * i
                p.mm(PB[b][:, lo:S], k[0:97, lo:lo + 128], q[0:97, lo:S], True, False, t_m, *self.fr[b], loose=True)
                m = p.mm(PB[b][:, lo:lo + 128], self.cst("ident"), self.cst("maskt"), False, True, sig=True, loose=True)
                t = p.act(pT[i][:, lo:S], PB[b][:, lo:S], ACT.Exp, m, *pt_read[i])
                self.fr[b] = (t,)
                used[j] = (m,)
                m = p.mm(PB[5][:, lo:S], vaug[:, i, h, :], pT[i][:, lo:S], i == 0, i == 3, t,
                         *(self.fr[5] if i == 0 else ()), sig=True, loose=True)
                pt_read[i] = (m,)
            o, s = (slice(0, 64), slice(64, 128)) if h % 2 == 0 else (slice(64, 128), slice(0, 64))
            t = p.recip(rc[o, :], PB[5][s, :], m)
            t = p.tt(H[o, h // 2, :], PB[5][o, :], rc[o, :], ALU.mult, t)
            self.fr[5] = (t,)

    def s5(self, u):
        p, H, WK, PB, sm = self.p, self.H, self.WK, self.PB, self.small
        br, tbr, s_br = self.load(self.ins["s5_br"], [128, 16, 32])
        bi, tbi, s_bi = self.load(self.ins["s5_bi"], [128, 16, 32])
        (dt, mag, th, k, r, cs, sn, nre, nim, den, zr, zi, f, t1) = (
            sm[:, 16 * i:16 * i + 16] for i in range(14))
        are, aim = self.col("a_re", n=16), self.col("a_im", n=16)
        M, A, SB = ALU.mult, ALU.add, ALU.subtract
        t = p.act(dt, self.col("log_dt", n=16), ACT.Exp)
        t = p.tt(mag, are, dt, M, t)
        t_mag = p.act(mag, mag, ACT.Exp, t)
        t = p.tt(th, aim, dt, M)
        t = p.ts(k, th, 1.0 / TWO_PI, MAGIC, M, A)
        t = p.ts(k, k, MAGIC, None, SB, None)
        t = p.stt(r, k, -C1, th, M, A)
        t = p.stt(r, k, -C2, r, M, A)
        t = p.stt(r, k, -C3, r, M, A)
        t = p.ts(r, r, PI_IN, -PI_IN, ALU.min, ALU.max)
        p.ts(f, r, 1.0 / TWO_PI, None, M, None)
        a = p.act(cs, r, ACT.Abs, t)
        a = p.act(cs, cs, ACT.Sin, a, scale=-1.0, bias=self.col("halfpi"))
        a = p.act(sn, r, ACT.Sin, t)
        p.tt(nre, mag, cs, M, a, t_mag)
        p.ts(nre, nre, -1.0, None, A, None)
        p.tt(nim, mag, sn, M)
        p.tt(den, are, are, M)
        p.tt(t1, aim, aim, M)
        p.tt(den, den, t1, A)
        p.recip(den, den)
        p.tt(zr, nre, are, M)
        p.tt(t1, nim, aim, M)
        p.tt(zr, zr, t1, A)
        p.tt(zr, zr, den, M)
        p.tt(zi, nim, are, M)
        p.tt(t1, nre, aim, M)
        p.tt(zi, zi, t1, SB)
        t_z = p.tt(zi, zi, den, M)
        v3 = lambda a: a.rearrange("p (s c) -> p s c", s=16)
        bbr, bbi, tx, bbrT, bbiT, T = (WK[:, i, :] for i in range(0, 6))
        bz = lambda a: a.unsqueeze(2).to_broadcast([128, 16, 32])
        p.tt(v3(bbr), br, bz(zr), M, tbr, tbi, t_z)
        p.tt(v3(tx), bi, bz(zi), M)
        t_r = p.tt(bbr, bbr, tx, SB)
        p.tt(v3(bbi), bi, bz(zr), M)
        p.tt(v3(tx), br, bz(zi), M)
        t_i = p.tt(bbi, bbi, tx, A)
        self.slot_free[s_br] = self.slot_free[s_bi] = (t_i,)
        for b, src, dst, t in ((0, bbr, bbrT, t_r), (1, bbi, bbiT, t_i)):
            for q in range(4):
                cc = slice(128 * q, 128 * q + 128)
                m = p.tr(PB[b][:, cc], src[:, cc], self.cst("ident"), t, *self.fr[b], sig=q == 3)
            t_bt = p.act(dst, PB[b][:, :], ACT.Copy, m)
            self.fr[b] = (t_bt,)
        ti = tx.bitcast(I32)
        t = p.put("pool", lambda e: e.iota(ti, [[1, S]], base=0, channel_multiplier=0), (t_i,))
        t_T = p.cp(T, ti, t)
        cre, tcr, s_cr = self.load(self.ins["s5_cr"], [128, 16, 128])
        cim, tci, s_ci = self.load(self.ins["s5_ci"], [128, 16, 128])
        W2 = [[WK[:, 6 + 10 * i + j, :] for j in range(7)] for i in range(1)] * 2
        co, si, wr, wi, x1, x2, ph = W2[0]
        ph2 = WK[:, 21, :]
        hr = [WK[:, 22, :], WK[:, 24, :]]
        hi = [WK[:, 23, :], WK[:, 25, :]]
        ys = [WK[:, i, :] for i in range(26, 30)]
        read = [(), ()]
        for st in range(16):
            q, kk = st % 4, st // 4
            rows = slice(32 * q, 32 * q + 32)
            bk = 2 * (st % 2)
            mr = p.mm(PB[bk][:, :], bbrT[rows, 128 * kk:128 * kk + 128], u[kk][rows, :], True, True, t_bt,
                      *self.fr[bk], sig=True)
            mi = p.mm(PB[bk + 1][:, :], bbiT[rows, 128 * kk:128 * kk + 128], u[kk][rows, :], True, True,
                      *self.fr[bk + 1], sig=True)
            p.ts(ph, T, f[:, st:st + 1], None, M, None, t_T, *read[st % 2])
            p.ts(ph2, ph, MAGIC, MAGIC, A, SB)
            t = p.tt(ph, ph, ph2, SB)
            a = p.act(si, ph, ACT.Sin, t, scale=6.283184)
            p.act(co, ph, ACT.Abs, t)
            a = p.act(co, co, ACT.Sin, a, scale=-6.283184, bias=self.col("halfpi"))
            p.tt(wr, PB[bk][:, :], co, M, a, mr)
            p.tt(x1, PB[bk + 1][:, :], si, M, mi)
            p.tt(wr, wr, x1, A)
            p.tt(wi, PB[bk + 1][:, :], co, M)
            t = p.tt(x2, PB[bk][:, :], si, M)
            self.fr[bk] = self.fr[bk + 1] = (t,)
            p.tt(wi, wi, x2, SB)
            mg = mag[:, st:st + 1].to_broadcast([128, S])
            p.scan(wr, mg, wr, 0.0, M, A)
            p.scan(wi, mg, wi, 0.0, M, A)
            h_r, h_i = hr[st % 2], hi[st % 2]
            p.tt(h_r, wr, co, M, *read[st % 2])
            p.tt(x1, wi, si, M)
            t_hr = p.tt(h_r, h_r, x1, SB)
            p.tt(x1, wr, si, M)
            p.tt(x2, wi, co, M)
            t_hi = p.stt(h_i, x1, -1.0, x2, M, SB)
            b = 4 + kk % 2
            m = p.mm(PB[b][:, :], cre[:, st, :], h_r, q == 0, False, tcr, t_hr, *(self.fr[b] if q == 0 else ()))
            m = p.mm(PB[b][:, :], cim[:, st, :], h_i, False, q == 3, tci, t_hi, sig=True)
            read[st % 2] = (m,)
            if q == 3:
                t = p.stt(ys[kk], u[kk], self.col("s5_d", kk), PB[b][:, :], M, A, m)
                self.fr[b] = (t,)
        self.slot_free[s_cr] = self.slot_free[s_ci] = (p.last["pe"],)
        ty = [p.act(ys[i], ys[i], ACT.Gelu_apprx_tanh, t) for i in range(4)]

        def use(i, b, m):
            a = p.act(x1 if i % 2 else x2, PB[b][:, :], ACT.Sigmoid, m, p.last["dve"], bias=self.col("b_glu", i))
            p.tt(H[:, 4 + i, :], ys[i], x1 if i % 2 else x2, M, a)
            return (a,)

        self.project("w_glu", 4, 4, ys, ty, (0, 1, 2, 3), use)

    def moe(self, layer):
        p, X, H, WK, PB, sm = self.p, self.X, self.H, self.WK, self.PB, self.small
        xs = [X[:, i, :] for i in range(KT)]
        M, A, SB = ALU.mult, ALU.add, ALU.subtract
        wr, tw, slot = self.load(self.ins[f"w_route{layer}"], [128, 8, 20])
        for q in range(4):
            m = p.group(PB[7][:, 20 * q:20 * q + 20],
                        [(xs[k][:, 128 * q:128 * q + 128], wr[:, k, :]) for k in range(KT)], tw,
                        *(self.fr[7] if q == 0 else ()))
        self.slot_free[slot] = (m,)
        off = [0]

        def tile(*shape):
            n = int(np.prod(shape))
            a = sm[:, off[0]:off[0] + n]
            off[0] += n
            if len(shape) == 2:
                return a.rearrange("p (a b) -> p a b", a=shape[0])
            if len(shape) == 3:
                return a.rearrange("p (a b c) -> p a b c", a=shape[0], b=shape[1])
            return a

        lg = tile(4, 20)
        t = p.tt(lg, PB[7][:, 0:80].rearrange("p (a b) -> p a b", a=4),
                 self.col(f"mb{layer}", n=20).unsqueeze(1).to_broadcast([128, 4, 20]), A, m)
        self.fr[7] = (t,)

        def wide(a, n=4):
            return a.unsqueeze(2).to_broadcast([128, 4, n])

        def softmax(src):
            mx, ex, sn = tile(4), tile(4, 4), tile(4)
            p.rmax(mx, src)
            t = p.tt(ex, src, wide(mx), SB)
            t = p.act(ex, ex, ACT.Exp, t)
            p.rsum(sn, ex, t)
            p.recip(sn, sn)
            p.tt(ex, ex, wide(sn), M)
            return ex

        def top(prob):
            mx, eq, free = tile(4), tile(4, 4), tile(4)
            p.rmax(mx, prob)
            p.tt(eq, prob, wide(mx), ALU.is_equal)
            p.memset(free, 1.0, eng="dve")
            for j in range(4):
                e = eq[:, :, j]
                p.tt(e, e, free, M)
                p.tt(free, free, e, SB)
            return mx, eq

        gp = softmax(lg[:, :, 0:4])
        gv, goh = top(gp)
        pick, el = tile(4, 4), tile(4, 4)
        for g in range(4):
            dst = el if g == 0 else pick
            p.tt(dst, lg[:, :, 4 + 4 * g:8 + 4 * g], wide(goh[:, :, g]), M)
            if g:
                p.tt(el, el, pick, A)
        ep = softmax(el)
        v1, oh1 = top(ep)
        rest = tile(4, 4)
        p.stt(rest, oh1, -2.0, ep, M, A)
        v2, oh2 = top(rest)
        den = tile(4)
        p.tt(den, v1, v2, A)
        p.recip(den, den)
        p.tt(den, den, gv, M)
        p.tt(v1, v1, den, M)
        p.tt(v2, v2, den, M)
        p.tt(oh1, oh1, wide(v1), M)
        p.tt(oh2, oh2, wide(v2), M)
        p.tt(oh1, oh1, oh2, A)
        cb = tile(4, 4, 4)
        for g in range(4):
            t = p.tt(cb[:, :, g, :], oh1, wide(goh[:, :, g]), M)
        cbT = WK[0:16, 32, :]
        for q in range(4):
            m = p.tr(PB[6][0:16, 128 * q:128 * q + 128], cb[:, q, :, :].rearrange("p a b -> p (a b)"),
                     self.cst("ident"), t, *self.fr[6], sig=q == 3)
        t_cb = p.cp(cbT, PB[6][0:16, :], m)
        self.fr[6] = (t_cb,)

        hid = [WK[:, i, :] for i in range(32)]
        sl = [WK[:, 33 + i, :] for i in range(3)]
        hold = {}
        done = []

        def use(t, b, m):
            e, f, n = t // 4, (t % 4) // 2, t // 2
            if t % 2 == 0:
                hold["s"] = p.act(sl[n % 3], PB[b][:, :], ACT.Silu, m, *(done[n - 3:n - 2] if n >= 3 else ()))
                return (hold["s"],)
            if f == 0:
                cbk = 6 + e % 2
                hold["c"] = p.mm(PB[cbk][:, :], self.cst("sel", 16, 128 * e, 128), cbT, True, True, t_cb,
                                 *self.fr[cbk], sig=True)
            x = p.tt(sl[n % 3], sl[n % 3], PB[b][:, :], M, m, hold["s"])
            d = p.tt(hid[n], sl[n % 3], PB[6 + e % 2][:, :], M, x, hold["c"])
            self.fr[6 + e % 2] = (d,)
            done.append(d)
            return (x,)

        self.project(f"moe_up{layer}", 64, KT, xs, None, (0, 1, 2, 3), use)
        self.add_out(f"moe_down{layer}", hid, done, ALPHA, 32, (4, 5))
        self.barrier()
        self.layernorm(2 * layer + 1)

    def odd1(self):
        p, X, H, WK, PB, sm = self.p, self.X, self.H, self.WK, self.PB, self.small
        xs = [X[:, i, :] for i in range(KT)]
        M, A, SB, MX = ALU.mult, ALU.add, ALU.subtract, ALU.max
        qk = [WK[:, i, :] for i in range(16)]
        vv = WK[:, 16:24, :].rearrange("p (q a) b -> p q (a b)", q=4)
        og = [WK[:, i, :] for i in range(24, 32)]

        def conv(i, b, m):
            ps, c = PB[b], qk[i]
            w = [self.col("mcw", 16 * j + i) for j in range(4)]
            a = p.act(c, ps[:, :], ACT.Identity, m, scale=w[3], bias=self.col("mcb", i))
            for j in range(3):
                s = 3 - j
                a = p.stt(c[:, s:S], ps[:, 0:S - s], w[j], c[:, s:S], M, A, a)
            p.act(c, c, ACT.Silu, a)
            return (a,)

        self.project("w_in_odd_2", 16, KT, xs, None, (0, 1, 2, 3), conv, 0)
        self.project_rows("w_in_odd_2", 16, 8, xs, None, (0, 1, 2, 3),
                          lambda n, q, b, m: (p.act(vv[:, q, 512 * n:512 * n + 512], PB[b][:, :], ACT.Copy, m),))
        self.project("w_in_odd_2", 8, KT, xs, None, (0, 1, 2, 3),
                     lambda i, b, m: (p.act(og[i - 24], PB[b][:, :], ACT.Sigmoid, m),), 24)
        wg, tw, slot = self.load(self.ins["w_mgate"], [128, 8, 64])
        m = p.group(PB[4][0:64, :], [(wg[:, k, :], xs[k]) for k in range(KT)], tw, *self.fr[4])
        self.slot_free[slot] = (m,)
        ig, z, t1, t2, F_, a_, mx, en = (WK[0:8, 32 + i, :] for i in range(8))
        one = WK[0:8, 40, :]
        t_one = p.memset(one, 1.0)
        t_i = p.ts(ig, PB[4][0:8, :], self.col("ib", 0, 0, 8), None, A, None, m)
        t = p.act(z, PB[4][32:40, :], ACT.Identity, m, bias=self.col("fb", 0, 32, 40))
        self.fr[4] = (t, t_i)
        t = self.log_sigmoid(z, z, t1, t2, (t,))
        p.scan(F_, one, z, 0.0, M, A, t, t_one)
        p.tt(a_, ig, F_, SB)
        t_mx = p.scan(mx, a_, a_, 0.0, MX, MX)
        t = p.tt(t1, F_, mx, A)
        t_en = p.act(en, t1, ACT.Exp, t, scale=-1.0)
        ac = sm[:, 0:32].rearrange("p (j h) -> p j h", j=4)
        for j in range(4):
            m = p.tr(PB[5][:, 8 * j:8 * j + 8], a_[:, 128 * j:128 * j + 128], self.cst("ident", 8, 0, 8), t_mx,
                     *self.fr[5], sig=j == 3)
        t_ac = p.cp(ac, PB[5][:, 0:32].rearrange("p (j h) -> p j h", j=4), m)
        self.barrier()
        dd = [WK[:, i, :] for i in (32, 33)]
        stt_ = [WK[:, i, :] for i in (34, 35, 36)]
        sc = 128.0 ** -0.5
        dread = [(), ()]
        sread = [(), (), ()]
        n = 0
        for h in range(8):
            mb = 6 + h % 2
            m_b = p.mm(PB[mb][:, :], self.cst("sel", 8, 128 * h, 128), mx, True, True, *self.fr[mb], sig=True)
            nb = 3 + h % 2
            for j in range(4):
                lo = 128 * j
                d, st = dd[n % 2], stt_[n % 3]
                t = p.ts(d[:, lo:S], PB[mb][:, lo:S], ac[:, j, h:h + 1], 0.0, SB, MX, m_b, *dread[n % 2])
                t = p.act(d[:, lo:S], d[:, lo:S], ACT.Exp, t, scale=-1.0)
                t_d = p.tt(d[:, lo:lo + 128], d[:, lo:lo + 128], self.cst("causal"), M, t, eng="pool")
                b = n % 3
                m = p.mm(PB[b][:, lo:S], qk[8 + h][:, lo:lo + 128], qk[h][:, lo:S], True, True, *self.fr[b], sig=True)
                t = p.stt(st[:, lo:S], PB[b][:, lo:S], sc, d[:, lo:S], M, M, m, t_d, *sread[n % 3])
                self.fr[b] = (t,)
                dread[n % 2] = (t,)
                m = p.mm(PB[nb][:, lo:S], vv[:, j, 128 * h:128 * h + 128], st[:, lo:S], j == 0, j == 3, t,
                         *(self.fr[nb] if j == 0 else ()), sig=True, loose=True)
                m = p.mm(PB[5][0:8, lo:S], self.cst("oh", 128, 8 * h, 8), st[:, lo:S], h == 0 and j == 0,
                         h == 7 and j == 3, sig=True, loose=True)
                sread[n % 3] = (m,)
                n += 1
            self.fr[mb] = dread[(n - 1) % 2]
            t = p.act(H[:, h, :], PB[nb][:, :], ACT.Copy, m)
            self.fr[nb] = (t,)
        den = WK[0:8, 37, :]
        t = p.act(den, PB[5][0:8, :], ACT.Abs, m)
        p.tt(den, den, en, MX, t, t_en)
        t = p.recip(den, den)
        for h in range(8):
            mb = 6 + h % 2
            m = p.mm(PB[mb][:, :], self.cst("sel", 8, 128 * h, 128), den, True, True, t, *self.fr[mb], sig=True)
            x = p.tt(H[:, h, :], H[:, h, :], PB[mb][:, :], M, m)
            self.fr[mb] = (x,)
            p.tt(H[:, h, :], H[:, h, :], og[h], M, x)
        self.barrier()
        self.add_out("w_out_odd_2", [H[:, i, :] for i in range(KT)], None, ALPHA)
        self.barrier()
        self.layernorm(2)

    PHASES = ("even0", "ffn0", "odd0", "ffn1", "even1", "moe0", "odd1", "moe1")

    def finish(self):
        p = self.p
        now = [p.last[k] for k in ("pe", "act", "dve", "pool") if p.last[k] is not None]
        s = self.sem("dout")
        t = p.dma("sp", self.out.rearrange("(t p) s -> p t s", p=128), self.X[:, :, :], s, 16, now)
        p.wait_all("sp", [t])
        with self.nc.Block() as block:
            @block.sync
            def _(e):
                p.run("sp", e)

            @block.tensor
            def _(e):
                p.run("pe", e)

            @block.scalar
            def _(e):
                p.run("act", e)

            @block.vector
            def _(e):
                p.run("dve", e)

            @block.gpsimd
            def _(e):
                p.run("pool", e)


def build(nc, ins, out, phases=Build.PHASES):
    b = Build(nc, ins, out)
    with b.ctx:
        b.setup()
        table = {"even0": b.even0, "ffn0": lambda: b.ffn(0), "odd0": b.odd0, "ffn1": lambda: b.ffn(1),
                 "even1": b.even1, "moe0": lambda: b.moe(0), "odd1": b.odd1, "moe1": lambda: b.moe(1)}
        for name in phases:
            table[name]()
        b.finish()


def tiles_of(w, order=None):
    k, n = w.shape
    nt = -(-n // 128)
    out = np.zeros((k, nt * 128), w.dtype)
    out[:, :n] = w
    out = out.reshape(k // 128, 128, nt, 128).transpose(2, 1, 0, 3)
    return np.ascontiguousarray(out if order is None else out[order])


def pair_up(a, b):
    ta, tb = tiles_of(a), tiles_of(b)
    return np.ascontiguousarray(np.stack([ta, tb], 1).reshape(-1, *ta.shape[1:]))


def rows_of(w):
    k, n = w.shape
    return np.ascontiguousarray(w.reshape(k // 128, 128, n).transpose(1, 0, 2))


def constants():
    c = np.zeros((128, NCST), np.float32)

    def at(name):
        a, w = CST[name]
        return c[:, a:a + w]

    i = np.arange(128)
    at("ident")[:] = np.eye(128)
    at("nident")[:] = -np.eye(128)
    at("ones")[:] = 1
    at("bd64")[:] = i[:, None] // 64 == i[None] // 64
    for name, lo, hi, size, half in (("rot64", 0, 128, 64, 32), ("rot96", 64, 96, 32, 16)):
        m = at(name)
        for o in range(lo, hi):
            if (o - lo) % size < half:
                m[o + half, o] = -1
            else:
                m[o - half, o] = 1
    at("maskn")[:] = np.where(i[None] > i[:, None], np.float32(-1e30), 0)
    at("maskt")[:] = np.where(i[:, None] > i[None], np.float32(-1e30), 0)
    same = i[:, None] // 64 == i[None] // 64
    at("mf")[:] = same & (i[:, None] <= i[None])
    at("mb")[:] = same & (i[:, None] > i[None])
    at("causal")[:] = i[:, None] <= i[None]
    for e in range(16):
        at("sel")[e, 128 * e:128 * e + 128] = 1
    for h in range(8):
        at("foxsel")[h, 128 * h + 64] = 1
        at("foxsel")[h, 128 * h + 96] = -1
        at("oh")[:, 8 * h + h] = 1
    return c


def layout(**a):
    f32 = np.float32
    a = {k: np.asarray(v) for k, v in a.items()}
    out = {}
    out["xT"] = np.ascontiguousarray(a["x"][0].T)
    out["posb"] = np.ascontiguousarray(np.broadcast_to(a["positions"].reshape(1, S), (128, S)))
    out["csts"] = constants()
    cols = np.zeros((128, NCOL), f32)

    def put(name, v, i=0):
        v = np.asarray(v).reshape(-1)
        n = -(-v.size // 128)
        full = np.zeros(n * 128, f32)
        full[:v.size] = v
        c = COL[name][0] + i
        cols[:, c:c + n] = full.reshape(n, 128).T

    put("mix_even", a["mix_norm_even"])
    put("q_norm", a["mla_q_norm"])
    put("kv_norm", a["mla_kv_norm"])
    put("qhn", a["mla_q_head_norm"])
    put("khn", a["mla_k_head_norm"])
    put("ret_norm", a["ret_out_norm"])
    for name, v, n in (("th_f", a["ret_theta_fwd"][0], 8), ("th_b", a["ret_theta_bwd"][0], 8)):
        cols[:, COL[name][0]:COL[name][0] + n] = v[None]
    put("mix_odd", a["mix_norm_odd"])
    put("gb_f", a["gla_b_gate_fwd"])
    put("gb_b", a["gla_b_gate_bwd"])
    put("gla_norm", a["gla_out_norm"])
    for l in range(2):
        put(f"ffn{l}", a["ffn_norm"][l])
        put(f"cw{l}", a["ffn_conv_w"][l])
        put(f"cb{l}", a["ffn_conv_b"][l])
        c = COL[f"mb{l}"][0]
        cols[:, c:c + 4] = a["moe_b_group_2"][l][None]
        cols[:, c + 4:c + 20] = a["moe_b_expert_2"][l].reshape(1, 16)
    put("lng", a["ln_g_2"])
    put("lnb", a["ln_b_2"])
    put("fox_fb", a["fox_f_bias_2"])
    put("a_re", a["s5_a_re_2"])
    put("a_im", a["s5_a_im_2"])
    put("log_dt", np.repeat(a["s5_log_dt_2"].reshape(32), 64))
    put("s5_d", a["s5_d_2"])
    put("b_glu", a["s5_b_glu_2"])
    put("mcw", a["mlstm_conv_w_2"])
    put("mcb", a["mlstm_conv_b_2"])
    put("ib", a["mlstm_i_bias_2"])
    cols[32:40, COL["fb"][0]] = a["mlstm_f_bias_2"][0]
    inv32 = (f32(10000.0) ** (-np.arange(32, dtype=f32) / f32(32))).astype(f32)
    inv16 = (f32(10000.0) ** (-np.arange(16, dtype=f32) / f32(16))).astype(f32)
    cols[:, COL["inv64"][0]] = np.tile(inv32, 4)
    cols[64:96, COL["inv96"][0]] = np.tile(inv16, 2)
    cols[:, COL["eps6"][0]] = 1e-6
    cols[:, COL["eps5"][0]] = 1e-5
    cols[:, COL["halfpi"][0]] = np.pi / 2
    cols[:, COL["one"][0]] = 1
    out["cols"] = cols

    w = a["w_in_even"][0]
    cut = np.cumsum([0, 384, 256, 32, 512, 512, 512, 512])
    cq, ckv, kro, rq, rk, rv, rg = (w[:, cut[i]:cut[i + 1]] for i in range(7))
    out["w_in_even"] = np.concatenate([tiles_of(x) for x in (rq, rk, rv, rg, cq, kro, ckv)])
    out["w_uq"] = np.ascontiguousarray(a["mla_w_uq"][0].reshape(3, 128, 8, 96).transpose(1, 2, 0, 3)).reshape(128, -1)
    kv = a["mla_w_ukv"][0].reshape(2, 128, 8, 2, 64).transpose(1, 3, 0, 2, 4)
    out["w_ukv"] = np.ascontiguousarray(kv).reshape(128, -1)
    out["w_out_even"] = tiles_of(a["w_out_even"][0])
    out["w_in_odd"] = tiles_of(a["w_in_odd"][0])
    g = np.zeros((32, 2, 512), f32)
    g[0:16, 0] = a["gla_w_gate_fwd"][0]
    g[16:32, 1] = a["gla_w_gate_bwd"][0]
    out["w_gate"] = g.reshape(32, -1)
    out["w_out_odd"] = tiles_of(a["w_out_odd"][0])
    for l in range(2):
        up = a["ffn_w_up"][l]
        out[f"w_up{l}"] = pair_up(up[:, :2816], up[:, 2816:])
        out[f"w_down{l}"] = tiles_of(a["ffn_w_down"][l])
        wr = np.concatenate([a["moe_w_group_2"][l], a["moe_w_expert_2"][l].transpose(1, 0, 2).reshape(D, 16)], 1)
        out[f"w_route{l}"] = rows_of(wr).reshape(128, -1)
        flat = lambda v: v.transpose(1, 0, 2).reshape(D, 16 * 256)
        out[f"moe_up{l}"] = pair_up(flat(a["moe_w_gate_2"][l]), flat(a["moe_w_up_2"][l]))
        out[f"moe_down{l}"] = tiles_of(a["moe_w_down_2"][l].reshape(16 * 256, D))
    w = a["even_w_in_2"][0]
    out["w_in_even_2"] = tiles_of(np.concatenate([w[:, 0:1536], w[:, 1544:2056]], 1))
    out["w_fox_f"] = rows_of(w[:, 1536:1544]).reshape(128, -1)
    for name, v in (("s5_br", a["s5_b_re_2"][0]), ("s5_bi", a["s5_b_im_2"][0])):
        m = np.zeros((16, 2, 64, 2, 16), f32)
        for g2 in range(2):
            m[:, g2, :, g2, :] = v[g2::2]
        out[name] = np.ascontiguousarray(m.transpose(1, 2, 0, 3, 4)).reshape(128, -1)
    for name, v in (("s5_cr", a["s5_c_re_2"][0]), ("s5_ci", a["s5_c_im_2"][0])):
        m = np.zeros((2, 64, 16, 128), f32)
        for st in range(16):
            for g2 in range(2):
                c = 32 * (st % 4) + 16 * g2
                m[g2, :, st, c:c + 16] = v[2 * st + g2].T
        out[name] = m.reshape(128, -1)
    out["w_glu"] = tiles_of(a["s5_w_glu_2"][0])
    out["w_out_even_2"] = tiles_of(a["even_w_out_2"][0])
    w = a["odd_w_in_2"][0]
    out["w_in_odd_2"] = tiles_of(w[:, :4096])
    g = np.zeros((D, 64), f32)
    g[:, 0:8] = w[:, 4096:4104]
    g[:, 32:40] = w[:, 4104:4112]
    out["w_mgate"] = rows_of(g).reshape(128, -1)
    out["w_out_odd_2"] = tiles_of(a["odd_w_out_2"][0])
    return out


def kernel(**inputs):
    import concourse.bacc as bacc
    from concourse.bass_utils import run_bass_kernel_spmd

    arrays = layout(**inputs)
    nc = bacc.Bacc("TRN2", target_bir_lowering=False, num_devices=1)
    ins = {k: nc.dram_tensor(f"in_{k}", v.shape, mybir.dt.from_np(v.dtype), kind="ExternalInput").ap()
           for k, v in arrays.items()}
    out = nc.dram_tensor("outT", (D, S), F32, kind="ExternalOutput").ap()
    build(nc, ins, out)
    r = run_bass_kernel_spmd(nc, [{f"in_{k}": v for k, v in arrays.items()}], core_ids=[0])
    return np.ascontiguousarray(r.results[0]["outT"].T)[None]
```

```python
from contextlib import ExitStack

import numpy as np

import concourse.bass as bass
from concourse import mybir

ALU = mybir.AluOpType
ACT = mybir.ActivationFunctionType
F32 = mybir.dt.float32
F16 = mybir.dt.float16
U32 = mybir.dt.uint32
I32 = mybir.dt.int32
AX = mybir.AxisListType.X

S = 512
D = 1024
KT = 8
FF = 22
SLOT = 4096
NT = 50
MAGIC = 12582912.0
TWO_PI = 6.283185307179586
C1 = 6.28125
C2 = 0.0019350051879882812
C3 = TWO_PI - C1 - C2
PI_IN = 3.1415925
ALPHA = 4.0 ** 0.25

COL = {}
_n = 0
for _name, _w in (
    ("mix_even", 8), ("q_norm", 3), ("kv_norm", 2), ("qhn", 1), ("khn", 1), ("ret_norm", 4),
    ("th_f", 8), ("th_b", 8), ("mix_odd", 8), ("gb_f", 4), ("gb_b", 4), ("gla_norm", 8),
    ("ffn0", 8), ("ffn1", 8), ("cw0", 66), ("cw1", 66), ("cb0", 22), ("cb1", 22),
    ("lng", 32), ("lnb", 32), ("fox_fb", 1), ("a_re", 16), ("a_im", 16), ("log_dt", 16),
    ("s5_d", 4), ("b_glu", 4), ("mcw", 64), ("mcb", 16), ("ib", 1), ("fb", 1),
    ("mb0", 20), ("mb1", 20), ("inv64", 1), ("inv96", 1), ("eps6", 1), ("eps5", 1),
    ("halfpi", 1), ("one", 1),
):
    COL[_name] = (_n, _w)
    _n += _w
NCOL = _n

CST = {}
_n = 0
for _name, _w in (
    ("ident", 128), ("nident", 128), ("ones", 128), ("bd64", 128), ("rot64", 128), ("rot96", 128),
    ("maskn", 128), ("maskt", 128), ("mf", 128), ("mb", 128), ("causal", 128),
    ("oh", 64),
):
    CST[_name] = (_n, _w)
    _n += _w
NCST = _n


WEIGHTS = (
    ("w_in_even", 22, 8), ("w_out_even", 8, 8), ("w_up0", 44, 8), ("w_down0", 8, 22),
    ("w_in_odd", 25, 8), ("w_out_odd", 8, 8), ("w_up1", 44, 8), ("w_down1", 8, 22),
    ("w_in_even_2", 16, 8), ("w_glu", 4, 4), ("w_out_even_2", 8, 8), ("w_in_odd_2", 32, 8), ("w_out_odd_2", 8, 8),
)
PHASE_OF = {
    "even0": ("w_in_even", "w_out_even"), "ffn0": ("w_up0", "w_down0"), "odd0": ("w_in_odd", "w_out_odd"),
    "ffn1": ("w_up1", "w_down1"), "even1": ("w_in_even_2", "w_glu", "w_out_even_2"),
    "moe0": (), "odd1": ("w_in_odd_2", "w_out_odd_2"), "moe1": (),
}


class Split:

    def __init__(self, hi, lo, ready, inv, t_inv):
        self.hi, self.lo, self.ready, self.inv, self.t_inv = hi, lo, ready, inv, t_inv


class Queues:

    def __init__(self, sem):
        self.make = sem
        self.q = {k: [] for k in ("pe", "act", "dve", "pool", "sp")}
        self.waited = {k: {} for k in self.q}
        self.last = {k: None for k in self.q}
        self.stage = 0
        self.fresh()

    def fresh(self):
        self.sem = {k: self.make(f"s_{k}{self.stage}") for k in ("pe", "act", "dve", "pool")}
        self.count = {k: 0 for k in self.sem}
        self.stage += 1

    def put(self, k, fn, after, sig=True):
        waits = []
        if k in ("act", "dve", "pool"):
            after = [*after, self.last[k]]
        for t in after:
            if t is None:
                continue
            if isinstance(t[0], tuple):
                self.put_waits(k, t, waits)
                continue
            s, v = t
            if self.waited[k].get(id(s), 0) < v:
                self.waited[k][id(s)] = v
                waits = [w for w in waits if w[0] is not s] + [t]
        tok = None
        if sig:
            self.count[k] += 1
            tok = (self.sem[k], self.count[k])
            self.last[k] = tok
        self.q[k].append((waits, fn, (tok[0], 1) if sig else None))
        return tok

    def put_waits(self, k, pair, waits):
        for s, v in pair:
            if self.waited[k].get(id(s), 0) < v:
                self.waited[k][id(s)] = v
                waits.append((s, v))

    def dma(self, k, out, in_, sem, value, after=()):
        waits = []
        for t in after:
            if t is not None and self.waited[k].get(id(t[0]), 0) < t[1]:
                self.waited[k][id(t[0])] = t[1]
                waits.append(t)
        self.q[k].append((waits, lambda e: e.dma_start(out, in_), (sem, 16)))
        return (sem, value)

    def gather(self, out, table, rows, sem, value, *after):
        waits = []
        for t in after:
            if t is not None and self.waited["pool"].get(id(t[0]), 0) < t[1]:
                self.waited["pool"][id(t[0])] = t[1]
                waits.append(t)
        at = bass.IndirectOffsetOnAxis(rows, 0)
        self.q["pool"].append((waits, lambda e: e.indirect_dma_start(out, None, table, at), (sem, 16)))
        return (sem, value)

    def wait_all(self, k, after):
        self.q[k].append((list(after), None, None))

    def run(self, k, e):
        for waits, fn, inc in self.q[k]:
            for s, v in waits:
                e.wait_ge(s, v)
            if fn is not None:
                ins = fn(e)
                if inc is not None:
                    ins.then_inc(*inc)

    def tt(self, out, a, b, op, *after, eng="dve"):
        return self.put(eng, lambda e: e.tensor_tensor(out, a, b, op), after)

    def ts(self, out, a, s1, s2, op0, op1, *after, eng="dve"):
        if s2 is None:
            return self.put(eng, lambda e: e.tensor_scalar(out, a, s1, None, op0), after)
        return self.put(eng, lambda e: e.tensor_scalar(out, a, s1, s2, op0, op1), after)

    def stt(self, out, a, s, b, op0, op1, *after):
        return self.put("dve", lambda e: e.scalar_tensor_tensor(out, a, s, b, op0, op1), after)

    def scan(self, out, d0, d1, init, op0, op1, *after):
        return self.put("dve", lambda e: e.tensor_tensor_scan(out, d0, d1, init, op0, op1), after)

    def rmax(self, out, a, *after):
        return self.put("dve", lambda e: e.tensor_reduce(out, a, AX, ALU.max), after)

    def rsum(self, out, a, *after):
        return self.put("dve", lambda e: e.tensor_reduce(out, a, AX, ALU.add), after)

    def recip(self, out, a, *after):
        return self.put("dve", lambda e: e.reciprocal(out, a), after)

    def cp(self, out, a, *after, eng="dve"):
        return self.put(eng, lambda e: e.tensor_copy(out, a), after)

    def cpred(self, out, mask, a, *after):
        return self.put("dve", lambda e: e.copy_predicated(out, mask, a), after)

    def memset(self, out, v, *after, eng="pool"):
        return self.put(eng, lambda e: e.memset(out, v), after)

    def act(self, out, a, f, *after, scale=1.0, bias=0.0, total=None):
        if total is not None:
            return self.put("act", lambda e: e.activation(out, a, f, bias=bias, scale=scale, accum_out=total), after)
        return self.put("act", lambda e: e.activation(out, a, f, bias=bias, scale=scale), after)

    def over_partitions(self, out, a, *after):
        return self.put("pool", lambda e: e.partition_all_reduce(out, a, 128, bass.bass_isa.ReduceOp.add), after)

    def mm(self, out, lhsT, rhs, start, stop, *after, sig=False, loose=False):
        return self.put("pe", lambda e: e.matmul(out, lhsT, rhs, start=start, stop=stop,
                                                 skip_group_check=loose), after, sig)

    def tr(self, out, a, ident, *after, sig=False):
        return self.put("pe", lambda e: e.transpose(out, a, ident), after, sig)

    def group(self, out, pairs, *after, start=True, stop=True, loose=False, each=None):
        t = None
        for i, (w, r) in enumerate(pairs):
            last = i == len(pairs) - 1
            own = after if i == 0 else ()
            if each is not None:
                own = (*own, each[i])
            t = self.mm(out, w, r, start and i == 0, stop and last, *own, sig=last, loose=loose)
        return t


class Build:
    def __init__(self, nc, ins, out):
        self.nc, self.ins, self.out = nc, ins, out
        self.ctx = ExitStack()

    def sb(self, name, shape, dt=F32):
        return self.ctx.enter_context(self.nc.sbuf_tensor(name, shape, dt))

    def sem(self, name):
        return self.ctx.enter_context(self.nc.semaphore(name))

    def col(self, name, i=0, p0=0, p1=128, n=1):
        a = COL[name][0] + i
        return self.cols[p0:p1, a:a + n]

    def cst(self, name, p=128, a=0, n=None):
        c, w = CST[name]
        n = w if n is None else n
        return self.csts[0:p, c + a:c + a + n]

    def setup(self, phases):
        nc = self.nc
        self.X = self.sb("X", [128, KT, S])
        self.T = self.sb("T", [128, NT, S])
        self.WK = self.T
        self.H = self.T[:, 42:50, :]
        self.AS = self.sb("AS", [128, 2 * KT, S], F16)
        self.raw = self.sb("raw", [128, 2, SLOT])
        self.WS = self.sb("WS", [128, 2, 2, SLOT], F16)
        self.junk = self.sb("junk", [128, 1024], F16)
        self.cols = self.sb("cols", [128, NCOL])
        self.csts = self.sb("csts", [128, NCST])
        self.small = self.sb("small", [128, 320])
        self.sc = self.sb("sc", [128, 96])
        self.PB = [self.ctx.enter_context(nc.psum_tensor(f"PB{i}", [128, S], F32)) for i in range(8)]
        self.p = Queues(self.sem)
        self.raw_sem = [self.sem(f"dw{i}") for i in range(2)]
        self.n_side = 0
        self.named = {}
        s0 = [self.sem(f"di{i}") for i in range(3)]
        p = self.p
        self.t_cols = p.dma("sp", self.cols[:, :], self.ins["cols"], s0[2], 16)
        self.t_x = p.dma("sp", self.X[:, :, :], self.ins["xT"].rearrange("(t p) s -> p t s", p=128), s0[0], 16)
        self.t_csts = p.dma("sp", self.csts[:, :], self.ins["csts"], s0[1], 16)
        self.fr = [()] * 8
        for k in ("pe", "act", "dve", "pool"):
            p.wait_all(k, [self.t_csts, self.t_cols, self.t_x])
        self.chunks = []
        names = [n for ph in phases for n in PHASE_OF[ph]]
        for name, nt, kt in WEIGHTS:
            per = min(4, SLOT // (kt * 128))
            if name in names:
                self.chunks += [(name, t, min(t + per, nt), kt) for t in range(0, nt, per)]
        self.raw_tok, self.raw_free, self.pe_done, self.evac, self.inv_tok = {}, {}, {}, {}, {}
        self.part_tok = {}
        self.at = 0
        self.todo = []
        self.prepared = -1
        self.load_chunk(0)
        self.load_chunk(1)
        for i, cs in enumerate((("mix_even", 0, 8), ("ffn0", 0, 8), ("mix_odd", 0, 8), ("ffn1", 0, 8))):
            t = p.act(self.junk[:, 0:8], self.col(cs[0], n=8), ACT.Square, total=self.sc[:, 48 + i:49 + i])
        for i in range(3):
            for name in ("lng", "lnb"):
                c = 56 + 2 * i + (name == "lnb")
                t = p.act(self.junk[:, 0:8], self.col(name, 8 * i, n=8), ACT.Square, total=self.sc[:, c:c + 1])
        v = self.sc[:, 56:62].rearrange("p (a b) -> p a b", b=2)
        t = p.tt(self.sc[:, 52:55], v[:, :, 0], v[:, :, 1], ALU.add, t)
        t = p.over_partitions(self.sc[:, 56:63], self.sc[:, 48:55], t)
        self.t_gain = self.scale_of(self.sc[:, 56:63], 10, self.sc[:, 64:71], self.sc[:, 72:79], self.sc[:, 80:87], t)
        self.flush()

    def scale_of(self, total, log2n, s, inv, tmp, *after):
        p = self.p
        ti, si = tmp.bitcast(I32), s.bitcast(I32)
        t = p.ts(ti, total.bitcast(I32), 23, None, ALU.logical_shift_right, None, *after)
        t = p.cp(s, ti, t)
        t = p.ts(s, s, -0.5, 130 + 63.5 + log2n / 2, ALU.mult, ALU.add, t)
        t = p.cp(ti, s, t)
        t = p.ts(si, ti, 23, None, ALU.logical_shift_left, None, t)
        return p.recip(inv, s, t)

    def load_chunk(self, i):
        if i >= len(self.chunks):
            return
        name, t0, t1, kt = self.chunks[i]
        out = self.raw[:, i % 2, 0:(t1 - t0) * kt * 128].rearrange("p (t n) -> p t n", t=t1 - t0)
        src = self.ins[name][t0:t1].rearrange("t p k c -> p t (k c)")
        self.raw_tok[i] = self.p.dma("sp", out, src, self.raw_sem[i % 2], 16 * (i // 2 + 1), self.raw_free.get(i - 2, ()))

    def steps(self, i):
        p = self.p
        name, t0, t1, kt = self.chunks[i]
        n = (t1 - t0) * kt * 32
        j = i % 2
        c = 16 * j
        st, ar, tot, s, inv, tmp = (self.sc[:, c + a:c + b] for a, b in ((0, 4), (4, 8), (8, 9), (9, 10), (10, 11), (11, 12)))
        raw = [self.raw[:, j, n * q:n * q + n] for q in range(4)]
        hi = [self.WS[:, j, 0, n * q:n * q + n] for q in range(4)]
        lo = [self.WS[:, j, 1, n * q:n * q + n] for q in range(4)]
        box = {}

        def square(q):
            box["t"] = p.act(self.junk[:, 0:n], raw[q], ACT.Square, self.raw_tok[i], total=st[:, q:q + 1])

        def scale():
            t = p.over_partitions(ar, st, box["t"])
            t = p.rsum(tot, ar, t)
            box["s"] = self.inv_tok[i] = self.scale_of(tot, 19, s, inv, tmp, t)

        def part(q):
            a = p.act(hi[q], raw[q], ACT.Identity, box["s"], self.pe_done.get(i - 2), scale=s)
            b = p.stt(lo[q], raw[q], s, hi[q], ALU.mult, ALU.subtract, a)
            if q == 3:
                self.raw_free[i] = (a, b)
                self.part_tok[i] = b
                self.load_chunk(i + 2)

        return [lambda q=q: square(q) for q in range(4)] + [scale] + [lambda q=q: part(q) for q in range(4)]

    def advance(self, n):
        for _ in range(n):
            if not self.todo:
                return
            self.todo.pop(0)()

    def flush(self):
        if self.prepared < self.at < len(self.chunks):
            self.todo = self.steps(self.at)
            self.prepared = self.at
        self.advance(len(self.todo))

    def chunk(self, name, t0, t1, kt, act):
        i = self.at
        assert self.chunks[i] == (name, t0, t1, kt), (self.chunks[i], name, t0, t1, kt)
        self.flush()
        c = 32 + i % 4
        sc = self.sc[:, c:c + 1]
        t_sc = self.p.tt(sc, self.sc[:, 16 * (i % 2) + 10:16 * (i % 2) + 11], act.inv, ALU.mult, self.inv_tok[i],
                         act.t_inv, *self.evac.get(i - 4, ()))
        w = [self.WS[:, i % 2, h, 0:(t1 - t0) * kt * 128].rearrange("p (t k c) -> p t k c", t=t1 - t0, k=kt)
             for h in range(2)]
        self.at += 1
        if self.at < len(self.chunks):
            self.todo = self.steps(self.at)
            self.prepared = self.at
        return i, w[0], w[1], sc, t_sc

    def side(self, name, out, *after):
        self.n_side += 1
        return self.p.dma("pool", out, self.ins[name], self.sem(f"dv{self.n_side}"), 16, after)

    def flat(self, t0, t1, n, p=128):
        return self.T[0:p, t0:t1, :].rearrange("p a b -> p (a b)")[:, 0:n]

    def barrier(self):
        p = self.p
        now = [p.last[k] for k in ("pe", "act", "dve", "pool") if p.last[k] is not None]
        for k in ("pe", "act", "dve", "pool"):
            p.wait_all(k, now)
        p.fresh()
        self.fr = [()] * 8

    def rstd(self, out, bank, n, eps, rows, *after):
        p = self.p
        t = p.act(out, bank, ACT.Ln, *after, scale=1.0 / n, bias=eps)
        return p.act(out, out, ACT.Exp, t, scale=-0.5)

    def norm_stat(self, src, n, bank, tmp, ready):
        p = self.p
        used = [(), ()]
        for i, a in enumerate(src):
            sq = tmp[i % 2]
            t = p.act(sq, a, ACT.Square, ready, *used[i % 2])
            m = p.mm(self.PB[bank][:, :], self.cst("ones"), sq, i == 0, i == len(src) - 1, t,
                     *(self.fr[bank] if i == 0 else ()), sig=True)
            used[i % 2] = (m,)
        t = self.rstd(tmp[2], self.PB[bank][:, :], n, self.col("eps6"), 128, m)
        self.fr[bank] = (t,)
        return t

    def rmsnorm(self, src, gain, dst, n, bank, tmp, ready):
        t = self.norm_stat(src, n, bank, tmp, ready)
        return [self.p.stt(d, a, g, tmp[2], ALU.mult, ALU.mult, t) for d, a, g in zip(dst, src, gain)]

    def normed(self, name, which, tmp):
        p = self.p
        src = [self.X[:, i, :] for i in range(KT)]
        t = self.norm_stat(src, D, 7, tmp, None)
        s, inv = self.sc[:, 64 + which:65 + which], self.sc[:, 72 + which:73 + which]
        hi = [self.AS[:, i, :] for i in range(KT)]
        lo = [self.AS[:, KT + i, :] for i in range(KT)]
        ready = []
        read = [(), ()]
        for i in range(KT):
            h = tmp[i % 2]
            a = p.stt(h, src[i], self.col(name, i), tmp[2], ALU.mult, ALU.mult, t, *read[i % 2])
            b = p.act(hi[i], h, ACT.Identity, a, self.t_gain, scale=s)
            c = p.stt(lo[i], h, s, hi[i], ALU.mult, ALU.subtract, b)
            read[i % 2] = (c,)
            ready.append(c)
        return Split(hi, lo, ready, inv, self.t_gain)

    def operand_scale(self, tiles, log2n, ready):
        p = self.p
        n = len(tiles)
        small = self.small
        for i, a in enumerate(tiles):
            t = p.act(self.junk[:, 0:S], a, ACT.Square, ready[i], total=small[:, 256 + i:257 + i])
        return self.scale_from(n, log2n, t)

    def scale_from(self, n, log2n, t):
        p, small, sc = self.p, self.small, self.sc
        t = p.rsum(small[:, 288:289], small[:, 256:256 + n], t)
        t = p.over_partitions(small[:, 289:290], small[:, 288:289], t)
        t = self.scale_of(small[:, 289:290], log2n, sc[:, 40:41], sc[:, 41:42], small[:, 290:291], t)
        return sc[:, 40:41], sc[:, 41:42], t

    def parts(self, tiles, ready, log2n=19):
        p = self.p
        s, inv, t = self.operand_scale(tiles, log2n, ready)
        hi = [self.AS[:, i, :] for i in range(KT)]
        lo = [self.AS[:, KT + i, :] for i in range(KT)]
        got = []
        for i, a in enumerate(tiles):
            b = p.act(hi[i], a, ACT.Identity, t, scale=s)
            got.append(p.stt(lo[i], a, s, hi[i], ALU.mult, ALU.subtract, b))
        return Split(hi, lo, got, inv, t)

    def parts_in_place(self, first, n, log2n, t):
        p = self.p
        s, inv, t = self.scale_from(n, log2n, t)
        hi, lo, got = [], [], []
        for i in range(first, first + n):
            v = self.T[:, i - 1, :].bitcast(F16)
            hi.append(v[:, 0:S])
            lo.append(v[:, S:2 * S])
            b = p.act(hi[-1], self.T[:, i, :], ACT.Identity, t, *got[-1:], scale=s)
            got.append(p.stt(lo[-1], self.T[:, i, :], s, hi[-1], ALU.mult, ALU.subtract, b))
        return Split(hi, lo, got, inv, t)

    def layernorm(self, row):
        p, X, PB = self.p, self.X, self.PB
        tmp = [self.WK[:, 36 + i, :] for i in range(4)]
        now = p.last["dve"]
        m = p.group(PB[0][:, :], [(self.cst("ones"), X[:, i, :]) for i in range(KT)], now, *self.fr[0])
        mu = p.act(tmp[3], PB[0][:, :], ACT.Copy, m, scale=1.0 / D)
        self.fr[0] = (mu,)
        used = [(), ()]
        for i in range(KT):
            c = p.tt(X[:, i, :], X[:, i, :], tmp[3], ALU.subtract, mu)
            t = p.act(tmp[i % 2], X[:, i, :], ACT.Square, c, *used[i % 2])
            m = p.mm(PB[1][:, :], self.cst("ones"), tmp[i % 2], i == 0, i == KT - 1, t,
                     *(self.fr[1] if i == 0 else ()), sig=True)
            used[i % 2] = (m,)
        t = self.rstd(tmp[2], PB[1][:, :], D, self.col("eps5"), 128, m)
        self.fr[1] = (t,)
        for i in range(KT):
            c = p.stt(X[:, i, :], X[:, i, :], self.col("lng", 8 * row + i), tmp[2], ALU.mult, ALU.mult, t)
            p.act(X[:, i, :], X[:, i, :], ACT.Identity, c, bias=self.col("lnb", 8 * row + i))
        self.barrier()

    def project(self, name, first, n_tiles, kt, act, banks, use, begin=None):
        p = self.p
        per = min(4, SLOT // (kt * 128))
        n = 0
        for t0 in range(first, first + n_tiles, per):
            t1 = min(t0 + per, first + n_tiles)
            i, wh, wl, sc, t_sc = self.chunk(name, t0, t1, kt, act)
            extra = begin(t0, t1, sc, t_sc) if begin else None
            t_w = self.part_tok[i]
            evac = []
            for t in range(t0, t1):
                b = banks[n % len(banks)]
                n += 1
                for k in range(kt):
                    w = wh[:, t - t0, k, :]
                    p.mm(self.PB[b][:, :], w, act.hi[k], k == 0, False, t_w, act.ready[k], *(self.fr[b] if k == 0 else ()))
                    p.mm(self.PB[b][:, :], w, act.lo[k], False, False)
                    m = p.mm(self.PB[b][:, :], wl[:, t - t0, k, :], act.hi[k], False, k == kt - 1, sig=k == kt - 1)
                self.pe_done[i] = m
                self.advance(9 if t1 - t0 == 1 else 3)
                self.fr[b] = use(t, b, (m, t_sc), sc, extra)
                evac += self.fr[b]
            self.evac[i] = evac

    def project_rows(self, name, first, n_tiles, act, banks, use):
        p = self.p
        n = 0
        for t0 in range(first, first + n_tiles, 4):
            i, wh, wl, sc, t_sc = self.chunk(name, t0, t0 + 4, KT, act)
            t_w = self.part_tok[i]
            evac = []
            for q in range(4):
                b = banks[n % len(banks)]
                n += 1
                out = self.PB[b][:, :].rearrange("p (a c) -> p a c", a=4)
                c = slice(128 * q, 128 * q + 128)
                for k in range(KT):
                    p.mm(out, act.hi[k][:, c], wh[:, :, k, :], k == 0, False, t_w, act.ready[k],
                         *(self.fr[b] if k == 0 else ()))
                    p.mm(out, act.hi[k][:, c], wl[:, :, k, :], False, False)
                    m = p.mm(out, act.lo[k][:, c], wh[:, :, k, :], False, k == KT - 1, sig=k == KT - 1)
                self.advance(3)
                self.fr[b] = use((t0 - first) // 4, q, b, (m, t_sc), sc)
                evac += self.fr[b]
            self.pe_done[i] = m
            self.evac[i] = evac

    def add_out(self, name, act, kt=KT, banks=(4, 5, 6, 7)):
        p, X = self.p, self.X

        def use(t, b, m, sc, extra):
            return (p.stt(X[:, t, :], self.PB[b][:, :], sc, X[:, t, :], ALU.mult, ALU.add, m),)

        self.project(name, 0, 8, kt, act, banks, use)

    def grow(self, *after):
        for i in range(KT):
            t = self.p.ts(self.X[:, i, :], self.X[:, i, :], ALPHA, None, ALU.mult, None, *after, eng="pool")
        return t

    def log_sigmoid(self, z, dst, t1, t2, after):
        p = self.p
        a = p.act(t1, z, ACT.Abs, *after)
        a = p.act(t1, t1, ACT.Exp, a, scale=-1.0)
        a = p.act(t1, t1, ACT.Ln, a, bias=1.0)
        b = p.ts(t2, z, 0.0, None, ALU.min, None, *after)
        return p.tt(dst, t2, t1, ALU.subtract, a, b)

    def rope_tables(self, inv, posf, cos, sin, tmp, after):
        p = self.p
        t = p.ts(sin, posf, inv, None, ALU.mult, None, after)
        t = p.ts(tmp, sin, 1.0 / TWO_PI, MAGIC, ALU.mult, ALU.add, t)
        t = p.ts(tmp, tmp, MAGIC, None, ALU.subtract, None, t)
        for c in (C1, C2, C3):
            t = p.stt(sin, tmp, -c, sin, ALU.mult, ALU.add, t)
        t = p.ts(sin, sin, PI_IN, -PI_IN, ALU.min, ALU.max, t)
        a = p.act(cos, sin, ACT.Abs, t)
        a = p.act(cos, cos, ACT.Sin, a, scale=-1.0, bias=self.col("halfpi"))
        return p.act(sin, sin, ACT.Sin, a)

    def given(self):
        return self.parts([self.X[:, i, :] for i in range(KT)], [None] * KT)

    def even0(self):
        p, X, H, WK, PB = self.p, self.X, self.H, self.WK, self.PB
        rq = [WK[:, i, :] for i in range(0, 4)]
        rk = [WK[:, i, :] for i in range(4, 8)]
        rv = [WK[:, i, :] for i in range(8, 12)]
        rg = [WK[:, i, :] for i in range(12, 16)]
        cq = [WK[:, i, :] for i in range(16, 19)]
        kro = WK[:, 19, :]
        ckv = [WK[:, i, :] for i in range(20, 22)]
        tmp = [WK[:, i, :] for i in range(22, 30)]
        c64, s64, c96, s96 = (WK[:, i, :] for i in range(30, 34))
        hs = [H[:, i, :] for i in range(KT)]

        posi = tmp[4].bitcast(I32)
        tp = p.dma("sp", posi, self.ins["posb"], self.sem("dpos"), 16)
        act = self.normed("mix_even", 0, tmp[0:3])
        t = p.cp(tmp[5], posi, tp)
        self.rope_tables(self.col("inv64"), tmp[5], c64, s64, tmp[6], t)
        t_rope = self.rope_tables(self.col("inv96"), tmp[5], c96, s96, tmp[6], p.last["dve"])

        roped = {}

        def rope_tile(dst, raw_tile):
            def use(i, b, m, sc, extra):
                j = i % 4
                raw = raw_tile[i % 2]
                c = p.act(raw, PB[b][:, :], ACT.Identity, m, *roped.get(i % 2, ()), scale=sc)
                rb = 6 + i % 2
                r = p.mm(PB[rb][:, :], self.cst("rot64"), raw, True, True, c, *self.fr[rb], sig=True)
                a = p.tt(dst[j], raw, c64, ALU.mult, c, t_rope)
                s = p.tt(tmp[4], PB[rb][:, :], s64, ALU.mult, r)
                self.fr[rb] = (s,)
                roped[i % 2] = (a, r)
                p.tt(dst[j], dst[j], tmp[4], ALU.add, a, s)
                return (c,)
            return use

        self.project("w_in_even", 0, 4, KT, act, (0, 1, 2, 3), rope_tile(rq, tmp[6:8]))
        self.project("w_in_even", 4, 4, KT, act, (0, 1, 2, 3), rope_tile(rk, tmp[6:8]))
        self.project_rows("w_in_even", 8, 4, act, (0, 1, 2, 3),
                          lambda n, q, b, m, sc: (p.act(rv[q], PB[b][:, :], ACT.Identity, m, scale=sc),))
        self.project("w_in_even", 12, 4, KT, act, (0, 1, 2, 3),
                     lambda i, b, m, sc, x: (p.act(rg[i - 12], PB[b][:, :], ACT.Silu, m, scale=sc),))
        self.project("w_in_even", 16, 6, KT, act, (0, 1, 2, 3),
                     lambda i, b, m, sc, x: (p.act(WK[:, i, :], PB[b][:, :], ACT.Identity, m, scale=sc),))
        t_c = p.last["act"]

        tq = self.rmsnorm(cq, [self.col("q_norm", i) for i in range(3)], cq, 384, 4, tmp[0:3], t_c)
        tkv = self.rmsnorm(ckv, [self.col("kv_norm", i) for i in range(2)], ckv, 256, 5, tmp[0:3], tq[-1])
        self.barrier()

        wide = self.AS[:, :, :].rearrange("p a b -> p (a b)").bitcast(F32)
        wq = wide[:, 0:2304]
        twq = self.side("w_uq", wq)
        self.retention(rq, rk, rv, rg, [tmp[i] for i in range(8)] + [WK[:, i, :] for i in range(34, 42)])
        self.barrier()
        self.mla(cq, ckv, kro, c96, s96, wq.rearrange("p (h c e) -> p h c e", h=8, c=3), twq)
        self.barrier()
        self.add_out("w_out_even", self.parts(hs, [None] * KT))
        self.barrier()

    def retention(self, rq, rk, rv, rg, w):
        p, H, PB, sm = self.p, self.H, self.PB, self.small
        y, u, lg, e = (sm[:, 16 * i:16 * i + 16] for i in range(4))
        th = self.col("th_f", n=16)
        t = p.act(y, th, ACT.Exp, scale=-0.6931471805599453)
        t = p.ts(u, y, -1.0, 1.0, ALU.mult, ALU.add, t)
        a = p.act(lg, u, ACT.Ln, t)
        t = p.ts(e, u, -1.0, None, ALU.add, None, t)
        t = p.tt(e, e, y, ALU.add, t)
        t2 = p.recip(y, u, t)
        t = p.tt(e, e, y, ALU.mult, t2)
        t_lg = p.tt(lg, lg, e, ALU.subtract, t, a)
        R = w[0][:, :]
        flat = self.WK[:, 22:24, :].rearrange("p a b -> p (a b)")[:, 0:896]
        flatn = self.WK[:, 24:26, :].rearrange("p a b -> p (a b)")[:, 0:896]
        ri = self.WK[:, 26:28, :].rearrange("p a b -> p (a b)")[:, 0:896].bitcast(I32)
        t = p.put("pool", lambda e_: e_.iota(ri, [[1, 896]], base=-384, channel_multiplier=-1), ())
        t = p.cp(flat, ri, t)
        t = p.ts(flatn, flat, -1.0, 0.0, ALU.mult, ALU.max, t)
        t_r = p.ts(flat, flat, 0.0, None, ALU.max, None, t)
        dtab = [self.WK[:, 26:28, :].rearrange("p a b -> p (a b)")[:, 0:896],
                self.WK[:, 28:30, :].rearrange("p a b -> p (a b)")[:, 0:896]]
        st = [w[i] for i in range(8, 12)]
        sq, r, nrm = w[12], w[13], w[14]
        read = [(), ()]
        st_read = [()] * 4
        tail = ()
        for h in range(8):
            d = dtab[h % 2]
            t = p.ts(d, flat, lg[:, h:h + 1], None, ALU.mult, None, t_lg, t_r, *read[h % 2])
            t = p.stt(d, flatn, lg[:, 8 + h:9 + h], d, ALU.mult, ALU.add, t)
            t_d = p.act(d, d, ACT.Exp, t)
            r0 = 64 * (h % 2)
            ob = 4 + (h // 2) % 2
            for j in range(4):
                b = j
                m = p.mm(PB[b][:, :], rk[h // 2][r0:r0 + 64, 128 * j:128 * j + 128], rq[h // 2][r0:r0 + 64, :],
                         True, True, *self.fr[b], sig=True)
                t = p.stt(st[j], PB[b][:, :], 0.125, d[:, 384 - 128 * j:896 - 128 * j], ALU.mult, ALU.mult,
                          m, t_d, *st_read[j])
                self.fr[b] = (t,)
                m = p.mm(PB[ob][r0:r0 + 64, :], rv[j][:, 64 * h:64 * h + 64], st[j], j == 0, j == 3, t,
                         *(self.fr[ob] if j == 0 else ()), sig=True)
                st_read[j] = (m,)
            read[h % 2] = (t,)
            if h % 2 == 1:
                i = h // 2
                t = p.act(sq, PB[ob][:, :], ACT.Square, m, *tail)
                m2 = p.mm(PB[6][:, :], self.cst("bd64"), sq, True, True, t, *self.fr[6], sig=True)
                t = self.rstd(r, PB[6][:, :], 64, self.col("eps6"), 128, m2)
                self.fr[6] = (t,)
                t = p.stt(nrm, PB[ob][:, :], self.col("ret_norm", i), r, ALU.mult, ALU.mult, t)
                self.fr[ob] = (t,)
                t = p.tt(H[:, 4 + i, :], nrm, rg[i], ALU.mult, t)
                tail = (t,)

    def mla(self, cq, ckv, kro, c96, s96, wq, tw):
        p, H, WK, PB, sm = self.p, self.H, self.WK, self.PB, self.small
        wkv = WK[:, 34:38, :]
        twk = self.side("w_ukv", self.flat(34, 38, 2048))
        vaug = WK[:, 0:8, :].rearrange("p a b -> p (a b)").rearrange("p (k h e) -> p k h e", k=4, h=8)
        qT = [WK[:, 8, :], WK[:, 9, :]]
        kT = [WK[:, 10, :], WK[:, 11, :]]
        pT = [WK[:, i, :] for i in range(12, 16)]
        sq, rs, qn, tr, raw, rc = (WK[:, i, :] for i in range(22, 28))
        mcol = [sm[:, 64:68], sm[:, 68:72]]
        t_one = [p.memset(kT[i][96:97, :], 1.0) for i in range(2)][-1]
        t_v1 = p.memset(vaug, 1.0)
        for k in range(4):
            b = k % 2
            m = p.group(PB[b][:, :], [(ckv[c][:, 128 * k:128 * k + 128], wkv[:, 2 + c, :]) for c in range(2)],
                        twk, *self.fr[b])
            v = PB[b][:, :].rearrange("p (h e) -> p h e", h=8)
            t = p.act(vaug[:, k, 0:8:2, 0:64], v[:, 0:8:2, :], ACT.Copy, m, t_v1)
            t = p.act(vaug[:, k, 1:8:2, 64:128], v[:, 1:8:2, :], ACT.Copy, m, t_v1)
            self.fr[b] = (t,)
        t_v = t
        scale = 96.0 ** -0.5
        used_q = [(), ()]
        used_k = [(), ()]
        pt_read = [()] * 4
        side = [()]

        def normed(src, sq_in_ready, gain, dst, free):
            t = p.act(sq[0:96, :], src, ACT.Square, *sq_in_ready, *side[0])
            m = p.mm(PB[7][0:96, :], self.cst("ones", 96, 0, 96), sq[0:96, :], True, True, t, *self.fr[7], sig=True)
            t = self.rstd(rs[0:96, :], PB[7][0:96, :], 96, self.col("eps6", 0, 0, 96), 96, m)
            n = p.stt(qn[0:96, :], src, gain, rs[0:96, :], ALU.mult, ALU.mult, t)
            m = p.mm(PB[7][0:96, :], self.cst("rot96", 96, 0, 96), qn[0:96, :], True, True, n, sig=True)
            a = p.tt(dst[0:96, :], qn[0:96, :], c96[0:96, :], ALU.mult, n, *free)
            s = p.tt(tr[64:96, :], PB[7][64:96, :], s96[64:96, :], ALU.mult, m)
            self.fr[7] = (s,)
            side[0] = (m, s)
            return n, p.tt(dst[64:96, :], dst[64:96, :], tr[64:96, :], ALU.add, a, s)

        def make(h):
            m = p.group(PB[6][0:96, :], [(wq[:, h, c, :], cq[c]) for c in range(3)], tw, *self.fr[6])
            n, tq = normed(PB[6][0:96, :], (m,), self.col("qhn", 0, 0, 96), qT[h % 2], used_q[h % 2])
            self.fr[6] = (n,)
            m = p.group(PB[6][0:64, :], [(wkv[:, c, 64 * h:64 * h + 64], ckv[c]) for c in range(2)], twk,
                        *self.fr[6])
            t = p.act(raw[0:64, :], PB[6][0:64, :], ACT.Copy, m)
            self.fr[6] = (t,)
            t = p.act(raw[64:96, :], kro[0:32, :], ACT.Copy, t)
            n, tk = normed(raw[0:96, :], (t,), self.col("khn", 0, 0, 96), kT[h % 2], (*used_k[h % 2], t_one))
            return tq, tk

        ready = make(0)
        for h in range(8):
            tq, tk = ready
            q, k = qT[h % 2], kT[h % 2]
            mc = mcol[h % 2]
            for i in range(4):
                b = i % 2
                m = p.mm(PB[b][:, :], q[0:96, 128 * i:128 * i + 128], k[0:96, :], True, True, tq, tk, *self.fr[b],
                         sig=True)
                t = p.rmax(mc[:, i:i + 1], PB[b][:, :], m)
                self.fr[b] = (t,)
            if h < 7:
                ready = make(h + 1)
            for i in range(4):
                m = p.mm(PB[4][96:97, 128 * i:128 * i + 128], mc[:, i:i + 1], self.cst("nident"), i == 0, i == 3, t,
                         *(self.fr[4] if i == 0 else ()), sig=i == 3, loose=True)
            t_m = p.act(q[96:97, :], PB[4][96:97, :], ACT.Copy, m)
            self.fr[4] = (t_m,)
            for i in range(4):
                b = 2 + i % 2
                m = p.mm(PB[b][:, :], k[0:97, 128 * i:128 * i + 128], q[0:97, :], True, True, t_m, *self.fr[b],
                         sig=True)
                t = p.act(pT[i], PB[b][:, :], ACT.Exp, m, *pt_read[i], scale=scale)
                self.fr[b] = (t,)
                used_q[h % 2] = used_k[h % 2] = (m,)
                m = p.mm(PB[5][:, :], vaug[:, i, h, :], pT[i], i == 0, i == 3, t, t_v,
                         *(self.fr[5] if i == 0 else ()), sig=True)
                pt_read[i] = (m,)
            o, s = (slice(0, 64), slice(64, 128)) if h % 2 == 0 else (slice(64, 128), slice(0, 64))
            t = p.recip(rc[o, :], PB[5][s, :], m)
            t = p.tt(H[o, h // 2, :], PB[5][o, :], rc[o, :], ALU.mult, t)
            self.fr[5] = (t,)

    def ffn(self, layer):
        p, WK, PB = self.p, self.WK, self.PB
        act = self.normed(f"ffn{layer}", 2 * layer + 1, [WK[:, 36 + i, :] for i in range(3)])
        hid = [WK[:, 1 + i, :] for i in range(FF)]
        cv = [WK[:, 24 + i, :] for i in range(3)]
        tap = [self.small[:, 6 * i:6 * i + 6].rearrange("p (j t) -> p j t", j=3) for i in range(2)]
        done, sums = [], []
        gate = {}

        def begin(t0, t1, sc, t_sc):
            i, w = t0 // 2, tap[(t0 // 4) % 2]
            c = COL[f"cw{layer}"][0]
            src = self.cols[:, c:c + 3 * FF].rearrange("p (j t) -> p j t", j=3)[:, :, i:i + 2]
            return w, p.ts(w, src, sc, None, ALU.mult, None, t_sc, *self.evac.get(self.at - 3, ()))

        def use(t, b, m, sc, extra):
            i = t // 2
            ps = PB[b]
            if t % 2 == 0:
                c = cv[i % 3]
                w = [extra[0][:, j, i % 2:i % 2 + 1] for j in range(3)]
                a = p.act(c, ps[:, :], ACT.Identity, m, extra[1], *(done[i - 3:i - 2] if i >= 3 else ()), scale=w[1],
                          bias=self.col(f"cb{layer}", i))
                a = p.stt(c[:, 1:S], ps[:, 0:S - 1], w[0], c[:, 1:S], ALU.mult, ALU.add, a)
                a = p.stt(c[:, 0:S - 1], ps[:, 1:S], w[2], c[:, 0:S - 1], ALU.mult, ALU.add, a)
                gate[i] = p.act(c, c, ACT.Silu, a)
                return (a,)
            d = p.stt(hid[i], ps[:, :], sc, cv[i % 3], ALU.mult, ALU.mult, m, gate[i])
            done.append(d)
            sums.append(p.act(self.junk[:, 0:S], hid[i], ACT.Square, d, total=self.small[:, 256 + i:257 + i]))
            return (d,)

        self.project(f"w_up{layer}", 0, 2 * FF, KT, act, (0, 1, 2, 3), use, begin)
        self.add_out(f"w_down{layer}", self.parts_in_place(1, FF, 20, sums[-1]), FF)
        self.barrier()

    def odd0(self):
        p, X, H, WK, PB, sm = self.p, self.X, self.H, self.WK, self.PB, self.small
        hs = [H[:, i, :] for i in range(KT)]
        act = self.normed("mix_odd", 2, [WK[:, 36 + i, :] for i in range(3)])
        gq = [WK[:, i, :] for i in range(0, 4)]
        gk = [WK[:, i, :] for i in range(4, 8)]
        gv = WK[:, 8:16, :].rearrange("p (q a) b -> p q (a b)", q=4)
        gr = [WK[:, i, :] for i in range(16, 24)]
        ga = WK[:, 24, :]
        sc = 128.0 ** -0.5
        qsc = [self.sc[:, 42:43]]

        def begin(t0, t1, sc_, t_sc):
            return p.ts(qsc[0], sc_, sc, None, ALU.mult, None, t_sc)

        self.project("w_in_odd", 0, 4, KT, act, (0, 1, 2, 3),
                     lambda i, b, m, s_, x: (p.act(gq[i], PB[b][:, :], ACT.Identity, m, x, scale=qsc[0]),), begin)
        self.project("w_in_odd", 4, 4, KT, act, (0, 1, 2, 3),
                     lambda i, b, m, s_, x: (p.act(gk[i - 4], PB[b][:, :], ACT.Identity, m, scale=s_),))
        self.project_rows("w_in_odd", 8, 8, act, (0, 1, 2, 3),
                          lambda n, q, b, m, s_: (p.act(gv[:, q, 512 * n:512 * n + 512], PB[b][:, :], ACT.Identity, m,
                                                        scale=s_),))
        self.project("w_in_odd", 16, 8, KT, act, (0, 1, 2, 3),
                     lambda i, b, m, s_, x: (p.act(gr[i - 16], PB[b][:, :], ACT.Silu, m, scale=s_),))
        self.project("w_in_odd", 24, 1, KT, act, (0,),
                     lambda i, b, m, s_, x: (p.act(ga, PB[b][:, :], ACT.Identity, m, scale=s_),))
        self.barrier()
        wide = self.AS[:, :, :].rearrange("p a b -> p (a b)").bitcast(F32)[0:32, 0:1024]
        tw = self.side("w_gate", wide)
        wg = wide.rearrange("p (d n) -> p d n", d=2)

        T = [WK[:, i, :] for i in range(25, 42)]
        at = T[0:2]
        chunk = T[2:4]
        for d in range(2):
            p.memset(at[d], 0.0)
            t = p.memset(chunk[d], 1.0)
            edge = 0 if d == 0 else 63
            t_c = p.memset(chunk[d][:, edge:S:64], 0.0, t)
        ax, bb = T[4], T[5]
        qc, kc, kd, qb = T[6], T[7], T[8], T[9:11]
        kdn = T[11:13]
        sst = [[T[13 + d][:, 256 * i:256 * i + 256] for i in range(2)] for d in range(2)]
        sq, rr = T[15], T[16]
        dec = [sm[:, 8 * d:8 * d + 8] for d in range(2)]
        mask = [self.cst("mf").bitcast(U32), self.cst("mb").bitcast(U32)]
        v3 = lambda a: a.rearrange("p (c t) -> p c t", t=64)
        tail = ()
        at_read = [(), ()]
        kdn_read = [(), ()]
        qb_read = [(), ()]
        s_read = [(), ()]
        kc_read = ()
        kd_read = ()
        for h in range(4):
            heads = []
            for d in range(2):
                m = p.mm(PB[0][:, :], wg[:, d, 128 * h:128 * h + 128], ga[0:32, :], True, True, tw, *self.fr[0],
                         sig=True)
                bias = self.col("gb_f" if d == 0 else "gb_b", h)
                z = p.ts(bb, PB[0][:, :], bias, None, ALU.add, None, m)
                self.fr[0] = (z,)
                t = self.log_sigmoid(bb, bb, ax, qc, (z, *kc_read))
                if d == 0:
                    t = p.scan(ax, chunk[0], bb, 0.0, ALU.mult, ALU.add, t, t_c)
                else:
                    t = p.scan(ax[:, ::-1], chunk[1][:, ::-1], bb[:, ::-1], 0.0, ALU.mult, ALU.add, t, t_c)
                b3 = v3(ax)
                mid, last = (32, 63) if d == 0 else (31, 0)
                t_b = t
                t = p.tt(v3(bb), b3, b3[:, :, mid:mid + 1].to_broadcast([128, 8, 64]), ALU.subtract, t_b)
                a = p.act(qc, bb, ACT.Exp, t, scale=1.0 / 16)
                a2 = p.act(kc, bb, ACT.Exp, t, scale=-1.0 / 16, *())
                t_q = p.tt(qc, qc, gq[h], ALU.mult, a)
                t_k = p.tt(kc, kc, gk[h], ALU.mult, a2)
                a = p.act(qb[d], ax, ACT.Exp, t_b, *qb_read[d], scale=1.0 / 16)
                t_qb = p.tt(qb[d], qb[d], gq[h], ALU.mult, a)
                t = p.tt(v3(bb), b3[:, :, last:last + 1].to_broadcast([128, 8, 64]), b3, ALU.subtract, a2)
                a = p.act(kd, bb, ACT.Exp, t, *kd_read, scale=1.0 / 16)
                t_kd = p.tt(kd, kd, gk[h], ALU.mult, a)
                t_dec = p.act(dec[d], b3[:, :, last:last + 1].rearrange("p c o -> p (c o)"), ACT.Exp, t_b, *s_read[d],
                              scale=1.0 / 16)
                for q in range(4):
                    c = slice(128 * q, 128 * q + 128)
                    m = p.mm(PB[1][:, c], kc[:, c], qc[:, c], True, True, t_q, t_k, *(self.fr[1] if q == 0 else ()),
                             sig=q == 3)
                kc_read = (m,)
                t_at = p.cpred(at[d].rearrange("p (q j) -> p q j", q=4),
                               mask[d].unsqueeze(1).to_broadcast([128, 4, 128]),
                               PB[1][:, :].rearrange("p (q j) -> p q j", q=4), m, *at_read[d])
                self.fr[1] = (t_at,)
                for q in range(4):
                    c = slice(128 * q, 128 * q + 128)
                    m = p.tr(PB[2][:, c], kd[:, c], self.cst("ident"), t_kd, *(self.fr[2] if q == 0 else ()),
                             sig=q == 3)
                kd_read = (m,)
                t_kn = p.act(kdn[d], PB[2][:, :], ACT.Copy, m, *kdn_read[d])
                self.fr[2] = (t_kn,)
                heads.append((t_qb, t_dec, t_at, t_kn))
            first = [True, True]

            def out(e, cols, w, r, *after, sig=False):
                m = p.mm(PB[3 + e][:, cols], w, r, first[e], False, *after, *(self.fr[3 + e] if first[e] else ()),
                         sig=sig, loose=True)
                first[e] = False
                return m

            for d in range(2):
                for q in range(4):
                    for e in range(2):
                        c = slice(128 * q, 128 * q + 128)
                        m = out(e, c, gv[:, q, 256 * h + 128 * e:256 * h + 128 * e + 128], at[d][:, c], heads[d][2],
                                sig=True)
                at_read[d] = (m,)
            t_s = [None, None]
            m_in = [None, None]
            for n in range(8):
                for d in range(2):
                    t_qb, t_dec, t_at, t_kn = heads[d]
                    c = n if d == 0 else 7 - n
                    cc = slice(64 * c, 64 * c + 64)
                    prev, new = sst[d][(n + 1) % 2], sst[d][n % 2]
                    if n > 0:
                        for e in range(2):
                            m_in[d] = out(e, cc, prev[:, 128 * e:128 * e + 128], qb[d][:, cc], t_s[d], t_qb, sig=True)
                    if n < 7:
                        r0 = 64 * (c % 2)
                        q = c // 2
                        b = 5 + d
                        m = p.mm(PB[b][:, 0:256], kdn[d][r0:r0 + 64, 128 * q:128 * q + 128],
                                 gv[r0:r0 + 64, q, 256 * h:256 * h + 256], True, True, t_kn, *self.fr[b], sig=True)
                        kdn_read[d] = (m,)
                        if n == 0:
                            t_s[d] = p.cp(new, PB[b][:, 0:256], m, *qb_read[d])
                        else:
                            t_s[d] = p.stt(new, prev, dec[d][:, c:c + 1], PB[b][:, 0:256], ALU.mult, ALU.add, m, t_dec,
                                           t_s[d])
                            s_read[d] = (t_s[d],)
                        self.fr[b] = (t_s[d],)
            qb_read = [(m_in[0],), (m_in[1],)]
            last = m_in[1]
            for e in range(2):
                t = p.act(sq, PB[3 + e][:, :], ACT.Square, last, *tail)
                m2 = p.mm(PB[7][:, :], self.cst("ones"), sq, e == 0, e == 1, t, *(self.fr[7] if e == 0 else ()),
                          sig=True)
                tail = (m2,)
            t = self.rstd(rr, PB[7][:, :], 256, self.col("eps6"), 128, m2)
            self.fr[7] = (t,)
            for e in range(2):
                i = 2 * h + e
                x = p.stt(H[:, i, :], PB[3 + e][:, :], self.col("gla_norm", i), rr, ALU.mult, ALU.mult, t)
                self.fr[3 + e] = (x,)
                p.tt(H[:, i, :], H[:, i, :], gr[i], ALU.mult, x)
        self.barrier()
        self.add_out("w_out_odd", self.parts(hs, [None] * KT))
        self.barrier()

    def even1(self):
        p, X, H, WK, PB, sm = self.p, self.X, self.H, self.WK, self.PB, self.small
        xs = [X[:, i, :] for i in range(KT)]
        fq = [WK[:, i, :] for i in range(0, 4)]
        fk = [WK[:, i, :] for i in range(4, 8)]
        vaug = WK[:, 8:16, :].rearrange("p a b -> p (a b)").rearrange("p (k h e) -> p k h e", k=4, h=8)
        u = [WK[:, i, :] for i in range(16, 20)]
        c = WK[0:8, 20, :]
        t1, t2, one = WK[0:8, 21, :], WK[0:8, 22, :], WK[0:8, 23, :]
        t_v1 = p.memset(vaug, 1.0)
        t_one = p.memset(one, 1.0)
        wf = self.flat(33, 34, 64).rearrange("p (k e) -> p k e", k=8)
        tw = self.side("w_fox_f", self.flat(33, 34, 64))
        act = self.parts(xs, [None] * KT)
        qsc = self.sc[:, 42:43]

        def begin(t0, t1, sc, t_sc):
            return p.ts(qsc, sc, 0.125, None, ALU.mult, None, t_sc)

        self.project("w_in_even_2", 0, 4, KT, act, (0, 1, 2, 3),
                     lambda i, b, m, s_, x: (p.act(fq[i], PB[b][:, :], ACT.Identity, m, x, scale=qsc),), begin)
        self.project("w_in_even_2", 4, 4, KT, act, (0, 1, 2, 3),
                     lambda i, b, m, s_, x: (p.act(fk[i - 4], PB[b][:, :], ACT.Identity, m, scale=s_),))

        def use_v(n, k, b, m, s_):
            v = PB[b][:, :].rearrange("p (h e) -> p h e", h=8)
            t = p.act(vaug[:, k, 0:8:2, 0:64], v[:, 0:8:2, :], ACT.Identity, m, t_v1, scale=s_)
            return (p.act(vaug[:, k, 1:8:2, 64:128], v[:, 1:8:2, :], ACT.Identity, m, t_v1, scale=s_),)

        self.project_rows("w_in_even_2", 8, 4, act, (0, 1, 2, 3), use_v)
        self.project("w_in_even_2", 12, 4, KT, act, (0, 1, 2, 3),
                     lambda i, b, m, s_, x: (p.act(u[i - 12], PB[b][:, :], ACT.Identity, m, scale=s_),))
        m = p.group(PB[4][0:8, :], [(wf[:, k, :], xs[k]) for k in range(KT)], tw, *self.fr[4])
        t = p.ts(c, PB[4][0:8, :], self.col("fox_fb", 0, 0, 8), None, ALU.add, None, m)
        self.fr[4] = (t,)
        t = self.log_sigmoid(c, c, t1, t2, (t,))
        t = p.scan(t1, one, c, 0.0, ALU.mult, ALU.add, t, t_one)
        cum = t1
        self.barrier()
        self.fox(fq, fk, vaug, cum)
        self.barrier()
        self.s5(u)
        self.barrier()
        self.grow()
        weights = self.moe_weights(0)
        self.add_out("w_out_even_2", self.parts([H[:, i, :] for i in range(KT)], [None] * KT))
        self.barrier()
        self.layernorm(0)
        return weights

    def fox(self, fq, fk, vaug, cum):
        p, H, WK, PB, sm = self.p, self.H, self.WK, self.PB, self.small
        qT = [WK[:, 24, :], WK[:, 25, :]]
        kT = [WK[:, 26, :], WK[:, 27, :]]
        pT = [WK[:, i, :] for i in range(28, 32)]
        rc = WK[:, 32, :]
        fsel = self.flat(33, 35, 1024, 8)
        t_fs = self.side("foxsel", fsel)
        mcol = [sm[:, 64:68], sm[:, 68:72]]
        for i in range(2):
            p.memset(qT[i][64:96, :], 0.0)
            p.memset(kT[i][64:96, :], 0.0)
            p.memset(qT[i][96:97, :], 1.0)
            t_one = p.memset(kT[i][64:65, :], 1.0)
        used = [(), ()]
        pt_read = [()] * 4

        def make(h):
            r0 = 64 * (h % 2)
            j = h % 2
            cb = 6 + j
            a = p.act(qT[j][0:64, :], fq[h // 2][r0:r0 + 64, :], ACT.Copy, *used[j])
            b = p.cp(kT[j][0:64, :], fk[h // 2][r0:r0 + 64, :], *used[j])
            m = p.mm(PB[cb][:, :], fsel[:, 128 * h:128 * h + 128], cum, True, False, t_fs, *self.fr[cb], sig=True,
                     loose=True)
            a = p.act(qT[j][64:65, :], PB[cb][64:65, :], ACT.Copy, m, t_one)
            b = p.cp(kT[j][96:97, :], PB[cb][96:97, :], m)
            return a, b

        ready = make(0)
        for h in range(8):
            tq, tk = ready
            j = h % 2
            cb = 6 + j
            q, k = qT[j], kT[j]
            mc = mcol[j]
            for i in range(4):
                b = i % 2
                n = 128 * i + 128
                p.mm(PB[b][:, 0:n], q[0:97, 128 * i:n], k[0:97, 0:n], True, False, tq, tk, *self.fr[b], loose=True)
                m = p.mm(PB[b][:, 128 * i:n], self.cst("ident"), self.cst("maskn"), False, True, sig=True, loose=True)
                t = p.rmax(mc[:, i:i + 1], PB[b][:, 0:n], m)
                self.fr[b] = (t,)
            for i in range(4):
                m = p.mm(PB[cb][64:65, 128 * i:128 * i + 128], mc[:, i:i + 1], self.cst("nident"), False, i == 3, t, tk,
                         sig=i == 3, loose=True)
            t_m = p.act(q[64:65, :], PB[cb][64:65, :], ACT.Copy, m)
            self.fr[cb] = (t_m, tk)
            if h < 7:
                ready = make(h + 1)
            for i in range(4):
                b = 2 + i % 2
                lo = 128 * i
                p.mm(PB[b][:, lo:S], k[0:97, lo:lo + 128], q[0:97, lo:S], True, False, t_m, *self.fr[b], loose=True)
                m = p.mm(PB[b][:, lo:lo + 128], self.cst("ident"), self.cst("maskt"), False, True, sig=True, loose=True)
                t = p.act(pT[i][:, lo:S], PB[b][:, lo:S], ACT.Exp, m, *pt_read[i])
                self.fr[b] = (t,)
                used[j] = (m,)
                m = p.mm(PB[5][:, lo:S], vaug[:, i, h, :], pT[i][:, lo:S], i == 0, i == 3, t,
                         *(self.fr[5] if i == 0 else ()), sig=True, loose=True)
                pt_read[i] = (m,)
            o, s = (slice(0, 64), slice(64, 128)) if h % 2 == 0 else (slice(64, 128), slice(0, 64))
            t = p.recip(rc[o, :], PB[5][s, :], m)
            t = p.tt(H[o, h // 2, :], PB[5][o, :], rc[o, :], ALU.mult, t)
            self.fr[5] = (t,)

    def s5(self, u):
        p, H, WK, PB, sm = self.p, self.H, self.WK, self.PB, self.small
        br, bi = (self.flat(13 + i, 14 + i, 512).rearrange("p (s c) -> p s c", s=16) for i in range(2))
        tbr = self.side("s5_br", self.flat(13, 14, 512))
        tbi = self.side("s5_bi", self.flat(14, 15, 512))
        cre, cim = (self.flat(30 + 4 * i, 34 + 4 * i, 2048).rearrange("p (s c) -> p s c", s=16) for i in range(2))
        tcr = self.side("s5_cr", self.flat(30, 34, 2048))
        tci = self.side("s5_ci", self.flat(34, 38, 2048))
        (dt, mag, th, k, r, cs, sn, nre, nim, den, zr, zi, f, t1) = (
            sm[:, 16 * i:16 * i + 16] for i in range(14))
        are, aim = self.col("a_re", n=16), self.col("a_im", n=16)
        M, A, SB = ALU.mult, ALU.add, ALU.subtract
        t = p.act(dt, self.col("log_dt", n=16), ACT.Exp)
        t = p.tt(mag, are, dt, M, t)
        t_mag = p.act(mag, mag, ACT.Exp, t)
        t = p.tt(th, aim, dt, M)
        t = p.ts(k, th, 1.0 / TWO_PI, MAGIC, M, A)
        t = p.ts(k, k, MAGIC, None, SB, None)
        t = p.stt(r, k, -C1, th, M, A)
        t = p.stt(r, k, -C2, r, M, A)
        t = p.stt(r, k, -C3, r, M, A)
        t = p.ts(r, r, PI_IN, -PI_IN, ALU.min, ALU.max)
        p.ts(f, r, 1.0 / TWO_PI, None, M, None)
        a = p.act(cs, r, ACT.Abs, t)
        a = p.act(cs, cs, ACT.Sin, a, scale=-1.0, bias=self.col("halfpi"))
        a = p.act(sn, r, ACT.Sin, t)
        p.tt(nre, mag, cs, M, a, t_mag)
        p.ts(nre, nre, -1.0, None, A, None)
        p.tt(nim, mag, sn, M)
        p.tt(den, are, are, M)
        p.tt(t1, aim, aim, M)
        p.tt(den, den, t1, A)
        p.recip(den, den)
        p.tt(zr, nre, are, M)
        p.tt(t1, nim, aim, M)
        p.tt(zr, zr, t1, A)
        p.tt(zr, zr, den, M)
        p.tt(zi, nim, are, M)
        p.tt(t1, nre, aim, M)
        p.tt(zi, zi, t1, SB)
        t_z = p.tt(zi, zi, den, M)
        v3 = lambda a: a.rearrange("p (s c) -> p s c", s=16)
        bbr, bbi, tx, bbrT, bbiT, T = (WK[:, i, :] for i in range(0, 6))
        bz = lambda a: a.unsqueeze(2).to_broadcast([128, 16, 32])
        p.tt(v3(bbr), br, bz(zr), M, tbr, tbi, t_z)
        p.tt(v3(tx), bi, bz(zi), M)
        t_r = p.tt(bbr, bbr, tx, SB)
        p.tt(v3(bbi), bi, bz(zr), M)
        p.tt(v3(tx), br, bz(zi), M)
        t_i = p.tt(bbi, bbi, tx, A)
        for b, src, dst, t in ((0, bbr, bbrT, t_r), (1, bbi, bbiT, t_i)):
            for q in range(4):
                cc = slice(128 * q, 128 * q + 128)
                m = p.tr(PB[b][:, cc], src[:, cc], self.cst("ident"), t, *self.fr[b], sig=q == 3)
            t_bt = p.act(dst, PB[b][:, :], ACT.Copy, m)
            self.fr[b] = (t_bt,)
        ti = tx.bitcast(I32)
        t = p.put("pool", lambda e: e.iota(ti, [[1, S]], base=0, channel_multiplier=0), (t_i,))
        t_T = p.cp(T, ti, t)
        W2 = [[WK[:, 6 + 10 * i + j, :] for j in range(7)] for i in range(1)] * 2
        co, si, wr, wi, x1, x2, ph = W2[0]
        ph2 = WK[:, 21, :]
        hr = [WK[:, 22, :], WK[:, 24, :]]
        hi = [WK[:, 23, :], WK[:, 25, :]]
        ys = [WK[:, i, :] for i in range(26, 30)]
        read = [(), ()]
        for st in range(16):
            q, kk = st % 4, st // 4
            rows = slice(32 * q, 32 * q + 32)
            bk = 2 * (st % 2)
            mr = p.mm(PB[bk][:, :], bbrT[rows, 128 * kk:128 * kk + 128], u[kk][rows, :], True, True, t_bt,
                      *self.fr[bk], sig=True)
            mi = p.mm(PB[bk + 1][:, :], bbiT[rows, 128 * kk:128 * kk + 128], u[kk][rows, :], True, True,
                      *self.fr[bk + 1], sig=True)
            p.ts(ph, T, f[:, st:st + 1], None, M, None, t_T, *read[st % 2])
            p.ts(ph2, ph, MAGIC, MAGIC, A, SB)
            t = p.tt(ph, ph, ph2, SB)
            a = p.act(si, ph, ACT.Sin, t, scale=6.283184)
            p.act(co, ph, ACT.Abs, t)
            a = p.act(co, co, ACT.Sin, a, scale=-6.283184, bias=self.col("halfpi"))
            p.tt(wr, PB[bk][:, :], co, M, a, mr)
            p.tt(x1, PB[bk + 1][:, :], si, M, mi)
            p.tt(wr, wr, x1, A)
            p.tt(wi, PB[bk + 1][:, :], co, M)
            t = p.tt(x2, PB[bk][:, :], si, M)
            self.fr[bk] = self.fr[bk + 1] = (t,)
            p.tt(wi, wi, x2, SB)
            mg = mag[:, st:st + 1].to_broadcast([128, S])
            p.scan(wr, mg, wr, 0.0, M, A)
            p.scan(wi, mg, wi, 0.0, M, A)
            h_r, h_i = hr[st % 2], hi[st % 2]
            p.tt(h_r, wr, co, M, *read[st % 2])
            p.tt(x1, wi, si, M)
            t_hr = p.tt(h_r, h_r, x1, SB)
            p.tt(x1, wr, si, M)
            p.tt(x2, wi, co, M)
            t_hi = p.stt(h_i, x1, -1.0, x2, M, SB)
            b = 4 + kk % 2
            m = p.mm(PB[b][:, :], cre[:, st, :], h_r, q == 0, False, tcr, t_hr, *(self.fr[b] if q == 0 else ()))
            m = p.mm(PB[b][:, :], cim[:, st, :], h_i, False, q == 3, tci, t_hi, sig=True)
            read[st % 2] = (m,)
            if q == 3:
                t = p.stt(ys[kk], u[kk], self.col("s5_d", kk), PB[b][:, :], M, A, m)
                self.fr[b] = (t,)
        ty = [p.act(ys[i], ys[i], ACT.Gelu_apprx_tanh, t) for i in range(4)]

        act = self.parts(ys, ty, 18)

        def use(i, b, m, s_, extra):
            a = p.act(x1 if i % 2 else x2, PB[b][:, :], ACT.Sigmoid, m, p.last["dve"], scale=s_,
                      bias=self.col("b_glu", i))
            p.tt(H[:, 4 + i, :], ys[i], x1 if i % 2 else x2, M, a)
            return (a,)

        self.project("w_glu", 0, 4, 4, act, (0, 1, 2, 3), use)

    def turn_of(self, name):
        sem, n = self.named.get(name) or (self.sem(name), 0)
        self.named[name] = (sem, n + 16)
        return sem, n + 16

    def moe_weights(self, layer):
        p = self.p
        gu = [self.flat(8 * i, 8 * i + 8, 4096) for i in range(3)]
        dn = [self.flat(24 + 4 * i, 28 + 4 * i, 2048) for i in range(3)]
        t_gu, t_dn = {}, {}
        now = [p.last[k] for k in ("pe", "act", "dve", "pool")]
        for b in range(3):
            t_gu[b] = p.dma("sp", gu[b], self.ins[f"moe_up{layer}"][128 * b:128 * b + 128, :], *self.turn_of(f"u{b}"), now)
            t_dn[b] = p.dma("sp", dn[b], self.ins[f"moe_down{layer}"][128 * b:128 * b + 128, :], *self.turn_of(f"d{b}"), now)
        return gu, dn, t_gu, t_dn

    def moe(self, layer, weights=None):
        p, X, T, PB, sm = self.p, self.X, self.T, self.PB, self.small
        NE, NB = 16, 23
        nc = self.nc
        gu, dn, t_gu, t_dn = weights or self.moe_weights(layer)
        xs = [X[:, i, :] for i in range(KT)]
        M, A, SB, MX = ALU.mult, ALU.add, ALU.subtract, ALU.max
        rows_d = nc.dram_tensor(f"moe_x{layer}", (S, D), F32, kind="Internal").ap()
        out_d = nc.dram_tensor(f"moe_y{layer}", (NB * 128, D), F32, kind="Internal").ap()

        xg = [self.flat(36 + 2 * i, 38 + 2 * i, 1024) for i in range(2)]
        xT = [self.flat(40 + 2 * i, 42 + 2 * i, 1024) for i in range(2)]
        hid = [T[:, 44, 256 * i:256 * i + 256] for i in range(2)]
        sl = [T[:, 45, 256 * i:256 * i + 256] for i in range(2)]
        hT = [T[:, 46, 256 * i:256 * i + 256] for i in range(2)]
        wr = T[:, 47, 0:160].rearrange("p (k e) -> p k e", k=8)
        slot = T[:, 48, :]
        xrow = self.AS[:, :, :].rearrange("p a b -> p (a b)").bitcast(F32).rearrange("p (q d) -> p q d", q=4)
        xflat = X[:, :, :].rearrange("p a b -> p (a b)")
        onehot = xflat[:, 0:2048].bitcast(F16).rearrange("p (k s) -> p k s", k=8)
        yst = [xflat[:, 2048 + 1024 * i:3072 + 1024 * i] for i in range(2)]

        tw = self.side(f"w_route{layer}", T[:, 47, 0:160])
        for q in range(4):
            m = p.group(PB[7][:, 20 * q:20 * q + 20],
                        [(xs[k][:, 128 * q:128 * q + 128], wr[:, k, :]) for k in range(KT)], tw,
                        *(self.fr[7] if q == 0 else ()))
        t_lg = m
        t_row = []
        for q in range(4):
            got = []
            for half in range(2):
                b = 2 * (q % 2) + half
                for i in range(4):
                    m = p.tr(PB[b][:, 128 * i:128 * i + 128], xs[4 * half + i][:, 128 * q:128 * q + 128], self.cst("ident"),
                             *(self.fr[b] if i == 0 else ()), sig=i == 3)
                t = p.act(xrow[:, q, 512 * half:512 * half + 512], PB[b][:, :], ACT.Copy, m)
                self.fr[b] = (t,)
                got.append(t)
            t_row.append(p.dma("sp", rows_d[128 * q:128 * q + 128, :], xrow[:, q, :],
                               *self.turn_of(f"r{q}"), got))
        x_read = m
        off = [0, 0]

        def tile(*shape, wide=False):
            n = int(np.prod(shape))
            a = (T[:, 49, :] if wide else sm)[:, off[wide]:off[wide] + n]
            off[wide] += n
            if len(shape) == 2:
                return a.rearrange("p (a b) -> p a b", a=shape[0])
            if len(shape) == 3:
                return a.rearrange("p (a b c) -> p a b c", a=shape[0], b=shape[1])
            return a

        ni = tile(64, wide=True)
        nint = ni.bitcast(I32)
        si = sl[0].bitcast(I32)
        t = p.put("pool", lambda e: e.iota(slot.bitcast(I32), [[1, S]], base=0, channel_multiplier=0), ())
        t_slot = p.cp(slot, slot.bitcast(I32), t, eng="pool")
        t = p.put("pool", lambda e: e.iota(nint[:, 0:NE], [[1, NE]], base=0, channel_multiplier=0), ())
        t = p.put("pool", lambda e: e.iota(nint[:, 32:36], [[128, 4]], base=0, channel_multiplier=1), ())
        num, tok = ni[:, 0:NE], ni[:, 32:36]
        t = p.cp(num, nint[:, 0:NE], eng="pool")
        t = p.cp(tok, nint[:, 32:36], eng="pool")
        tok16 = tile(2, wide=True).bitcast(F16)
        t_num = p.cp(tok16, tok, eng="pool")

        lg = tile(4, 20)
        t = p.tt(lg, PB[7][:, 0:80].rearrange("p (a b) -> p a b", a=4),
                 self.col(f"mb{layer}", n=20).unsqueeze(1).to_broadcast([128, 4, 20]), A, t_lg)
        self.fr[7] = (t,)

        def wide(a, n=4):
            return a.unsqueeze(2).to_broadcast([128, 4, n])

        def softmax(src):
            mx, ex, sn = tile(4), tile(4, 4), tile(4)
            p.rmax(mx, src)
            t = p.tt(ex, src, wide(mx), SB)
            t = p.act(ex, ex, ACT.Exp, t)
            p.rsum(sn, ex, t)
            p.recip(sn, sn)
            p.tt(ex, ex, wide(sn), M)
            return ex

        def top(prob):
            mx, eq, free = tile(4), tile(4, 4), tile(4)
            p.rmax(mx, prob)
            p.tt(eq, prob, wide(mx), ALU.is_equal)
            p.memset(free, 1.0, eng="dve")
            for j in range(4):
                e = eq[:, :, j]
                p.tt(e, e, free, M)
                p.tt(free, free, e, SB)
            return mx, eq

        gp = softmax(lg[:, :, 0:4])
        gv, goh = top(gp)
        pick, el = tile(4, 4), tile(4, 4)
        for g in range(4):
            dst = el if g == 0 else pick
            p.tt(dst, lg[:, :, 4 + 4 * g:8 + 4 * g], wide(goh[:, :, g]), M)
            if g:
                p.tt(el, el, pick, A)
        ep = softmax(el)
        v1, oh1 = top(ep)
        rest = tile(4, 4)
        p.stt(rest, oh1, -2.0, ep, M, A)
        v2, oh2 = top(rest)
        one = [tile(4, 4, 4, wide=True) for _ in range(2)]
        both = tile(4, 16, wide=True)
        for a, oh in zip(one, (oh1, oh2)):
            for g in range(4):
                t = p.tt(a[:, :, g, :], oh, wide(goh[:, :, g]), M)
        pairs = [a.rearrange("p q g e -> p q (g e)") for a in one]
        t = p.tt(both, pairs[0], pairs[1], A, t)
        r3 = lambda a: a.rearrange("p (q e) -> p q e", q=4)
        flat = both.rearrange("p q e -> p (q e)")
        upto, all_ = PB[6][:, 0:64], PB[6][:, 64:80]
        p.mm(upto, self.cst("causal"), flat, True, False, t, *self.fr[6], loose=True)
        for q in range(3):
            for r in range(q + 1, 4):
                p.mm(upto[:, 16 * r:16 * r + 16], self.cst("ones"), both[:, q, :], False, q == 2, loose=True)
        for q in range(4):
            m = p.mm(all_, self.cst("ones"), both[:, q, :], q == 0, q == 3, loose=True, sig=q == 3)
        den = tile(4)
        p.tt(den, v1, v2, A)
        p.recip(den, den)
        p.tt(den, den, gv, M)
        p.tt(v1, v1, den, M)
        t_v = p.tt(v2, v2, den, M)
        more, end, far, one16 = (tile(16, wide=True) for _ in range(4))
        p.memset(one16, 1.0, eng="dve")
        p.ts(end, all_, -1.0, 0.0, A, MX, m)
        p.cp(far.bitcast(I32), end)
        p.ts(end.bitcast(I32), far.bitcast(I32), 7, None, ALU.logical_shift_right, None)
        p.cp(more, end.bitcast(I32))
        p.scan(end, one16, more, 0.0, M, A)
        p.tt(far, end, more, SB)
        p.tt(far, far, num, SB, t_num)
        p.ts(far, far, float(NE - 1), 128.0, A, M)
        p.ts(one16, num, 128.0, -1.0, M, A)
        at, over = tile(4, 16, wide=True), tile(4, 16, wide=True)
        q16 = lambda a: a.unsqueeze(1).to_broadcast([128, 4, 16])
        p.ts(over, r3(upto), 128.5, None, ALU.is_gt, None)
        p.tt(over, over, q16(far), M)
        t = p.tt(at, r3(upto), q16(one16), A)
        self.fr[6] = (t,)
        p.tt(at, at, over, A)
        pos, rel = tile(2, 4, wide=True), tile(8, wide=True)
        for a, ps in zip(pairs, (pos[:, 0, :], pos[:, 1, :])):
            p.tt(a, a, at, M)
            p.rsum(ps, a)
        pos = pos.rearrange("p k q -> p (k q)")
        pos_i, w_i, x_i = (sm[:, o:o + n].bitcast(U32) for o, n in ((256, 8), (264, NB - NE), (288, NB)))
        t_pos = p.cp(pos_i, pos)
        w_f = tile(NB - NE, wide=True)
        cmp_ = T[:, 47, 192:192 + 16 * (NB - NE)].rearrange("p (b e) -> p b e", b=NB - NE)
        for b in range(NB - NE):
            p.ts(cmp_[:, b, :], end, float(b), None, ALU.is_le, None)
        p.rsum(w_f, cmp_)
        p.ts(w_f, w_f, 15.0, 128.0, ALU.min, M)
        p.ts(w_f, w_f, tok[:, 0:1], None, A, None)
        t_w = p.cp(w_i, w_f)

        one_read, t_ids, t_one = [x_read], {}, {}

        def match(r, k0, k1):
            for k in range(k0, k1):
                if k == 0:
                    p.ts(rel, pos, float(512 * r), None, SB, None)
                t_one[r] = p.ts(onehot[:, k, :], slot, rel[:, k:k + 1], None, ALU.is_equal, None, t_slot, *one_read)

        def ids(r):
            n = min(4, NB - 4 * r)
            for b in range(4 * r, 4 * r + n):
                c = 128 * (b - 4 * r)
                for k in range(8):
                    m = p.mm(PB[7][:, b:b + 1], onehot[:, k, c:c + 128], tok16[:, k % 4:k % 4 + 1], k == 0, k == 7,
                             t_one[r], t_num, *self.fr[7], loose=True, sig=k == 7)
            one_read[0] = m
            t_ids[r] = p.cp(x_i[:, 4 * r:4 * r + n], PB[7][:, 4 * r:4 * r + n], m)

        t_x, gu_read, dn_read, xg_read, y_done = {}, {}, {}, {}, {}

        def load(b, to, table, name, read):
            if b < NE:
                return p.dma("sp", to[b % 3], self.ins[table][128 * b:128 * b + 128, :], *self.turn_of(f"{name}{b % 3}"),
                             [read[b - 3]])
            return p.gather(to[b % 3], self.ins[table], w_i[:, b - NE:b - NE + 1], *self.turn_of(f"more_{name}{b % 3}"),
                            t_w, read[b - 3])

        def load_gu(b):
            if b < NB:
                t_gu[b] = load(b, gu, f"moe_up{layer}", "u", gu_read)

        def load_dn(b):
            if b < NB:
                t_dn[b] = load(b, dn, f"moe_down{layer}", "d", dn_read)

        def load_x(b):
            if b < NB:
                t_x[b] = p.gather(xg[b % 2], rows_d, x_i[:, b:b + 1], *self.turn_of(f"x{b % 2}"), t_ids[b // 4],
                                  xg_read.get(b - 2), *t_row)

        xT_tok, xT_read, hid_tok, h_read, hT_tok, hT_read, sl_tok = {}, {}, {}, {}, {}, {}, {}

        def turn(b):
            got = []
            for half in range(2):
                for i in range(4):
                    m = p.tr(PB[half][:, 128 * i:128 * i + 128], xg[b % 2][:, 512 * half + 128 * i:512 * half + 128 * i + 128],
                             self.cst("ident"), t_x[b], *(self.fr[half] if i == 0 else ()), sig=i == 3)
                dst = xT[b % 2][:, 512 * half:512 * half + 512]
                t = (p.act(dst, PB[0][:, :], ACT.Copy, m, xT_read.get(b - 2)) if half == 0
                     else p.cp(dst, PB[1][:, :], m, xT_read.get(b - 2)))
                self.fr[half] = (t,)
                got.append(t)
            xg_read[b] = m
            xT_tok[b] = tuple(got)

        def up(b):
            bank = 2 + b % 2
            m = p.group(PB[bank][:, :], [(xT[b % 2][:, 128 * k:128 * k + 128], gu[b % 3][:, 512 * k:512 * k + 512])
                                         for k in range(KT)], t_gu[b], xT_tok[b], *self.fr[bank])
            gu_read[b] = xT_read[b] = m
            s = p.act(sl[b % 2], PB[bank][:, 0:256], ACT.Silu, m, hid_tok.get(b - 2))
            hid_tok[b] = p.tt(hid[b % 2], sl[b % 2], PB[bank][:, 256:512], M, s, m, h_read.get(b - 2))
            self.fr[bank] = (hid_tok[b],)

        def turn_hid(b):
            for c in range(2):
                m = p.tr(PB[4][:, 128 * c:128 * c + 128], hid[b % 2][:, 128 * c:128 * c + 128], self.cst("ident"),
                         hid_tok[b], *(self.fr[4] if c == 0 else ()), sig=c == 1)
            h_read[b] = m
            hT_tok[b] = p.cp(hT[b % 2], PB[4][:, 0:256], m, hT_read.get(b - 2))
            self.fr[4] = (hT_tok[b],)

        def down(b):
            got = []
            for half in range(2):
                bank = 5 + half
                m = p.group(PB[bank][:, :], [(hT[b % 2][:, 128 * c:128 * c + 128],
                                              dn[b % 3][:, 1024 * c + 512 * half:1024 * c + 512 * half + 512])
                                             for c in range(2)], hT_tok[b], t_dn[b], *self.fr[bank])
                dst = yst[b % 2][:, 512 * half:512 * half + 512]
                t = (p.act(dst, PB[bank][:, :], ACT.Copy, m, x_read, y_done.get(b - 2)) if half == 0
                     else p.cp(dst, PB[bank][:, :], m, x_read, y_done.get(b - 2)))
                self.fr[bank] = (t,)
                got.append(t)
            hT_read[b] = dn_read[b] = m
            y_done[b] = p.dma("sp", out_d[128 * b:128 * b + 128, :], yst[b % 2], *self.turn_of(f"y{b % 2}"), got)

        match(0, 0, 8)
        ids(0)
        for b in range(2):
            load_x(b)
        turn(0)
        for b in range(NB):
            up(b)
            load_gu(b + 3)
            r = (b + 2) // 4
            if b % 4 == 2 and 4 * r < NB:
                ids(r)
            if b + 1 < NB:
                turn(b + 1)
            if b + 2 < NB:
                load_x(b + 2)
            if b > 0:
                down(b - 1)
                load_dn(b + 2)
            turn_hid(b)
            if b < 2:
                match(1, 4 * b, 4 * b + 4)
            elif 4 * (r + 1) < NB:
                k = 2 * ((b + 2) % 4)
                match(r + 1, k, k + 2)
        down(NB - 1)

        y = [self.flat(2 * i, 2 * i + 2, 1024) for i in range(8)]
        z = [self.flat(16 + 2 * q, 18 + 2 * q, 1024) for q in range(4)]
        st = [sm[:, 312 + i:313 + i] for i in range(4)]
        junk = self.flat(24, 26, 1024)
        row = 2 * layer + 1
        lastm = p.last["pe"]
        first, sums = {}, []
        for q in range(4):
            for k in range(2):
                n = 2 * q + k
                first[n] = p.gather(y[n], out_d, pos_i[:, 4 * k + q:4 * k + q + 1], *self.turn_of(f"g{n}"), t_pos, lastm,
                                    y_done[NB - 1], y_done[NB - 2])
        mu, var, rs, neg = (sm[:, o:o + 4] for o in (80, 84, 88, 92))
        def weigh(q):
            a, c = y[2 * q], y[2 * q + 1]
            t = p.act(a, a, ACT.Identity, first[2 * q], t_v, scale=v1[:, q:q + 1])
            t = p.stt(a, c, v2[:, q:q + 1], a, M, A, first[2 * q + 1], t)
            sums.append(p.stt(z[q], xrow[:, q, :], ALPHA, a, M, A, t))

        weigh(0)
        for q in range(4):
            if q < 3:
                weigh(q + 1)
            t = p.act(junk, z[q], ACT.Identity, sums[q], total=mu[:, q:q + 1])
            t = p.act(neg[:, q:q + 1], mu[:, q:q + 1], ACT.Copy, t, scale=-1.0 / D)
            t = p.act(junk, z[q], ACT.Square, t, bias=neg[:, q:q + 1], total=var[:, q:q + 1])
            t = self.rstd(rs[:, q:q + 1], var[:, q:q + 1], D, self.col("eps5"), 128, t)
            t = p.ts(z[q], z[q], neg[:, q:q + 1], rs[:, q:q + 1], A, M, t)
            for i in range(KT):
                m = p.tr(PB[i][:, 128 * q:128 * q + 128], z[q][:, 128 * i:128 * i + 128], self.cst("ident"), t,
                         *(self.fr[i] if q == 0 else ()), sig=q == 3)
                if q == 3:
                    self.fr[i] = (m,)
        s, inv = self.sc[:, 68 + row:69 + row], self.sc[:, 76 + row:77 + row]
        hi = [self.AS[:, i, :] for i in range(KT)]
        lo = [self.AS[:, KT + i, :] for i in range(KT)]
        got = []
        for i in range(KT):
            t = p.act(X[:, i, :], PB[i][:, :], ACT.Identity, *self.fr[i], y_done[NB - 1], y_done[NB - 2],
                      scale=self.col("lng", 8 * row + i), bias=self.col("lnb", 8 * row + i))
            self.fr[i] = (t,)
            if row < 3:
                a = p.act(hi[i], X[:, i, :], ACT.Identity, t, self.t_gain, scale=s)
                got.append(p.stt(lo[i], X[:, i, :], s, hi[i], M, SB, a))
        self.barrier()
        return Split(hi, lo, got, inv, self.t_gain) if row < 3 else None

    def odd1(self, act):
        p, X, H, WK, PB, sm = self.p, self.X, self.H, self.WK, self.PB, self.small
        xs = [X[:, i, :] for i in range(KT)]
        M, A, SB, MX = ALU.mult, ALU.add, ALU.subtract, ALU.max
        qk = [WK[:, i, :] for i in range(16)]
        vv = WK[:, 16:24, :].rearrange("p (q a) b -> p q (a b)", q=4)
        og = [WK[:, i, :] for i in range(24, 32)]

        wg = self.flat(41, 42, 512).rearrange("p (k e) -> p k e", k=8)
        tw = self.side("w_mgate", self.flat(41, 42, 512))
        tap = [sm[:, 32 + 16 * i:48 + 16 * i].rearrange("p (j t) -> p j t", j=4) for i in range(2)]

        def begin(t0, t1, sc, t_sc):
            w = tap[(t0 // 4) % 2]
            c = COL["mcw"][0]
            src = self.cols[:, c:c + 64].rearrange("p (j t) -> p j t", j=4)[:, :, t0:t0 + 4]
            return w, p.ts(w, src, sc, None, M, None, t_sc, *self.evac.get(self.at - 3, ()))

        def conv(i, b, m, sc, extra):
            ps, c = PB[b], qk[i]
            w = [extra[0][:, j, i % 4:i % 4 + 1] for j in range(4)]
            a = p.act(c, ps[:, :], ACT.Identity, m, extra[1], scale=w[3], bias=self.col("mcb", i))
            for j in range(3):
                s = 3 - j
                a = p.stt(c[:, s:S], ps[:, 0:S - s], w[j], c[:, s:S], M, A, a)
            p.act(c, c, ACT.Silu, a)
            return (a,)

        self.project("w_in_odd_2", 0, 16, KT, act, (0, 1, 2, 3), conv, begin)
        self.project_rows("w_in_odd_2", 16, 8, act, (0, 1, 2, 3),
                          lambda n, q, b, m, s_: (p.act(vv[:, q, 512 * n:512 * n + 512], PB[b][:, :], ACT.Identity, m,
                                                        scale=s_),))
        self.project("w_in_odd_2", 24, 8, KT, act, (0, 1, 2, 3),
                     lambda i, b, m, s_, x: (p.act(og[i - 24], PB[b][:, :], ACT.Sigmoid, m, scale=s_),))
        m = p.group(PB[4][0:64, :], [(wg[:, k, :], xs[k]) for k in range(KT)], tw, *self.fr[4])
        ig, z, t1, t2, F_, a_, mx, en = (WK[0:8, 32 + i, :] for i in range(8))
        one = WK[0:8, 40, :]
        t_one = p.memset(one, 1.0)
        t_i = p.ts(ig, PB[4][0:8, :], self.col("ib", 0, 0, 8), None, A, None, m)
        t = p.act(z, PB[4][32:40, :], ACT.Identity, m, bias=self.col("fb", 0, 32, 40))
        self.fr[4] = (t, t_i)
        t = self.log_sigmoid(z, z, t1, t2, (t,))
        p.scan(F_, one, z, 0.0, M, A, t, t_one)
        p.tt(a_, ig, F_, SB)
        t_mx = p.scan(mx, a_, a_, 0.0, MX, MX)
        t = p.tt(t1, F_, mx, A)
        t_en = p.act(en, t1, ACT.Exp, t, scale=-1.0)
        ac = sm[:, 0:32].rearrange("p (j h) -> p j h", j=4)
        for j in range(4):
            m = p.tr(PB[5][:, 8 * j:8 * j + 8], a_[:, 128 * j:128 * j + 128], self.cst("ident", 8, 0, 8), t_mx,
                     *self.fr[5], sig=j == 3)
        t_ac = p.cp(ac, PB[5][:, 0:32].rearrange("p (j h) -> p j h", j=4), m)
        self.barrier()
        sel = self.flat(40, 42, 1024, 8)
        t_sel = self.side("sel8", sel)
        self.grow()
        dd = [WK[:, i, :] for i in (32, 33)]
        stt_ = [WK[:, i, :] for i in (34, 35, 36)]
        sc = 128.0 ** -0.5
        dread = [(), ()]
        sread = [(), (), ()]
        n = 0
        for h in range(8):
            mb = 6 + h % 2
            m_b = p.mm(PB[mb][:, :], sel[:, 128 * h:128 * h + 128], mx, True, True, t_sel, *self.fr[mb], sig=True)
            nb = 3 + h % 2
            for j in range(4):
                lo = 128 * j
                d, st = dd[n % 2], stt_[n % 3]
                t = p.ts(d[:, lo:S], PB[mb][:, lo:S], ac[:, j, h:h + 1], 0.0, SB, MX, m_b, *dread[n % 2])
                t = p.act(d[:, lo:S], d[:, lo:S], ACT.Exp, t, scale=-1.0)
                t_d = p.tt(d[:, lo:lo + 128], d[:, lo:lo + 128], self.cst("causal"), M, t, eng="pool")
                b = n % 3
                m = p.mm(PB[b][:, lo:S], qk[8 + h][:, lo:lo + 128], qk[h][:, lo:S], True, True, *self.fr[b], sig=True)
                t = p.stt(st[:, lo:S], PB[b][:, lo:S], sc, d[:, lo:S], M, M, m, t_d, *sread[n % 3])
                self.fr[b] = (t,)
                dread[n % 2] = (t,)
                m = p.mm(PB[nb][:, lo:S], vv[:, j, 128 * h:128 * h + 128], st[:, lo:S], j == 0, j == 3, t,
                         *(self.fr[nb] if j == 0 else ()), sig=True, loose=True)
                m = p.mm(PB[5][0:8, lo:S], self.cst("oh", 128, 8 * h, 8), st[:, lo:S], h == 0 and j == 0,
                         h == 7 and j == 3, sig=True, loose=True)
                sread[n % 3] = (m,)
                n += 1
            self.fr[mb] = dread[(n - 1) % 2]
            t = p.act(H[:, h, :], PB[nb][:, :], ACT.Copy, m)
            self.fr[nb] = (t,)
        den = WK[0:8, 37, :]
        t = p.act(den, PB[5][0:8, :], ACT.Abs, m)
        p.tt(den, den, en, MX, t, t_en)
        t = p.recip(den, den)
        for h in range(8):
            mb = 6 + h % 2
            m = p.mm(PB[mb][:, :], sel[:, 128 * h:128 * h + 128], den, True, True, t, *self.fr[mb], sig=True)
            x = p.tt(H[:, h, :], H[:, h, :], PB[mb][:, :], M, m)
            self.fr[mb] = (x,)
            p.tt(H[:, h, :], H[:, h, :], og[h], M, x)
        self.barrier()
        weights = self.moe_weights(1)
        self.add_out("w_out_odd_2", self.parts([H[:, i, :] for i in range(KT)], [None] * KT))
        self.barrier()
        self.layernorm(2)
        return weights

    PHASES = ("even0", "ffn0", "odd0", "ffn1", "even1", "moe0", "odd1", "moe1")

    def finish(self):
        p = self.p
        now = [p.last[k] for k in ("pe", "act", "dve", "pool") if p.last[k] is not None]
        s = self.sem("dout")
        t = p.dma("sp", self.out.rearrange("(t p) s -> p t s", p=128), self.X[:, :, :], s, 16, now)
        p.wait_all("sp", [t])
        with self.nc.Block() as block:
            @block.sync
            def _(e):
                p.run("sp", e)

            @block.tensor
            def _(e):
                p.run("pe", e)

            @block.scalar
            def _(e):
                p.run("act", e)

            @block.vector
            def _(e):
                p.run("dve", e)

            @block.gpsimd
            def _(e):
                p.run("pool", e)


def build(nc, ins, out, phases=Build.PHASES):
    b = Build(nc, ins, out)
    with b.ctx:
        b.setup(phases)
        act = weights = None
        for name in phases:
            if name in ("ffn0", "ffn1"):
                b.ffn(int(name[3]))
            elif name == "even0":
                b.even0()
            elif name == "odd0":
                b.odd0()
            elif name == "even1":
                weights = b.even1()
            elif name == "odd1":
                weights = b.odd1(act or b.given())
            else:
                act = b.moe(int(name[3]), weights)
                weights = None
        b.finish()


def tiles_of(w, order=None):
    k, n = w.shape
    nt = -(-n // 128)
    out = np.zeros((k, nt * 128), w.dtype)
    out[:, :n] = w
    out = out.reshape(k // 128, 128, nt, 128).transpose(2, 1, 0, 3)
    return np.ascontiguousarray(out if order is None else out[order])


def pair_up(a, b):
    ta, tb = tiles_of(a), tiles_of(b)
    return np.ascontiguousarray(np.stack([ta, tb], 1).reshape(-1, *ta.shape[1:]))


def rows_of(w):
    k, n = w.shape
    return np.ascontiguousarray(w.reshape(k // 128, 128, n).transpose(1, 0, 2))


def constants():
    c = np.zeros((128, NCST), np.float32)

    def at(name):
        a, w = CST[name]
        return c[:, a:a + w]

    i = np.arange(128)
    at("ident")[:] = np.eye(128)
    at("nident")[:] = -np.eye(128)
    at("ones")[:] = 1
    at("bd64")[:] = i[:, None] // 64 == i[None] // 64
    for name, lo, hi, size, half in (("rot64", 0, 128, 64, 32), ("rot96", 64, 96, 32, 16)):
        m = at(name)
        for o in range(lo, hi):
            if (o - lo) % size < half:
                m[o + half, o] = -1
            else:
                m[o - half, o] = 1
    at("maskn")[:] = np.where(i[None] > i[:, None], np.float32(-1e30), 0)
    at("maskt")[:] = np.where(i[:, None] > i[None], np.float32(-1e30), 0)
    same = i[:, None] // 64 == i[None] // 64
    at("mf")[:] = same & (i[:, None] <= i[None])
    at("mb")[:] = same & (i[:, None] > i[None])
    at("causal")[:] = i[:, None] <= i[None]
    for h in range(8):
        at("oh")[:, 8 * h + h] = 1
    return c


def selectors():
    sel = np.zeros((8, 8 * 128), np.float32)
    fox = np.zeros((8, 8 * 128), np.float32)
    for h in range(8):
        sel[h, 128 * h:128 * h + 128] = 1
        fox[h, 128 * h + 64] = 1
        fox[h, 128 * h + 96] = -1
    return sel, fox


def layout(**a):
    f32 = np.float32
    a = {k: np.asarray(v) for k, v in a.items()}
    out = {}
    out["xT"] = np.ascontiguousarray(a["x"][0].T)
    out["posb"] = np.ascontiguousarray(np.broadcast_to(a["positions"].reshape(1, S), (128, S)))
    out["csts"] = constants()
    out["sel8"], out["foxsel"] = selectors()
    cols = np.zeros((128, NCOL), f32)

    def put(name, v, i=0):
        v = np.asarray(v).reshape(-1)
        n = -(-v.size // 128)
        full = np.zeros(n * 128, f32)
        full[:v.size] = v
        c = COL[name][0] + i
        cols[:, c:c + n] = full.reshape(n, 128).T

    put("mix_even", a["mix_norm_even"])
    put("q_norm", a["mla_q_norm"])
    put("kv_norm", a["mla_kv_norm"])
    put("qhn", a["mla_q_head_norm"])
    put("khn", a["mla_k_head_norm"])
    put("ret_norm", a["ret_out_norm"])
    for name, v, n in (("th_f", a["ret_theta_fwd"][0], 8), ("th_b", a["ret_theta_bwd"][0], 8)):
        cols[:, COL[name][0]:COL[name][0] + n] = v[None]
    put("mix_odd", a["mix_norm_odd"])
    put("gb_f", a["gla_b_gate_fwd"])
    put("gb_b", a["gla_b_gate_bwd"])
    put("gla_norm", a["gla_out_norm"])
    for l in range(2):
        put(f"ffn{l}", a["ffn_norm"][l])
        put(f"cw{l}", a["ffn_conv_w"][l])
        put(f"cb{l}", a["ffn_conv_b"][l])
        c = COL[f"mb{l}"][0]
        cols[:, c:c + 4] = a["moe_b_group_2"][l][None]
        cols[:, c + 4:c + 20] = a["moe_b_expert_2"][l].reshape(1, 16)
    put("lng", a["ln_g_2"])
    put("lnb", a["ln_b_2"])
    put("fox_fb", a["fox_f_bias_2"])
    put("a_re", a["s5_a_re_2"])
    put("a_im", a["s5_a_im_2"])
    put("log_dt", np.repeat(a["s5_log_dt_2"].reshape(32), 64))
    put("s5_d", a["s5_d_2"])
    put("b_glu", a["s5_b_glu_2"])
    put("mcw", a["mlstm_conv_w_2"])
    put("mcb", a["mlstm_conv_b_2"])
    put("ib", a["mlstm_i_bias_2"])
    cols[32:40, COL["fb"][0]] = a["mlstm_f_bias_2"][0]
    inv32 = (f32(10000.0) ** (-np.arange(32, dtype=f32) / f32(32))).astype(f32)
    inv16 = (f32(10000.0) ** (-np.arange(16, dtype=f32) / f32(16))).astype(f32)
    cols[:, COL["inv64"][0]] = np.tile(inv32, 4)
    cols[64:96, COL["inv96"][0]] = np.tile(inv16, 2)
    cols[:, COL["eps6"][0]] = 1e-6
    cols[:, COL["eps5"][0]] = 1e-5
    cols[:, COL["halfpi"][0]] = np.pi / 2
    cols[:, COL["one"][0]] = 1
    out["cols"] = cols

    w = a["w_in_even"][0]
    cut = np.cumsum([0, 384, 256, 32, 512, 512, 512, 512])
    cq, ckv, kro, rq, rk, rv, rg = (w[:, cut[i]:cut[i + 1]] for i in range(7))
    out["w_in_even"] = np.concatenate([tiles_of(x) for x in (rq, rk, rv, rg, cq, kro, ckv)])
    out["w_uq"] = np.ascontiguousarray(a["mla_w_uq"][0].reshape(3, 128, 8, 96).transpose(1, 2, 0, 3)).reshape(128, -1)
    kv = a["mla_w_ukv"][0].reshape(2, 128, 8, 2, 64).transpose(1, 3, 0, 2, 4)
    out["w_ukv"] = np.ascontiguousarray(kv).reshape(128, -1)
    out["w_out_even"] = tiles_of(a["w_out_even"][0])
    out["w_in_odd"] = tiles_of(a["w_in_odd"][0])
    g = np.zeros((32, 2, 512), f32)
    g[0:16, 0] = a["gla_w_gate_fwd"][0]
    g[16:32, 1] = a["gla_w_gate_bwd"][0]
    out["w_gate"] = g.reshape(32, -1)
    out["w_out_odd"] = tiles_of(a["w_out_odd"][0])
    for l in range(2):
        up = a["ffn_w_up"][l]
        out[f"w_up{l}"] = pair_up(up[:, :2816], up[:, 2816:])
        out[f"w_down{l}"] = tiles_of(a["ffn_w_down"][l])
        wr = np.concatenate([a["moe_w_group_2"][l], a["moe_w_expert_2"][l].transpose(1, 0, 2).reshape(D, 16)], 1)
        out[f"w_route{l}"] = rows_of(wr).reshape(128, -1)
        up = np.concatenate([a["moe_w_gate_2"][l], a["moe_w_up_2"][l]], 2).reshape(16, 8, 128, 512)
        out[f"moe_up{l}"] = np.ascontiguousarray(up.transpose(0, 2, 1, 3)).reshape(16 * 128, 4096)
        down = a["moe_w_down_2"][l].reshape(16, 2, 128, 1024)
        out[f"moe_down{l}"] = np.ascontiguousarray(down.transpose(0, 2, 1, 3)).reshape(16 * 128, 2048)
    w = a["even_w_in_2"][0]
    out["w_in_even_2"] = tiles_of(np.concatenate([w[:, 0:1536], w[:, 1544:2056]], 1))
    out["w_fox_f"] = rows_of(w[:, 1536:1544]).reshape(128, -1)
    for name, v in (("s5_br", a["s5_b_re_2"][0]), ("s5_bi", a["s5_b_im_2"][0])):
        m = np.zeros((16, 2, 64, 2, 16), f32)
        for g2 in range(2):
            m[:, g2, :, g2, :] = v[g2::2]
        out[name] = np.ascontiguousarray(m.transpose(1, 2, 0, 3, 4)).reshape(128, -1)
    for name, v in (("s5_cr", a["s5_c_re_2"][0]), ("s5_ci", a["s5_c_im_2"][0])):
        m = np.zeros((2, 64, 16, 128), f32)
        for st in range(16):
            for g2 in range(2):
                c = 32 * (st % 4) + 16 * g2
                m[g2, :, st, c:c + 16] = v[2 * st + g2].T
        out[name] = m.reshape(128, -1)
    out["w_glu"] = tiles_of(a["s5_w_glu_2"][0])
    out["w_out_even_2"] = tiles_of(a["even_w_out_2"][0])
    w = a["odd_w_in_2"][0]
    out["w_in_odd_2"] = tiles_of(w[:, :4096])
    g = np.zeros((D, 64), f32)
    g[:, 0:8] = w[:, 4096:4104]
    g[:, 32:40] = w[:, 4104:4112]
    out["w_mgate"] = rows_of(g).reshape(128, -1)
    out["w_out_odd_2"] = tiles_of(a["odd_w_out_2"][0])
    return out


def kernel(**inputs):
    import concourse.bacc as bacc
    from concourse.bass_utils import run_bass_kernel_spmd

    arrays = layout(**inputs)
    nc = bacc.Bacc("TRN2", target_bir_lowering=False, num_devices=1)
    ins = {k: nc.dram_tensor(f"in_{k}", v.shape, mybir.dt.from_np(v.dtype), kind="ExternalInput").ap()
           for k, v in arrays.items()}
    out = nc.dram_tensor("outT", (D, S), F32, kind="ExternalOutput").ap()
    build(nc, ins, out)
    r = run_bass_kernel_spmd(nc, [{f"in_{k}": v for k, v in arrays.items()}], core_ids=[0])
    return np.ascontiguousarray(r.results[0]["outT"].T)[None]
```

```python
from contextlib import ExitStack

import numpy as np

import concourse.bass as bass
from concourse import mybir

ALU = mybir.AluOpType
ACT = mybir.ActivationFunctionType
F32 = mybir.dt.float32
F16 = mybir.dt.float16
U32 = mybir.dt.uint32
I32 = mybir.dt.int32
AX = mybir.AxisListType.X

S = 512
D = 1024
KT = 8
FF = 22
SLOT = 4096
NT = 50
MAGIC = 12582912.0
TWO_PI = 6.283185307179586
C1 = 6.28125
C2 = 0.0019350051879882812
C3 = TWO_PI - C1 - C2
PI_IN = 3.1415925
ALPHA = 4.0 ** 0.25

COL = {}
_n = 0
for _name, _w in (
    ("mix_even", 8), ("q_norm", 3), ("kv_norm", 2), ("qhn", 1), ("khn", 1), ("ret_norm", 4),
    ("th_f", 8), ("th_b", 8), ("mix_odd", 8), ("gb_f", 4), ("gb_b", 4), ("gla_norm", 8),
    ("ffn0", 8), ("ffn1", 8), ("cw0", 66), ("cw1", 66), ("cb0", 22), ("cb1", 22),
    ("lng", 32), ("lnb", 32), ("fox_fb", 1), ("a_re", 16), ("a_im", 16), ("log_dt", 16),
    ("s5_d", 4), ("b_glu", 4), ("mcw", 64), ("mcb", 16), ("ib", 1), ("fb", 1),
    ("mb0", 20), ("mb1", 20), ("inv64", 1), ("inv96", 1), ("eps6", 1), ("eps5", 1),
    ("halfpi", 1), ("one", 1),
):
    COL[_name] = (_n, _w)
    _n += _w
NCOL = _n

CST = {}
_n = 0
for _name, _w in (
    ("ident", 128), ("nident", 128), ("ones", 128), ("bd64", 128), ("rot64", 128), ("rot96", 128),
    ("maskn", 128), ("maskt", 128), ("mf", 128), ("mb", 128), ("causal", 128),
    ("oh", 64),
):
    CST[_name] = (_n, _w)
    _n += _w
NCST = _n


WEIGHTS = (
    ("w_in_even", 22, 8), ("w_out_even", 8, 8), ("w_up0", 44, 8), ("w_down0", 8, 22),
    ("w_odd_qk", 9, 8), ("w_odd_v", 16, 8), ("w_out_odd", 8, 8), ("w_up1", 44, 8), ("w_down1", 8, 22),
    ("w_in_even_2", 16, 8), ("w_glu", 4, 4), ("w_out_even_2", 8, 8), ("w_in_odd_2", 32, 8), ("w_out_odd_2", 8, 8),
)
PER = {name: min(4, SLOT // (kt * 128)) for name, _, kt in WEIGHTS}
PER["w_odd_qk"] = 3
PHASE_OF = {
    "even0": ("w_in_even", "w_out_even"), "ffn0": ("w_up0", "w_down0"), "odd0": ("w_odd_qk", "w_odd_v", "w_out_odd"),
    "ffn1": ("w_up1", "w_down1"), "even1": ("w_in_even_2", "w_glu", "w_out_even_2"),
    "moe0": (), "odd1": ("w_in_odd_2", "w_out_odd_2"), "moe1": (),
}


class Split:

    def __init__(self, hi, lo, ready, inv, t_inv):
        self.hi, self.lo, self.ready, self.inv, self.t_inv = hi, lo, ready, inv, t_inv


class Queues:

    def __init__(self, sem):
        self.make = sem
        self.q = {k: [] for k in ("pe", "act", "dve", "pool", "sp")}
        self.waited = {k: {} for k in self.q}
        self.last = {k: None for k in self.q}
        self.stage = 0
        self.fresh()

    def fresh(self):
        self.sem = {k: self.make(f"s_{k}{self.stage}") for k in ("pe", "act", "dve", "pool")}
        self.count = {k: 0 for k in self.sem}
        self.stage += 1

    def put(self, k, fn, after, sig=True):
        waits = []
        if k in ("act", "dve", "pool"):
            after = [*after, self.last[k]]
        for t in after:
            if t is None:
                continue
            if isinstance(t[0], tuple):
                self.put_waits(k, t, waits)
                continue
            s, v = t
            if self.waited[k].get(id(s), 0) < v:
                self.waited[k][id(s)] = v
                waits = [w for w in waits if w[0] is not s] + [t]
        tok = None
        if sig:
            self.count[k] += 1
            tok = (self.sem[k], self.count[k])
            self.last[k] = tok
        self.q[k].append((waits, fn, (tok[0], 1) if sig else None))
        return tok

    def put_waits(self, k, pair, waits):
        for s, v in pair:
            if self.waited[k].get(id(s), 0) < v:
                self.waited[k][id(s)] = v
                waits.append((s, v))

    def dma(self, k, out, in_, sem, value, after=()):
        waits = []
        for t in after:
            if t is not None and self.waited[k].get(id(t[0]), 0) < t[1]:
                self.waited[k][id(t[0])] = t[1]
                waits.append(t)
        self.q[k].append((waits, lambda e: e.dma_start(out, in_), (sem, 16)))
        return (sem, value)

    def gather(self, out, table, rows, sem, value, *after):
        waits = []
        for t in after:
            if t is not None and self.waited["pool"].get(id(t[0]), 0) < t[1]:
                self.waited["pool"][id(t[0])] = t[1]
                waits.append(t)
        at = bass.IndirectOffsetOnAxis(rows, 0)
        self.q["pool"].append((waits, lambda e: e.indirect_dma_start(out, None, table, at), (sem, 16)))
        return (sem, value)

    def wait_all(self, k, after):
        self.q[k].append((list(after), None, None))

    def run(self, k, e):
        for waits, fn, inc in self.q[k]:
            for s, v in waits:
                e.wait_ge(s, v)
            if fn is not None:
                ins = fn(e)
                if inc is not None:
                    ins.then_inc(*inc)

    def tt(self, out, a, b, op, *after, eng="dve"):
        return self.put(eng, lambda e: e.tensor_tensor(out, a, b, op), after)

    def ts(self, out, a, s1, s2, op0, op1, *after, eng="dve"):
        if s2 is None:
            return self.put(eng, lambda e: e.tensor_scalar(out, a, s1, None, op0), after)
        return self.put(eng, lambda e: e.tensor_scalar(out, a, s1, s2, op0, op1), after)

    def stt(self, out, a, s, b, op0, op1, *after):
        return self.put("dve", lambda e: e.scalar_tensor_tensor(out, a, s, b, op0, op1), after)

    def scan(self, out, d0, d1, init, op0, op1, *after):
        return self.put("dve", lambda e: e.tensor_tensor_scan(out, d0, d1, init, op0, op1), after)

    def rmax(self, out, a, *after):
        return self.put("dve", lambda e: e.tensor_reduce(out, a, AX, ALU.max), after)

    def rsum(self, out, a, *after):
        return self.put("dve", lambda e: e.tensor_reduce(out, a, AX, ALU.add), after)

    def recip(self, out, a, *after):
        return self.put("dve", lambda e: e.reciprocal(out, a), after)

    def cp(self, out, a, *after, eng="dve"):
        return self.put(eng, lambda e: e.tensor_copy(out, a), after)

    def cpred(self, out, mask, a, *after):
        return self.put("dve", lambda e: e.copy_predicated(out, mask, a), after)

    def memset(self, out, v, *after, eng="pool"):
        return self.put(eng, lambda e: e.memset(out, v), after)

    def act(self, out, a, f, *after, scale=1.0, bias=0.0, total=None):
        if total is not None:
            return self.put("act", lambda e: e.activation(out, a, f, bias=bias, scale=scale, accum_out=total), after)
        return self.put("act", lambda e: e.activation(out, a, f, bias=bias, scale=scale), after)

    def over_partitions(self, out, a, *after):
        return self.put("pool", lambda e: e.partition_all_reduce(out, a, 128, bass.bass_isa.ReduceOp.add), after)

    def mm(self, out, lhsT, rhs, start, stop, *after, sig=False, loose=False):
        return self.put("pe", lambda e: e.matmul(out, lhsT, rhs, start=start, stop=stop,
                                                 skip_group_check=loose), after, sig)

    def tr(self, out, a, ident, *after, sig=False):
        return self.put("pe", lambda e: e.transpose(out, a, ident), after, sig)

    def group(self, out, pairs, *after, start=True, stop=True, loose=False, each=None):
        t = None
        for i, (w, r) in enumerate(pairs):
            last = i == len(pairs) - 1
            own = after if i == 0 else ()
            if each is not None:
                own = (*own, each[i])
            t = self.mm(out, w, r, start and i == 0, stop and last, *own, sig=last, loose=loose)
        return t


class Build:
    def __init__(self, nc, ins, out):
        self.nc, self.ins, self.out = nc, ins, out
        self.ctx = ExitStack()

    def sb(self, name, shape, dt=F32):
        return self.ctx.enter_context(self.nc.sbuf_tensor(name, shape, dt))

    def sem(self, name):
        return self.ctx.enter_context(self.nc.semaphore(name))

    def col(self, name, i=0, p0=0, p1=128, n=1):
        a = COL[name][0] + i
        return self.cols[p0:p1, a:a + n]

    def cst(self, name, p=128, a=0, n=None):
        c, w = CST[name]
        n = w if n is None else n
        return self.csts[0:p, c + a:c + a + n]

    def setup(self, phases):
        nc = self.nc
        self.X = self.sb("X", [128, KT, S])
        self.T = self.sb("T", [128, NT, S])
        self.WK = self.T
        self.H = self.T[:, 42:50, :]
        self.AS = self.sb("AS", [128, 2 * KT, S], F16)
        self.raw = self.sb("raw", [128, 2, SLOT])
        self.WS = self.sb("WS", [128, 2, 2, SLOT], F16)
        self.junk = self.sb("junk", [128, 1024], F16)
        self.cols = self.sb("cols", [128, NCOL])
        self.csts = self.sb("csts", [128, NCST])
        self.small = self.sb("small", [128, 320])
        self.sc = self.sb("sc", [128, 96])
        self.PB = [self.ctx.enter_context(nc.psum_tensor(f"PB{i}", [128, S], F32)) for i in range(8)]
        self.p = Queues(self.sem)
        self.raw_sem = [self.sem(f"dw{i}") for i in range(2)]
        self.n_side = 0
        self.named = {}
        self.x_tok = [()] * KT
        self.have = None
        s0 = [self.sem(f"di{i}") for i in range(3)]
        p = self.p
        self.t_cols = p.dma("sp", self.cols[:, :], self.ins["cols"], s0[2], 16)
        self.t_x = p.dma("sp", self.X[:, :, :], self.ins["xT"].rearrange("(t p) s -> p t s", p=128), s0[0], 16)
        self.t_csts = p.dma("sp", self.csts[:, :], self.ins["csts"], s0[1], 16)
        self.fr = [()] * 8
        for k in ("pe", "act", "dve", "pool"):
            p.wait_all(k, [self.t_csts, self.t_cols, self.t_x])
        self.chunks = []
        names = [n for ph in phases for n in PHASE_OF[ph]]
        for name, nt, kt in WEIGHTS:
            per = PER[name]
            if name in names:
                self.chunks += [(name, t, min(t + per, nt), kt) for t in range(0, nt, per)]
        self.raw_tok, self.raw_free, self.pe_done, self.evac, self.inv_tok = {}, {}, {}, {}, {}
        self.part_tok = {}
        self.at = 0
        self.todo = []
        self.prepared = -1
        self.load_chunk(0)
        self.load_chunk(1)
        for i, cs in enumerate((("mix_even", 0, 8), ("ffn0", 0, 8), ("mix_odd", 0, 8), ("ffn1", 0, 8))):
            t = p.act(self.junk[:, 0:8], self.col(cs[0], n=8), ACT.Square, total=self.sc[:, 48 + i:49 + i])
        for i in range(3):
            for name in ("lng", "lnb"):
                c = 56 + 2 * i + (name == "lnb")
                t = p.act(self.junk[:, 0:8], self.col(name, 8 * i, n=8), ACT.Square, total=self.sc[:, c:c + 1])
        v = self.sc[:, 56:62].rearrange("p (a b) -> p a b", b=2)
        t = p.tt(self.sc[:, 52:55], v[:, :, 0], v[:, :, 1], ALU.add, t)
        t = p.over_partitions(self.sc[:, 56:63], self.sc[:, 48:55], t)
        self.t_gain = self.scale_of(self.sc[:, 56:63], 10, self.sc[:, 64:71], self.sc[:, 72:79], self.sc[:, 80:87], t)

    def scale_of(self, total, log2n, s, inv, tmp, *after):
        p = self.p
        ti, si = tmp.bitcast(I32), s.bitcast(I32)
        t = p.ts(ti, total.bitcast(I32), 23, None, ALU.logical_shift_right, None, *after)
        t = p.ts(ti, ti, -0.5, 130 + 63.5 + log2n / 2, ALU.mult, ALU.add, t)
        t = p.ts(si, ti, 23, None, ALU.logical_shift_left, None, t)
        return p.recip(inv, s, t)

    def load_chunk(self, i):
        if i >= len(self.chunks):
            return
        name, t0, t1, kt = self.chunks[i]
        out = self.raw[:, i % 2, 0:(t1 - t0) * kt * 128].rearrange("p (t n) -> p t n", t=t1 - t0)
        src = self.ins[name][t0:t1].rearrange("t p k c -> p t (k c)")
        self.raw_tok[i] = self.p.dma("sp", out, src, self.raw_sem[i % 2], 16 * (i // 2 + 1), self.raw_free.get(i - 2, ()))

    def steps(self, i):
        p = self.p
        name, t0, t1, kt = self.chunks[i]
        n = (t1 - t0) * kt * 32
        j = i % 2
        c = 16 * j
        st, ar, tot, s, inv, tmp = (self.sc[:, c + a:c + b] for a, b in ((0, 4), (4, 8), (8, 9), (9, 10), (10, 11), (11, 12)))
        raw = [self.raw[:, j, n * q:n * q + n] for q in range(4)]
        hi = [self.WS[:, j, 0, n * q:n * q + n] for q in range(4)]
        lo = [self.WS[:, j, 1, n * q:n * q + n] for q in range(4)]
        box = {}

        def square(q):
            box["t"] = p.act(self.junk[:, 0:n], raw[q], ACT.Square, self.raw_tok[i], total=st[:, q:q + 1])

        def scale():
            t = p.over_partitions(ar, st, box["t"])
            t = p.rsum(tot, ar, t)
            box["s"] = self.inv_tok[i] = self.scale_of(tot, 19, s, inv, tmp, t)

        def part(q):
            a = p.act(hi[q], raw[q], ACT.Identity, box["s"], self.pe_done.get(i - 2), scale=s)
            b = p.stt(lo[q], raw[q], s, hi[q], ALU.mult, ALU.subtract, a)
            if q == 3:
                self.raw_free[i] = (a, b)
                self.part_tok[i] = b
                self.load_chunk(i + 2)

        return [lambda q=q: square(q) for q in range(4)] + [scale] + [lambda q=q: part(q) for q in range(4)]

    def advance(self, n):
        for _ in range(n):
            if not self.todo:
                return
            self.todo.pop(0)()

    def flush(self):
        if self.prepared < self.at < len(self.chunks):
            self.todo = self.steps(self.at)
            self.prepared = self.at
        self.advance(len(self.todo))

    def chunk(self, name, t0, t1, kt, act):
        i = self.at
        assert self.chunks[i] == (name, t0, t1, kt), (self.chunks[i], name, t0, t1, kt)
        self.flush()
        c = 32 + i % 4
        sc = self.sc[:, c:c + 1]
        t_sc = self.p.tt(sc, self.sc[:, 16 * (i % 2) + 10:16 * (i % 2) + 11], act.inv, ALU.mult, self.inv_tok[i],
                         act.t_inv, *self.evac.get(i - 4, ()))
        w = [self.WS[:, i % 2, h, 0:(t1 - t0) * kt * 128].rearrange("p (t k c) -> p t k c", t=t1 - t0, k=kt)
             for h in range(2)]
        self.at += 1
        if self.at < len(self.chunks):
            self.todo = self.steps(self.at)
            self.prepared = self.at
        return i, w[0], w[1], sc, t_sc

    def side(self, name, out, *after):
        self.n_side += 1
        return self.p.dma("pool", out, self.ins[name], self.sem(f"dv{self.n_side}"), 16, after)

    def flat(self, t0, t1, n, p=128):
        return self.T[0:p, t0:t1, :].rearrange("p a b -> p (a b)")[:, 0:n]

    def settle(self):
        p = self.p
        now = [p.last[k] for k in ("pe", "act", "dve", "pool") if p.last[k] is not None]
        for k in ("act", "dve", "pool", "sp"):
            p.wait_all(k, now)

    def barrier(self):
        p = self.p
        now = [p.last[k] for k in ("pe", "act", "dve", "pool") if p.last[k] is not None]
        for k in ("pe", "act", "dve", "pool"):
            p.wait_all(k, now)
        p.fresh()
        self.fr = [()] * 8

    def rstd(self, out, bank, n, eps, rows, *after):
        p = self.p
        t = p.act(out, bank, ACT.Ln, *after, scale=1.0 / n, bias=eps)
        return p.act(out, out, ACT.Exp, t, scale=-0.5)

    def norm_stat(self, src, n, bank, tmp, ready):
        p = self.p
        used = [(), ()]
        for i, a in enumerate(src):
            sq = tmp[i % 2]
            t = p.act(sq, a, ACT.Square, ready, *used[i % 2])
            m = p.mm(self.PB[bank][:, :], self.cst("ones"), sq, i == 0, i == len(src) - 1, t,
                     *(self.fr[bank] if i == 0 else ()), sig=True)
            used[i % 2] = (m,)
        if self.prepared < self.at < len(self.chunks):
            self.todo = self.steps(self.at)
            self.prepared = self.at
            self.advance(5)
        t = self.rstd(tmp[2], self.PB[bank][:, :], n, self.col("eps6"), 128, m)
        self.fr[bank] = (t,)
        return t

    def rmsnorm(self, src, gain, dst, n, bank, tmp, ready):
        t = self.norm_stat(src, n, bank, tmp, ready)
        return [self.p.stt(d, a, g, tmp[2], ALU.mult, ALU.mult, t) for d, a, g in zip(dst, src, gain)]

    def normed(self, name, which, tmp):
        p = self.p
        src = [self.X[:, i, :] for i in range(KT)]
        if self.have == "rms":
            t = self.rstd(tmp[2], self.PB[3][:, :], D, self.col("eps6"), 128)
            self.fr[3] = (t,)
        else:
            t = self.norm_stat(src, D, 7, tmp, None)
        self.have = None
        self.flush()
        s, inv = self.sc[:, 64 + which:65 + which], self.sc[:, 72 + which:73 + which]
        hi = [self.AS[:, i, :] for i in range(KT)]
        lo = [self.AS[:, KT + i, :] for i in range(KT)]
        ready = []
        read = [(), ()]
        for i in range(KT):
            h = tmp[i % 2]
            a = p.stt(h, src[i], self.col(name, i), tmp[2], ALU.mult, ALU.mult, t, *read[i % 2])
            b = p.act(hi[i], h, ACT.Identity, a, self.t_gain, scale=s)
            c = p.stt(lo[i], h, s, hi[i], ALU.mult, ALU.subtract, b)
            read[i % 2] = (c,)
            ready.append(c)
        return Split(hi, lo, ready, inv, self.t_gain)

    def square_sum(self, i, a, *after):
        return self.p.act(self.junk[:, 0:S], a, ACT.Square, *after, total=self.small[:, 256 + i:257 + i])

    def scale_from(self, n, log2n, t):
        p, small, sc = self.p, self.small, self.sc
        t = p.rsum(small[:, 288:289], small[:, 256:256 + n], t)
        t = p.over_partitions(small[:, 289:290], small[:, 288:289], t)
        t = self.scale_of(small[:, 289:290], log2n, sc[:, 40:41], sc[:, 41:42], small[:, 290:291], t)
        return sc[:, 40:41], sc[:, 41:42], t

    def parts(self, tiles, ready=None, log2n=19, measured=None, after=None):
        p = self.p
        t = measured
        if measured is None:
            for i, a in enumerate(tiles):
                t = self.square_sum(i, a, *(ready[i:i + 1] if ready else ()))
        s, inv, t = self.scale_from(len(tiles), log2n, t)
        hi = [self.AS[:, i, :] for i in range(KT)]
        lo = [self.AS[:, KT + i, :] for i in range(KT)]
        got = []
        for i, a in enumerate(tiles):
            b = p.act(hi[i], a, ACT.Identity, t, after, scale=s)
            got.append(p.stt(lo[i], a, s, hi[i], ALU.mult, ALU.subtract, b))
        return Split(hi, lo, got, inv, t)

    def parts_in_place(self, first, n, log2n, t):
        p = self.p
        s, inv, t = self.scale_from(n, log2n, t)
        hi, lo, got = [], [], []
        for i in range(first, first + n):
            v = self.T[:, i - 3, :].bitcast(F16)
            hi.append(v[:, 0:S])
            lo.append(v[:, S:2 * S])
            b = p.act(hi[-1], self.T[:, i, :], ACT.Identity, t, *(got[-3:-2] if len(got) > 2 else ()), scale=s)
            got.append(p.stt(lo[-1], self.T[:, i, :], s, hi[-1], ALU.mult, ALU.subtract, b))
        return Split(hi, lo, got, inv, t)

    def layernorm(self, row):
        p, X, PB = self.p, self.X, self.PB
        tmp = [self.WK[:, 36 + i, :] for i in range(4)]
        mu = p.act(tmp[3], PB[3][:, :], ACT.Copy, scale=1.0 / D)
        self.fr[3] = (mu,)
        self.have = None
        used = [(), ()]
        for i in range(KT):
            c = p.tt(X[:, i, :], X[:, i, :], tmp[3], ALU.subtract, mu)
            t = p.act(tmp[i % 2], X[:, i, :], ACT.Square, c, *used[i % 2])
            m = p.mm(PB[1][:, :], self.cst("ones"), tmp[i % 2], i == 0, i == KT - 1, t,
                     *(self.fr[1] if i == 0 else ()), sig=True)
            used[i % 2] = (m,)
        t = self.rstd(tmp[2], PB[1][:, :], D, self.col("eps5"), 128, m)
        self.fr[1] = (t,)
        for i in range(KT):
            c = p.stt(X[:, i, :], X[:, i, :], self.col("lng", 8 * row + i), tmp[2], ALU.mult, ALU.mult, t)
            self.x_tok[i] = (p.act(X[:, i, :], X[:, i, :], ACT.Identity, c, bias=self.col("lnb", 8 * row + i)),)
        self.settle()

    def project(self, name, first, n_tiles, kt, act, banks, use, begin=None):
        p = self.p
        per = PER[name]
        n = 0
        for t0 in range(first, first + n_tiles, per):
            t1 = min(t0 + per, first + n_tiles)
            i, wh, wl, sc, t_sc = self.chunk(name, t0, t1, kt, act)
            extra = begin(t0, t1, sc, t_sc) if begin else None
            t_w = self.part_tok[i]
            evac = []
            for t in range(t0, t1):
                b = banks[n % len(banks)]
                n += 1
                for k in range(kt):
                    w = wh[:, t - t0, k, :]
                    p.mm(self.PB[b][:, :], w, act.hi[k], k == 0, False, t_w, act.ready[k], *(self.fr[b] if k == 0 else ()))
                    p.mm(self.PB[b][:, :], w, act.lo[k], False, False)
                    m = p.mm(self.PB[b][:, :], wl[:, t - t0, k, :], act.hi[k], False, k == kt - 1, sig=k == kt - 1)
                self.pe_done[i] = m
                self.advance(9 if t1 - t0 == 1 else 5)
                self.fr[b] = use(t, b, (m, t_sc), sc, extra)
                evac += self.fr[b]
            self.evac[i] = evac

    def project_rows(self, name, first, n_tiles, act, banks, use):
        p = self.p
        n = 0
        for t0 in range(first, first + n_tiles, 4):
            i, wh, wl, sc, t_sc = self.chunk(name, t0, t0 + 4, KT, act)
            t_w = self.part_tok[i]
            evac = []
            for q in range(4):
                b = banks[n % len(banks)]
                n += 1
                out = self.PB[b][:, :].rearrange("p (a c) -> p a c", a=4)
                c = slice(128 * q, 128 * q + 128)
                for k in range(KT):
                    p.mm(out, act.hi[k][:, c], wh[:, :, k, :], k == 0, False, t_w, act.ready[k],
                         *(self.fr[b] if k == 0 else ()))
                    p.mm(out, act.hi[k][:, c], wl[:, :, k, :], False, False)
                    m = p.mm(out, act.lo[k][:, c], wh[:, :, k, :], False, k == KT - 1, sig=k == KT - 1)
                self.advance(5)
                self.fr[b] = use((t0 - first) // 4, q, b, (m, t_sc), sc)
                evac += self.fr[b]
            self.pe_done[i] = m
            self.evac[i] = evac

    def add_out(self, name, act, kt=KT, banks=(4, 5, 6, 7), then=None):
        p, X = self.p, self.X
        sq = [self.WK[:, 36, :], self.WK[:, 37, :]]
        held, read = [], [(), ()]

        def total():
            if held:
                i, src, t_src = held.pop(0)
                m = p.mm(self.PB[3][:, :], self.cst("ones"), src, i == 0, i == KT - 1, t_src,
                         *(self.fr[3] if i == 0 else ()), sig=True)
                read[i % 2] = (m,)

        def use(t, b, m, sc, extra):
            total()
            t_x = p.stt(X[:, t, :], self.PB[b][:, :], sc, X[:, t, :], ALU.mult, ALU.add, m)
            if then == "rms":
                a = p.act(sq[t % 2], X[:, t, :], ACT.Square, t_x, *read[t % 2])
                held.append((t, sq[t % 2], a))
            elif then == "mean":
                held.append((t, X[:, t, :], t_x))
            elif then == "sum":
                self.t_sums = self.square_sum(t, X[:, t, :], t_x)
            return (t_x,)

        self.project(name, 0, 8, kt, act, banks, use)
        total()
        self.have = then

    def grow(self, i, *after):
        self.p.ts(self.X[:, i, :], self.X[:, i, :], ALPHA, None, ALU.mult, None, *after, eng="pool")

    def log_sigmoid(self, z, dst, t1, t2, after):
        p = self.p
        a = p.act(t1, z, ACT.Abs, *after)
        a = p.act(t1, t1, ACT.Exp, a, scale=-1.0)
        a = p.act(t1, t1, ACT.Ln, a, bias=1.0)
        b = p.ts(t2, z, 0.0, None, ALU.min, None, *after)
        return p.tt(dst, t2, t1, ALU.subtract, a, b)

    def rope_tables(self, inv, posf, cos, sin, tmp, after):
        p = self.p
        t = p.ts(sin, posf, inv, None, ALU.mult, None, after)
        t = p.ts(tmp, sin, 1.0 / TWO_PI, MAGIC, ALU.mult, ALU.add, t)
        t = p.ts(tmp, tmp, MAGIC, None, ALU.subtract, None, t)
        for c in (C1, C2, C3):
            t = p.stt(sin, tmp, -c, sin, ALU.mult, ALU.add, t)
        t = p.ts(sin, sin, PI_IN, -PI_IN, ALU.min, ALU.max, t)
        a = p.act(cos, sin, ACT.Abs, t)
        a = p.act(cos, cos, ACT.Sin, a, scale=-1.0, bias=self.col("halfpi"))
        return p.act(sin, sin, ACT.Sin, a)

    def given(self):
        return self.parts([self.X[:, i, :] for i in range(KT)], [None] * KT)

    def even0(self):
        p, X, H, WK, PB = self.p, self.X, self.H, self.WK, self.PB
        rq = [WK[:, i, :] for i in range(0, 4)]
        rk = [WK[:, i, :] for i in range(4, 8)]
        rv = [WK[:, i, :] for i in range(8, 12)]
        rg = [WK[:, i, :] for i in range(12, 16)]
        cq = [WK[:, i, :] for i in range(16, 19)]
        kro = WK[:, 19, :]
        ckv = [WK[:, i, :] for i in range(20, 22)]
        tmp = [WK[:, i, :] for i in range(22, 30)]
        c64, s64, c96, s96 = (WK[:, i, :] for i in range(30, 34))

        posi = tmp[4].bitcast(I32)
        tp = p.dma("sp", posi, self.ins["posb"], self.sem("dpos"), 16)
        act = self.normed("mix_even", 0, tmp[0:3])
        got = {}

        def keep(i, b, m, sc, x):
            got[i] = p.act(WK[:, 16 + i % 16, :], PB[b][:, :], ACT.Identity, m, scale=sc)
            return (got[i],)

        self.project("w_in_even", 0, 4, KT, act, (0, 1, 2, 3), keep)
        self.project_rows("w_in_even", 4, 4, act, (0, 1, 2, 3),
                          lambda n, q, b, m, sc: (p.act(rv[q], PB[b][:, :], ACT.Identity, m, scale=sc),))
        t_rv = p.last["act"]
        t = p.cp(tmp[5], posi, tp)
        self.rope_tables(self.col("inv64"), tmp[5], c64, s64, tmp[6], t)
        t_rope = self.rope_tables(self.col("inv96"), tmp[5], c96, s96, tmp[6], p.last["dve"])
        tables = self.retention_tables()
        self.project("w_in_even", 8, 4, KT, act, (0, 1, 2, 3),
                     lambda i, b, m, sc, x: (p.act(rg[i - 8], PB[b][:, :], ACT.Silu, m, scale=sc),))
        tq = self.rmsnorm(cq, [self.col("q_norm", i) for i in range(3)], cq, 384, 4, tmp[0:3], got[2])

        roped = {}

        def rope_tile(dst, raw_tile):
            def use(i, b, m, sc, extra):
                j = i % 4
                raw = raw_tile[i % 2]
                c = p.act(raw, PB[b][:, :], ACT.Identity, m, *roped.get(i % 2, ()), scale=sc)
                rb = 6 + i % 2
                r = p.mm(PB[rb][:, :], self.cst("rot64"), raw, True, True, c, *self.fr[rb], sig=True)
                a = p.tt(dst[j], raw, c64, ALU.mult, c, t_rope)
                s = p.tt(tmp[4], PB[rb][:, :], s64, ALU.mult, r)
                self.fr[rb] = (s,)
                roped[i % 2] = (a, r)
                p.tt(dst[j], dst[j], tmp[4], ALU.add, a, s)
                return (c,)
            return use

        self.project("w_in_even", 12, 4, KT, act, (0, 1, 2, 3), rope_tile(rq, tmp[6:8]))
        self.project("w_in_even", 16, 4, KT, act, (0, 1, 2, 3), rope_tile(rk, tmp[6:8]))
        t_rot = p.last["dve"]
        self.project("w_in_even", 20, 2, KT, act, (0, 1, 2, 3), keep)
        t_act = self.pe_done[self.at - 1]

        wide = self.AS[:, :, :].rearrange("p a b -> p (a b)").bitcast(F32)
        wq = wide[:, 0:2304].rearrange("p (h c e) -> p h c e", h=8, c=3)
        wk = wide[:, 2304:3328]
        wv = self.flat(30, 32, 1024)
        t_w = (p.dma("pool", wide[:, 0:2304], self.ins["w_uq"], self.sem("dmq"), 16, [t_act]),
               p.dma("pool", wk, self.ins["w_ukv"][:, 0:1024], self.sem("dmk"), 16),
               p.dma("pool", wv, self.ins["w_ukv"][:, 1024:2048], self.sem("dmv"), 16, [t_rot]))
        box = {}

        def low_rank():
            box["kv"] = self.rmsnorm(ckv, [self.col("kv_norm", i) for i in range(2)], ckv, 256, 7, tmp[4:7], got[21])

        ret_logs, ret_finish = self.retention(rq, rk, rv, tables, (t_rot, t_rv), wide[:, 3328:3840], t_act, low_rank)
        t = self.mla(cq, ckv, kro, c96, s96, wq, wk.rearrange("p (c n) -> p c n", c=2),
                     wv.rearrange("p (c n) -> p c n", c=2), t_w, got[3], tq[-1], box["kv"][-1],
                     ret_logs, lambda: ret_finish(rg))
        self.add_out("w_out_even", self.parts([H[:, i, :] for i in range(KT)], measured=t), then="rms")
        self.barrier()

    def retention_tables(self):
        p, sm = self.p, self.small
        y, u, lg, e = (sm[:, 16 * i:16 * i + 16] for i in range(4))
        th = self.col("th_f", n=16)
        t = p.act(y, th, ACT.Exp, scale=-0.6931471805599453)
        t = p.ts(u, y, -1.0, 1.0, ALU.mult, ALU.add, t)
        a = p.act(lg, u, ACT.Ln, t)
        t = p.ts(e, u, -1.0, None, ALU.add, None, t)
        t = p.tt(e, e, y, ALU.add, t)
        t2 = p.recip(y, u, t)
        t = p.tt(e, e, y, ALU.mult, t2)
        t_lg = p.tt(lg, lg, e, ALU.subtract, t, a)
        flat, flatn = self.flat(34, 36, 896), self.flat(36, 38, 896)
        ri = self.flat(38, 40, 896).bitcast(I32)
        t = p.put("pool", lambda e_: e_.iota(ri, [[1, 896]], base=-384, channel_multiplier=-1), ())
        t = p.cp(flat, ri, t)
        t = p.ts(flatn, flat, -1.0, 0.0, ALU.mult, ALU.max, t)
        t_r = p.ts(flat, flat, 0.0, None, ALU.max, None, t)
        return lg, flat, flatn, (t_lg, t_r)

    def retention(self, rq, rk, rv, tables, ready, sq, t_sq, between):
        p, H, PB = self.p, self.H, self.PB
        lg, flat, flatn, t_tab = tables
        dtab = [self.flat(38, 40, 896), self.flat(40, 42, 896)]
        st = [self.WK[:, 22 + i, :] for i in range(4)]
        read = [(), ()]
        st_read = [()] * 4
        t_d, st_tok, pair_m = {}, {}, {}
        sums, outs = {}, {}

        def table(h):
            d = dtab[h % 2]
            t = p.ts(d, flat, lg[:, h:h + 1], None, ALU.mult, None, *t_tab, *read[h % 2])
            t = p.stt(d, flatn, lg[:, 8 + h:9 + h], d, ALU.mult, ALU.add, t)
            t_d[h] = p.act(d, d, ACT.Exp, t)

        def score(h, j):
            r0 = 64 * (h % 2)
            m = p.mm(PB[j][:, :], rk[h // 2][r0:r0 + 64, 128 * j:128 * j + 128], rq[h // 2][r0:r0 + 64, :],
                     True, True, *self.fr[j], ready[0], sig=True)
            return m

        def weigh(h, j, m):
            d = dtab[h % 2]
            t = p.stt(st[j], PB[j][:, :], 0.125, d[:, 384 - 128 * j:896 - 128 * j], ALU.mult, ALU.mult,
                      m, t_d[h], *st_read[j])
            self.fr[j] = (t,)
            st_tok[h, j] = t
            read[h % 2] = (t,)

        def value(h, j):
            r0 = 64 * (h % 2)
            ob = 4 + (h // 2) % 2
            m = p.mm(PB[ob][r0:r0 + 64, :], rv[j][:, 64 * h:64 * h + 64], st[j], j == 0, j == 3, st_tok[h, j],
                     ready[1], *(self.fr[ob] if j == 0 else ()), sig=True)
            st_read[j] = (m,)
            pair_m[h // 2] = m

        def square(i):
            ob = 4 + i % 2
            t = p.act(sq, PB[ob][:, :], ACT.Square, pair_m[i], *sums.get(i - 1, ()), t_sq)
            outs[i] = p.act(H[:, 4 + i, :], PB[ob][:, :], ACT.Copy)
            self.fr[ob] = (outs[i],)
            sums[i] = (t,)

        def total(i):
            m = p.mm(PB[6][:, :], self.cst("bd64"), sq, True, True, *sums[i], *self.fr[6], sig=True)
            sums[i] = (m,)
            t = p.act(H[:, i, :], PB[6][:, :], ACT.Copy, m)
            self.fr[6] = (t,)

        table(0)
        for h in range(9):
            if h < 7:
                table(h + 1)
            for j in range(4):
                if h < 8:
                    m = score(h, j)
                if h > 0:
                    value(h - 1, j)
                if h < 8:
                    weigh(h, j, m)
            if h == 1:
                between()
            if h > 0 and h % 2 == 0:
                square(h // 2 - 1)
            if h > 2 and h % 2 == 1:
                total((h - 3) // 2)
        self.t_ret = pair_m[3]

        def logs():
            total(3)
            for i in range(4):
                p.act(H[:, i, :], H[:, i, :], ACT.Ln, scale=1.0 / 64, bias=self.col("eps6"))

        def finish(rg):
            for i in range(4):
                t = p.act(H[:, i, :], H[:, i, :], ACT.Exp, scale=-0.5)
                p.stt(H[:, 4 + i, :], H[:, 4 + i, :], self.col("ret_norm", i), H[:, i, :], ALU.mult, ALU.mult, t)
                t = p.tt(H[:, 4 + i, :], H[:, 4 + i, :], rg[i], ALU.mult)
                self.square_sum(4 + i, H[:, 4 + i, :], t)
            return t

        return logs, finish

    def mla(self, cq, ckv, kro, c96, s96, wq, wk, wv, t_w, t_kro, t_cq, t_ckv, ret_logs, ret_finish):
        p, H, WK, PB, sm = self.p, self.H, self.WK, self.PB, self.small
        vaug = WK[:, 0:8, :].rearrange("p a b -> p (a b)").rearrange("p (k h e) -> p k h e", k=4, h=8)
        qT = [WK[:, 34 + i, :] for i in range(8)]
        kT = [WK[:, i, :] for i in (8, 9, 10, 11, 22, 23, 24, 25)]
        sq = [WK[:, 26, :], WK[:, 27, :]]
        sel = self.flat(28, 30, 1024, 8)
        rsum = [WK[0:8, 20, :], WK[0:8, 21, :]]
        pT = [WK[:, i, :] for i in range(12, 16)]
        tr, rc = [WK[:, 16, :], WK[:, 17, :]], [WK[:, 18, :], WK[:, 19, :]]
        mcol = [sm[:, 64:68], sm[:, 68:72]]
        free = self.t_ret
        t_sel = self.side("sel8", sel, free, p.last["act"], p.last["dve"])
        t_v1 = p.memset(vaug, 1.0, free)
        for h in range(8):
            p.cp(kT[h][64:96, :], kro[0:32, :], t_kro, eng="pool")
            t_one = p.memset(kT[h][96:97, :], 1.0)
        t_k = t_one
        s_tok = [(), ()]
        n = [0]
        first = [True, True]
        held = []

        def squares(which, src, rows, lhsT, m):
            s = sq[n[0] % 2]
            t = p.act(s[0:rows, :], src, ACT.Square, m, *s_tok[n[0] % 2])
            held.append((which, s[0:rows, :], lhsT, t, n[0] % 2))
            n[0] += 1
            return t

        def add_up(last=False):
            while held:
                which, s, lhsT, t, i = held.pop(0)
                m = p.mm(PB[4 + which][0:8, :], lhsT, s, first[which], last and which == 0 or last and not held, t,
                         *(self.fr[4 + which] if first[which] else ()), sig=True, loose=True)
                first[which] = False
                s_tok[i] = (m,)
                self.t_sum = m

        squares(1, kro[0:32, :], 32, self.cst("ones", 32, 0, 8), t_kro)
        for h in range(8):
            if h == 2:
                ret_logs()
            b = h % 2
            m = p.group(PB[b][0:96, :], [(wq[:, h, c, :], cq[c]) for c in range(3)], t_w[0], t_cq, *self.fr[b])
            add_up()
            t = squares(0, PB[b][0:96, :], 96, self.cst("oh", 96, 8 * h, 8), m)
            c = p.cp(qT[h][0:96, :], PB[b][0:96, :], m, free, t)
            self.fr[b] = (c, t)
            b = 2 + h % 2
            m = p.group(PB[b][0:64, :], [(wk[:, c_, 64 * h:64 * h + 64], ckv[c_]) for c_ in range(2)], t_w[1], t_ckv,
                        *self.fr[b])
            add_up()
            t = squares(1, PB[b][0:64, :], 64, self.cst("oh", 64, 8 * h, 8), m)
            c = p.cp(kT[h][0:64, :], PB[b][0:64, :], m, free, t)
            self.fr[b] = (c, t)
        for k in range(4):
            b = 6 + k % 2
            m = p.group(PB[b][:, :], [(ckv[c][:, 128 * k:128 * k + 128], wv[:, c, :]) for c in range(2)],
                        t_w[2], *self.fr[b])
            if k == 0:
                add_up(True)
            v = PB[b][:, :].rearrange("p (h e) -> p h e", h=8)
            t = p.act(vaug[:, k, 0:8:2, 0:64], v[:, 0:8:2, :], ACT.Copy, m, t_v1)
            t = p.act(vaug[:, k, 1:8:2, 64:128], v[:, 1:8:2, :], ACT.Copy, m, t_v1)
            self.fr[b] = (t,)
        t_v = (t, m)
        t_kv = m
        for i in range(2):
            t = p.act(rsum[i], PB[4 + i][0:8, :], ACT.Ln, self.t_sum, t_kv, scale=1.0 / 96, bias=self.col("eps6", 0, 0, 8))
        for i in range(2):
            t = p.act(rsum[i], rsum[i], ACT.Exp, t, scale=-0.5)
        self.fr[4] = self.fr[5] = (t,)
        t_rs = t
        scale = 96.0 ** -0.5
        ready = {}

        def spread(h):
            for i, (dst, gain) in enumerate(((qT[h], "qhn"), (kT[h], "khn"))):
                b = 6 + i
                m = p.mm(PB[b][0:96, :], sel[:, 128 * h:128 * h + 96], rsum[i], True, True, t_rs, t_sel, *self.fr[b],
                         sig=True, loose=True)
                t = p.stt(dst[0:96, :], dst[0:96, :], self.col(gain, 0, 0, 96), PB[b][0:96, :], ALU.mult, ALU.mult, m, t_k)
                self.fr[b] = (t,)
                ready[h, i] = t

        def turn(h):
            for i, dst in enumerate((qT[h], kT[h])):
                b = 6 + i
                m = p.mm(PB[b][0:96, :], self.cst("rot96", 96, 0, 96), dst[0:96, :], True, True, ready[h, i], *self.fr[b],
                         sig=True, loose=True)
                a = p.tt(dst[64:96, :], dst[64:96, :], c96[64:96, :], ALU.mult, m, eng="pool")
                s = p.tt(tr[i][64:96, :], PB[b][64:96, :], s96[64:96, :], ALU.mult, m, t_kv)
                self.fr[b] = (s,)
                ready[h, i] = p.tt(dst[64:96, :], dst[64:96, :], tr[i][64:96, :], ALU.add, a, s)

        top = {}

        def score(h, i):
            b = i % 2
            m = p.mm(PB[b][:, :], qT[h][0:96, 128 * i:128 * i + 128], kT[h][0:96, :], True, True, ready[h, 0], ready[h, 1],
                     *self.fr[b], sig=True)
            top[h] = p.rmax(mcol[h % 2][:, i:i + 1], PB[b][:, :], m)
            self.fr[b] = (top[h],)

        def bound(h):
            for i in range(4):
                m = p.mm(PB[7][96:97, 128 * i:128 * i + 128], mcol[h % 2][:, i:i + 1], self.cst("nident"), i == 0, i == 3,
                         top[h], *self.fr[7], sig=i == 3, loose=True)
            t = p.act(qT[h][96:97, :], PB[7][96:97, :], ACT.Copy, m)
            self.fr[7] = (t, *self.fr[7])
            ready[h, 2] = t

        pt_read = [()] * 4
        pt_tok = {}

        def prob(h, i):
            b = 2 + i % 2
            m = p.mm(PB[b][:, :], kT[h][0:97, 128 * i:128 * i + 128], qT[h][0:97, :], True, True, ready[h, 2], t_one,
                     *self.fr[b], sig=True)
            t = p.act(pT[i], PB[b][:, :], ACT.Exp, m, *pt_read[i], t_fin, scale=scale)
            self.fr[b] = (t,)
            pt_tok[i] = t

        def value(h, i):
            b = 4 + h % 2
            m = p.mm(PB[b][:, :], vaug[:, i, h, :], pT[i], i == 0, i == 3, pt_tok[i], t_v,
                     *(self.fr[b] if i == 0 else ()), sig=True)
            pt_read[i] = (m,)
            return m

        def divide(h, m):
            b = 4 + h % 2
            o, s = (slice(0, 64), slice(64, 128)) if h % 2 == 0 else (slice(64, 128), slice(0, 64))
            t = p.recip(rc[h % 2][o, :], PB[b][s, :], m)
            t = p.tt(H[o, h // 2, :], PB[b][o, :], rc[h % 2][o, :], ALU.mult, t)
            self.fr[b] = (t,)
            return t

        def nothing(*_):
            pass

        spread(0)
        turn(0)
        spread(1)
        for i in range(4):
            score(0, i)
        turn(1)
        bound(0)
        t_fin = ret_finish()
        for h in range(8):
            s1 = score if h < 7 else nothing
            prob(h, 0)
            prob(h, 1)
            s1(h + 1, 0)
            value(h, 0)
            s1(h + 1, 1)
            prob(h, 2)
            s1(h + 1, 2)
            value(h, 1)
            s1(h + 1, 3)
            prob(h, 3)
            if h > 0 and h % 2 == 0:
                self.square_sum(h // 2 - 1, H[:, h // 2 - 1, :], t)
            if h < 6:
                spread(h + 2)
            value(h, 2)
            m = value(h, 3)
            if h < 7:
                bound(h + 1)
            if h < 6:
                turn(h + 2)
            t = divide(h, m)
        return self.square_sum(3, H[:, 3, :], t)

    def ffn(self, layer):
        p, WK, PB = self.p, self.WK, self.PB
        act = self.normed(f"ffn{layer}", 2 * layer + 1, [WK[:, 36 + i, :] for i in range(3)])
        hid = [WK[:, 3 + i, :] for i in range(FF)]
        cv = [WK[:, 25 + i, :] for i in range(3)]
        tap = [self.small[:, 6 * i:6 * i + 6].rearrange("p (j t) -> p j t", j=3) for i in range(2)]
        done, sums = [], []
        gate = {}

        def begin(t0, t1, sc, t_sc):
            i, w = t0 // 2, tap[(t0 // 4) % 2]
            c = COL[f"cw{layer}"][0]
            src = self.cols[:, c:c + 3 * FF].rearrange("p (j t) -> p j t", j=3)[:, :, i:i + 2]
            return w, p.ts(w, src, sc, None, ALU.mult, None, t_sc, *self.evac.get(self.at - 3, ()))

        def use(t, b, m, sc, extra):
            i = t // 2
            ps = PB[b]
            if t % 2 == 0:
                c = cv[i % 3]
                w = [extra[0][:, j, i % 2:i % 2 + 1] for j in range(3)]
                a = p.act(c, ps[:, :], ACT.Identity, m, extra[1], *(done[i - 3:i - 2] if i >= 3 else ()), scale=w[1],
                          bias=self.col(f"cb{layer}", i))
                a = p.stt(c[:, 1:S], ps[:, 0:S - 1], w[0], c[:, 1:S], ALU.mult, ALU.add, a)
                a = p.stt(c[:, 0:S - 1], ps[:, 1:S], w[2], c[:, 0:S - 1], ALU.mult, ALU.add, a)
                gate[i] = p.act(c, c, ACT.Silu, a)
                return (a,)
            d = p.stt(hid[i], ps[:, :], sc, cv[i % 3], ALU.mult, ALU.mult, m, gate[i])
            done.append(d)
            sums.append(p.act(self.junk[:, 0:S], hid[i], ACT.Square, d, total=self.small[:, 256 + i:257 + i]))
            return (d,)

        self.project(f"w_up{layer}", 0, 2 * FF, KT, act, (0, 1, 2, 3), use, begin)
        self.add_out(f"w_down{layer}", self.parts_in_place(3, FF, 20, sums[-1]), FF,
                     then="sum" if layer else "rms")
        self.barrier()

    def odd0(self):
        p, X, H, WK, PB, sm = self.p, self.X, self.H, self.WK, self.PB, self.small
        act = self.normed("mix_odd", 2, [WK[:, 36 + i, :] for i in range(3)])
        gq = [WK[:, i, :] for i in range(0, 4)]
        gk = [WK[:, i, :] for i in range(4, 8)]
        gv = WK[:, 8:16, :].rearrange("p (q a) b -> p q (a b)", q=4)
        gr = [WK[:, i, :] for i in range(16, 24)]
        ga = WK[:, 24, :]
        sc = 128.0 ** -0.5
        qsc = [self.sc[:, 42:43], self.sc[:, 43:44]]
        T = [WK[:, i, :] for i in range(25, 40)]
        wide = self.AS[:, :, :].rearrange("p a b -> p (a b)").bitcast(F32).rearrange("p (t s) -> p t s", t=8)
        wg = self.flat(40, 42, 1024, 32)
        tw = self.side("w_gate", wg)
        wg = wg.rearrange("p (d n) -> p d n", d=2)

        def begin(t0, t1, sc_, t_sc):
            q = qsc[t0 // 3 % 2]
            return q, p.ts(q, sc_, sc, None, ALU.mult, None, t_sc, *self.evac.get(self.at - 3, ()))

        def use_qk(i, b, m, s_, x):
            dst = gq[i] if i < 4 else gk[i - 4] if i < 8 else ga
            return (p.act(dst, PB[b][:, :], ACT.Identity, m, x[1], scale=x[0] if i < 4 else s_),)

        self.project("w_odd_qk", 0, 9, KT, act, (0, 1, 2, 3), use_qk, begin)
        t_ga = p.last["act"]
        ax, bb, qc = T[0:2], T[2:4], T[4:6]
        at = [T[6:8], [wide[:, i, :] for i in (0, 1)]]
        qb = [T[8:10], [wide[:, i, :] for i in (2, 3)]]
        kc = [T[10:12], [wide[:, i, :] for i in (4, 5)]]
        chunk, rr = T[12:14], T[14]
        sst = [[wide[:, 6 + d, 256 * i:256 * i + 256] for i in range(2)] for d in range(2)]
        dec = [[sm[:, 16 * e + 8 * d:16 * e + 8 * d + 8] for d in range(2)] for e in range(2)]
        mask = [self.cst("mf").bitcast(U32), self.cst("mb").bitcast(U32)]
        v3 = lambda a: a.rearrange("p (c t) -> p c t", t=64)
        for d in range(2):
            p.memset(at[0][d], 0.0)
            t = p.memset(chunk[d], 1.0)
            edge = 0 if d == 0 else 63
            t_c = p.memset(chunk[d][:, edge:S:64], 0.0, t)
        none = [(), ()]
        bb_read, qc_read = list(none), list(none)
        at_read, qb_read, kdn_read = ([list(none), list(none)] for _ in range(3))
        done = {}
        ZB, AB, TB, NB, SB_ = 4, 0, 1, 1, (2, 5)
        obank = lambda h: (3, 4) if h % 2 == 0 else (6, 7)

        def gates(h, zb, ab, tb):
            e = h % 2
            tok = [{}, {}]
            D2 = range(2)
            for d in D2:
                k = tok[d]
                m = p.mm(PB[zb][:, :], wg[:, d, 128 * h:128 * h + 128], ga[0:32, :], True, True, tw, t_ga, *self.fr[zb],
                         sig=True)
                z = p.ts(bb[d], PB[zb][:, :], self.col("gb_f" if d == 0 else "gb_b", h), None, ALU.add, None, m, *bb_read[d])
                self.fr[zb] = (z,)
                k["min"] = p.ts(qc[d], bb[d], 0.0, None, ALU.min, None, *qc_read[d])
                p.act(ax[d], bb[d], ACT.Abs, z)
                p.act(ax[d], ax[d], ACT.Exp, scale=-1.0)
                yield
            for d in D2:
                tok[d]["ln"] = p.act(ax[d], ax[d], ACT.Ln, bias=1.0)
                yield
            for d in D2:
                k = tok[d]
                p.tt(bb[d], qc[d], ax[d], ALU.subtract, k["ln"])
                if d == 0:
                    k["b"] = p.scan(ax[d], chunk[0], bb[d], 0.0, ALU.mult, ALU.add, t_c)
                else:
                    k["b"] = p.scan(ax[d][:, ::-1], chunk[1][:, ::-1], bb[d][:, ::-1], 0.0, ALU.mult, ALU.add, t_c)
                mid = 32 if d == 0 else 31
                b3 = v3(ax[d])
                k["mid"] = p.tt(v3(bb[d]), b3, b3[:, :, mid:mid + 1].to_broadcast([128, 8, 64]), ALU.subtract)
                yield
            for d in D2:
                k = tok[d]
                b3 = v3(ax[d])
                last = 63 if d == 0 else 0
                k["q"] = p.act(qc[d], bb[d], ACT.Exp, k["mid"], scale=1.0 / 16)
                k["k"] = p.act(kc[e][d], bb[d], ACT.Exp, *kdn_read[e][d], scale=-1.0 / 16)
                k["qb"] = p.act(qb[e][d], ax[d], ACT.Exp, *qb_read[e][d], scale=1.0 / 16)
                k["dec"] = p.act(dec[e][d], b3[:, :, last:last + 1].rearrange("p c o -> p (c o)"), ACT.Exp, scale=1.0 / 16)
                yield
            for d in D2:
                k = tok[d]
                b3 = v3(ax[d])
                last = 63 if d == 0 else 0
                k["far"] = p.tt(v3(bb[d]), b3[:, :, last:last + 1].to_broadcast([128, 8, 64]), b3, ALU.subtract, k["k"])
                k["q"] = p.tt(qc[d], qc[d], gq[h], ALU.mult, k["q"], eng="pool")
                k["k"] = p.tt(kc[e][d], kc[e][d], gk[h], ALU.mult, k["k"], eng="pool")
                k["kd"] = p.act(bb[d], bb[d], ACT.Exp, k["far"], scale=1.0 / 16)
                yield
            for d in D2:
                k = tok[d]
                k["kd"] = p.tt(bb[d], bb[d], gk[h], ALU.mult, k["kd"], eng="pool")
                k["qb"] = p.tt(qb[e][d], qb[e][d], gq[h], ALU.mult, k["qb"], eng="pool")
                yield
            for d in D2:
                k = tok[d]
                for q in range(4):
                    c = slice(128 * q, 128 * q + 128)
                    m = p.mm(PB[ab][:, c], kc[e][d][:, c], qc[d][:, c], True, True, k["q"], k["k"],
                             *(self.fr[ab] if q == 0 else ()), sig=q == 3)
                qc_read[d] = (m,)
                k["at"] = p.cpred(at[e][d].rearrange("p (q j) -> p q j", q=4),
                                  mask[d].unsqueeze(1).to_broadcast([128, 4, 128]),
                                  PB[ab][:, :].rearrange("p (q j) -> p q j", q=4), m, t_c, *at_read[e][d])
                self.fr[ab] = (k["at"],)
                yield
            for d in D2:
                k = tok[d]
                for q in range(4):
                    c = slice(128 * q, 128 * q + 128)
                    m = p.tr(PB[tb][:, c], bb[d][:, c], self.cst("ident"), k["kd"], *(self.fr[tb] if q == 0 else ()),
                             sig=q == 3)
                bb_read[d] = (m,)
                k["kdn"] = p.act(kc[e][d], PB[tb][:, :], ACT.Copy, m)
                self.fr[tb] = (k["kdn"],)
                yield
            done[h] = tok

        g = gates(0, ZB, 5, 6)

        def use_v(n, q, b, m, s_):
            t = p.act(gv[:, q, 512 * n:512 * n + 512], PB[b][:, :], ACT.Identity, m, scale=s_)
            if n == 1:
                next(g, None)
            return (t,)

        self.project_rows("w_odd_v", 0, 8, act, (0, 1, 2, 3), use_v)
        t_gv = p.last["act"]

        def use_r(i, b, m, s_, x):
            t = p.act(gr[i - 8], PB[b][:, :], ACT.Silu, m, scale=s_)
            next(g, None)
            next(g, None)
            return (t,)

        self.project("w_odd_v", 8, 8, KT, act, (0, 1, 2, 3), use_r)
        m_act = self.pe_done[self.at - 1]
        for _ in g:
            pass
        for d in range(2):
            t_c = p.memset(at[1][d], 0.0, m_act)
        finals = {}

        def squares(h):
            for e, b in enumerate(obank(h)):
                finals[h, e] = p.act(H[:, 2 * h + e, :], PB[b][:, :], ACT.Square, finals[h])

        def total(h):
            for e in range(2):
                m = p.mm(PB[NB][:, :], self.cst("ones"), H[:, 2 * h + e, :], e == 0, e == 1, finals[h, e],
                         *(self.fr[NB] if e == 0 else ()), sig=True)
            finals[h] = m

        def scaled(h, step):
            if step == 0:
                finals[h] = self.rstd(rr, PB[NB][:, :], 256, self.col("eps6"), 128, finals[h])
                self.fr[NB] = (finals[h],)
                return
            e = step - 1
            b = obank(h)[e]
            i = 2 * h + e
            x = p.stt(H[:, i, :], PB[b][:, :], self.col("gla_norm", i), rr, ALU.mult, ALU.mult, finals[h])
            self.fr[b] = (x,)
            finals[h, e] = p.tt(H[:, i, :], H[:, i, :], gr[i], ALU.mult)

        def head_sum(h):
            for e in range(2):
                t = self.square_sum(2 * h + e, H[:, 2 * h + e, :], finals[h, e])
            return t

        for h in range(4):
            e_ = h % 2
            tok = done[h]
            banks = obank(h)
            first = [True, True]

            def out(e, cols, w, r, *after, sig=False):
                b = banks[e]
                m = p.mm(PB[b][:, cols], w, r, first[e], False, *after, *(self.fr[b] if first[e] else ()),
                         sig=sig, loose=True)
                first[e] = False
                return m

            for d in range(2):
                for q in range(4):
                    for e in range(2):
                        c = slice(128 * q, 128 * q + 128)
                        m = out(e, c, gv[:, q, 256 * h + 128 * e:256 * h + 128 * e + 128], at[e_][d][:, c], tok[d]["at"],
                                t_gv, sig=True)
                at_read[e_][d] = (m,)
            t_s = [None, None]
            m_in = [None, None]
            g = gates(h + 1, AB, AB, TB) if h < 3 else iter(())
            fr_s = [self.fr[b] for b in SB_]
            for n in range(8):
                for d in range(2):
                    k = tok[d]
                    c = n if d == 0 else 7 - n
                    cc = slice(64 * c, 64 * c + 64)
                    prev, new = sst[d][(n + 1) % 2], sst[d][n % 2]
                    ps = PB[SB_[d]][:, 0:256]
                    if n < 7:
                        r0 = 64 * (c % 2)
                        q = c // 2
                        m = p.mm(ps, kc[e_][d][r0:r0 + 64, 128 * q:128 * q + 128],
                                 gv[r0:r0 + 64, q, 256 * h:256 * h + 256], True, True, k["kdn"], *fr_s[d], sig=True, loose=True)
                        kdn_read[e_][d] = (m,)
                    if n > 0:
                        for e in range(2):
                            m_in[d] = out(e, cc, prev[:, 128 * e:128 * e + 128], qb[e_][d][:, cc], t_s[d], k["qb"], sig=True)
                    if n < 7:
                        if n == 0:
                            t_s[d] = p.cp(new, ps, m, *qb_read[1 - e_][d], m_act)
                        else:
                            t_s[d] = p.stt(new, prev, dec[e_][d][:, c:c + 1], ps, ALU.mult, ALU.add, m, k["dec"], *was[d])
                        fr_s[d] = (t_s[d],)
                    next(g, None)
                was = [(m_in[0],), (m_in[1],)]
                if h > 0 and n == 1:
                    total(h - 1)
                if h > 0 and n in (2, 3, 4):
                    scaled(h - 1, n - 2)
                if h > 0 and n == 6:
                    head_sum(h - 1)
            for _ in g:
                pass
            for d in range(2):
                self.fr[SB_[d]] = fr_s[d]
            qb_read[e_] = [(m_in[0],), (m_in[1],)]
            finals[h] = m_in[1]
            squares(h)
        total(3)
        t_tot = finals[3]
        for step in range(3):
            scaled(3, step)
        t = head_sum(3)
        self.add_out("w_out_odd", self.parts([H[:, i, :] for i in range(KT)], measured=t, after=t_tot), then="rms")
        self.barrier()

    def even1(self):
        p, X, H, WK, PB, sm = self.p, self.X, self.H, self.WK, self.PB, self.small
        xs = [X[:, i, :] for i in range(KT)]
        fq = [WK[:, i, :] for i in range(0, 4)]
        fk = [WK[:, i, :] for i in range(4, 8)]
        vaug = WK[:, 8:16, :].rearrange("p a b -> p (a b)").rearrange("p (k h e) -> p k h e", k=4, h=8)
        u = [WK[:, i, :] for i in range(16, 20)]
        c = WK[0:8, 20, :]
        t1, t2, one = WK[0:8, 21, :], WK[0:8, 22, :], WK[0:8, 23, :]
        act = self.parts(xs, measured=self.t_sums if self.have == "sum" else None)
        self.have = None
        t_v1 = p.memset(vaug, 1.0)
        t_one = p.memset(one, 1.0)
        wf = self.flat(33, 34, 64).rearrange("p (k e) -> p k e", k=8)
        tw = self.side("w_fox_f", self.flat(33, 34, 64))
        qsc = self.sc[:, 42:43]

        def begin(t0, t1, sc, t_sc):
            return p.ts(qsc, sc, 0.125, None, ALU.mult, None, t_sc)

        self.project("w_in_even_2", 0, 4, KT, act, (0, 1, 2, 3),
                     lambda i, b, m, s_, x: (p.act(fq[i], PB[b][:, :], ACT.Identity, m, x, scale=qsc),), begin)
        m = p.group(PB[4][0:8, :], [(wf[:, k, :], xs[k]) for k in range(KT)], tw, *self.fr[4])
        t = p.ts(c, PB[4][0:8, :], self.col("fox_fb", 0, 0, 8), None, ALU.add, None, m)
        self.fr[4] = (t,)
        t = self.log_sigmoid(c, c, t1, t2, (t,))
        t_cum = p.scan(t1, one, c, 0.0, ALU.mult, ALU.add, t, t_one)
        cum = t1
        s5, s5_turn = self.s5_setup()
        t_f = m

        def use_k(i, b, m, s_, x):
            self.grow(i - 4, t_f, *act.ready)
            return (p.act(fk[i - 4], PB[b][:, :], ACT.Identity, m, scale=s_),)

        self.project("w_in_even_2", 4, 4, KT, act, (0, 1, 2, 3), use_k)

        def use_v(n, k, b, m, s_):
            self.grow(4 + k)
            v = PB[b][:, :].rearrange("p (h e) -> p h e", h=8)
            t = p.act(vaug[:, k, 0:8:2, 0:64], v[:, 0:8:2, :], ACT.Identity, m, t_v1, scale=s_)
            return (p.act(vaug[:, k, 1:8:2, 64:128], v[:, 1:8:2, :], ACT.Identity, m, t_v1, scale=s_),)

        self.project_rows("w_in_even_2", 8, 4, act, (0, 1, 2, 3), use_v)
        s5_turn()
        self.project("w_in_even_2", 12, 4, KT, act, (0, 1, 2, 3),
                     lambda i, b, m, s_, x: (p.act(u[i - 12], PB[b][:, :], ACT.Identity, m, scale=s_),))
        self.barrier()
        t_y = self.fox_s5(fq, fk, vaug, cum, u, s5)
        ys = [H[:, 4 + i, :] for i in range(4)]
        for i in range(4):
            p.act(ys[i], ys[i], ACT.Gelu_apprx_tanh, t_y[i])
            t = self.square_sum(i, ys[i])
        act = self.parts(ys, log2n=18, measured=t)
        gate = [WK[:, 20 + i, :] for i in range(4)]

        def use(i, b, m, s_, extra):
            a = p.act(gate[i], PB[b][:, :], ACT.Sigmoid, m, scale=s_, bias=self.col("b_glu", i))
            t = p.tt(ys[i], ys[i], gate[i], ALU.mult, a, act.ready[3])
            self.square_sum(i, H[:, i, :])
            self.square_sum(4 + i, ys[i], t)
            return (a,)

        self.project("w_glu", 0, 4, 4, act, (0, 1, 2, 3), use)
        t = p.last["act"]
        weights = self.moe_weights(0)
        self.add_out("w_out_even_2", self.parts([H[:, i, :] for i in range(KT)], measured=t, after=self.pe_done[self.at - 1]),
                     then="mean")
        self.barrier()
        self.layernorm(0)
        return weights

    def s5_setup(self):
        p, WK, PB, sm = self.p, self.WK, self.PB, self.small
        br, bi = (self.flat(38 + i, 39 + i, 512).rearrange("p (s c) -> p s c", s=16) for i in range(2))
        tbr = self.side("s5_br", self.flat(38, 39, 512))
        tbi = self.side("s5_bi", self.flat(39, 40, 512))
        (dt, mag, th, k, r, cs, sn, nre, nim, den, zr, zi, f, t1) = (
            sm[:, 16 * i:16 * i + 16] for i in range(14))
        are, aim = self.col("a_re", n=16), self.col("a_im", n=16)
        M, A, SB = ALU.mult, ALU.add, ALU.subtract
        t = p.act(dt, self.col("log_dt", n=16), ACT.Exp)
        t = p.tt(mag, are, dt, M, t)
        t_mag = p.act(mag, mag, ACT.Exp, t)
        t = p.tt(th, aim, dt, M)
        t = p.ts(k, th, 1.0 / TWO_PI, MAGIC, M, A)
        t = p.ts(k, k, MAGIC, None, SB, None)
        t = p.stt(r, k, -C1, th, M, A)
        t = p.stt(r, k, -C2, r, M, A)
        t = p.stt(r, k, -C3, r, M, A)
        t = p.ts(r, r, PI_IN, -PI_IN, ALU.min, ALU.max)
        p.ts(f, r, 1.0 / TWO_PI, None, M, None)
        a = p.act(cs, r, ACT.Abs, t)
        a = p.act(cs, cs, ACT.Sin, a, scale=-1.0, bias=self.col("halfpi"))
        a = p.act(sn, r, ACT.Sin, t)
        p.tt(nre, mag, cs, M, a, t_mag)
        p.ts(nre, nre, -1.0, None, A, None)
        p.tt(nim, mag, sn, M)
        p.tt(den, are, are, M)
        p.tt(t1, aim, aim, M)
        p.tt(den, den, t1, A)
        p.recip(den, den)
        p.tt(zr, nre, are, M)
        p.tt(t1, nim, aim, M)
        p.tt(zr, zr, t1, A)
        p.tt(zr, zr, den, M)
        p.tt(zi, nim, are, M)
        p.tt(t1, nre, aim, M)
        p.tt(zi, zi, t1, SB)
        t_z = p.tt(zi, zi, den, M)
        v3 = lambda a: a.rearrange("p (s c) -> p s c", s=16)
        bbr, bbi, tx = (WK[:, i, :] for i in (40, 41, 24))
        bbrT, bbiT, T = (WK[:, i, :] for i in (35, 36, 37))
        bz = lambda a: a.unsqueeze(2).to_broadcast([128, 16, 32])
        p.tt(v3(bbr), br, bz(zr), M, tbr, tbi, t_z)
        p.tt(v3(tx), bi, bz(zi), M)
        t_r = p.tt(bbr, bbr, tx, SB)
        p.tt(v3(bbi), bi, bz(zr), M)
        p.tt(v3(tx), br, bz(zi), M)
        t_i = p.tt(bbi, bbi, tx, A)
        ti = tx.bitcast(I32)
        t = p.put("pool", lambda e: e.iota(ti, [[1, S]], base=0, channel_multiplier=0), (t_i,))
        p.cp(T, ti, t, eng="pool")

        def turn():
            for b, src, dst, t in ((5, bbr, bbrT, t_r), (6, bbi, bbiT, t_i)):
                for q in range(4):
                    cc = slice(128 * q, 128 * q + 128)
                    m = p.tr(PB[b][:, cc], src[:, cc], self.cst("ident"), t, *self.fr[b], sig=q == 3)
                self.fr[b] = (p.act(dst, PB[b][:, :], ACT.Copy, m),)

        return (bbrT, bbiT, T, mag, f), turn

    def fox_s5(self, fq, fk, vaug, cum, u, system):
        p, H, WK, PB, sm = self.p, self.H, self.WK, self.PB, self.small
        M, A, SB = ALU.mult, ALU.add, ALU.subtract
        wide = self.AS[:, :, :].rearrange("p a b -> p (a b)").bitcast(F32).rearrange("p (t s) -> p t s", t=8)
        qT = [WK[:, 24, :], WK[:, 25, :]]
        kT = [WK[:, 26, :], WK[:, 27, :]]
        pT = [WK[:, i, :] for i in range(28, 32)]
        rc = WK[:, 32, :]
        fsel = self.flat(33, 35, 1024, 8)
        t_fs = self.side("foxsel", fsel)
        mcol = [sm[:, 224:228], sm[:, 228:232]]
        for i in range(2):
            p.memset(qT[i][64:96, :], 0.0)
            p.memset(kT[i][64:96, :], 0.0)
            p.memset(qT[i][96:97, :], 1.0)
            t_one = p.memset(kT[i][64:65, :], 1.0)
        used = [(), ()]
        pt_read = [()] * 4
        pt_tok = {}
        ready, top, n_s = {}, {}, [0]
        CB, OB = 3, 4

        def bank():
            n_s[0] += 1
            return n_s[0] % 3

        def make(h):
            r0 = 64 * (h % 2)
            j = h % 2
            m = p.mm(PB[CB][:, :], fsel[:, 128 * h:128 * h + 128], cum, True, False, t_fs, *self.fr[CB], sig=True,
                     loose=True)
            p.act(qT[j][0:64, :], fq[h // 2][r0:r0 + 64, :], ACT.Copy, *used[j])
            b = p.cp(kT[j][0:64, :], fk[h // 2][r0:r0 + 64, :], *used[j], eng="pool")
            p.act(qT[j][64:65, :], PB[CB][64:65, :], ACT.Copy, m, t_one)
            a = p.act(kT[j][96:97, :], PB[CB][96:97, :], ACT.Copy, m, *used[j])
            ready[h] = (a, b)

        def score(h, i):
            b = bank()
            n = 128 * i + 128
            p.mm(PB[b][:, 0:n], qT[h % 2][0:97, 128 * i:n], kT[h % 2][0:97, 0:n], True, False, *ready[h], *self.fr[b],
                 loose=True)
            m = p.mm(PB[b][:, 128 * i:n], self.cst("ident"), self.cst("maskn"), False, True, sig=True, loose=True)
            top[h] = p.rmax(mcol[h % 2][:, i:i + 1], PB[b][:, 0:n], m)
            self.fr[b] = (top[h],)

        def bound(h):
            for i in range(4):
                m = p.mm(PB[CB][64:65, 128 * i:128 * i + 128], mcol[h % 2][:, i:i + 1], self.cst("nident"), False, i == 3,
                         top[h], sig=i == 3, loose=True)
            ready[h] = (p.act(qT[h % 2][64:65, :], PB[CB][64:65, :], ACT.Copy, m),)
            self.fr[CB] = ready[h]

        def prob(h, i):
            b = bank()
            lo = 128 * i
            p.mm(PB[b][:, lo:S], kT[h % 2][0:97, lo:lo + 128], qT[h % 2][0:97, lo:S], True, False, *ready[h], *self.fr[b],
                 loose=True)
            m = p.mm(PB[b][:, lo:lo + 128], self.cst("ident"), self.cst("maskt"), False, True, sig=True, loose=True)
            t = p.act(pT[i][:, lo:S], PB[b][:, lo:S], ACT.Exp, m, *pt_read[i])
            self.fr[b] = (t,)
            used[h % 2] = (m,)
            pt_tok[i] = t

        def value(h, i):
            lo = 128 * i
            m = p.mm(PB[OB][:, lo:S], vaug[:, i, h, :], pT[i][:, lo:S], i == 0, i == 3, pt_tok[i],
                     *(self.fr[OB] if i == 0 else ()), sig=True, loose=True)
            pt_read[i] = (m,)
            return m

        def divide(h, m):
            o, s = (slice(0, 64), slice(64, 128)) if h % 2 == 0 else (slice(64, 128), slice(0, 64))
            t = p.recip(rc[o, :], PB[OB][s, :], m)
            t = p.tt(H[o, h // 2, :], PB[OB][o, :], rc[o, :], M, t)
            self.fr[OB] = (t,)

        bbrT, bbiT, T, mag, f = system
        cre, cim = (wide[:, i, :].rearrange("p (s c) -> p s c", s=16) for i in range(2))
        tcr = self.side("s5_cr", wide[:, 0, :])
        tci = self.side("s5_ci", wide[:, 1, :])
        tci = p.act(wide[:, 1, :], wide[:, 1, :], ACT.Copy, tci, scale=-1.0)
        nre = wide[:, 2, :]
        tcr = p.act(nre, wide[:, 0, :], ACT.Copy, tcr, scale=-1.0)
        nre = nre.rearrange("p (s c) -> p s c", s=16)
        x1 = WK[:, 23, :]
        ws = [(WK[:, 20, :], WK[:, 22, :]), (wide[:, 7, :], H[:, 7, :])]
        xs = [(wide[:, 3, :], wide[:, 4, :]), (wide[:, 5, :], wide[:, 6, :])]
        turn = [(WK[:, 38, :], WK[:, 39, :]), (WK[:, 40, :], WK[:, 41, :])]
        t_turn, turn_read, h_read, y_m, h_tok = {}, [(), ()], [(), ()], {}, {}
        UB, YB = (5, 6), 7

        def angle(st):
            if st < 16:
                co, si = turn[st % 2]
                p.ts(si, T, f[:, st:st + 1], None, M, None, *turn_read[st % 2], eng="pool")
                p.ts(co, si, MAGIC, MAGIC, A, SB, eng="pool")
                t_turn[st] = p.tt(si, si, co, SB, eng="pool")

        def sines(st):
            if st < 16:
                co, si = turn[st % 2]
                p.act(co, si, ACT.Abs, t_turn[st])
                p.act(co, co, ACT.Sin, scale=-6.283184, bias=self.col("halfpi"))
                t_turn[st] = p.act(si, si, ACT.Sin, scale=6.283184)

        def drive(st):
            rows, kk = slice(32 * (st % 4), 32 * (st % 4) + 32), st // 4
            m = p.mm(PB[UB[0]][:, :], bbrT[rows, 128 * kk:128 * kk + 128], u[kk][rows, :], True, True, *self.fr[UB[0]])
            m = p.mm(PB[UB[1]][:, :], bbiT[rows, 128 * kk:128 * kk + 128], u[kk][rows, :], True, True, *self.fr[UB[1]],
                     sig=True)
            return m

        def states(st, m):
            co, si = turn[st % 2]
            ur, ui = PB[UB[0]], PB[UB[1]]
            wr, wi = ws[st % 2]
            rc_, is_ = xs[st % 2]
            p.tt(wr, ur[:, :], co, M, m, t_turn[st], *h_read[st % 2])
            p.tt(x1, ui[:, :], si, M)
            p.tt(wr, wr, x1, A)
            p.tt(wi, ui[:, :], co, M)
            t = p.tt(x1, ur[:, :], si, M)
            self.fr[UB[0]] = self.fr[UB[1]] = (t,)
            p.tt(wi, wi, x1, SB)
            mg = mag[:, st:st + 1].to_broadcast([128, S])
            t = p.scan(wr, mg, wr, 0.0, M, A)
            p.tt(rc_, wr, co, M, t, *h_read[st % 2], eng="pool")
            t_p = p.tt(wr, wr, si, M, eng="pool")
            p.scan(wi, mg, wi, 0.0, M, A)
            p.tt(is_, wi, si, M)
            t = p.tt(wi, wi, co, M)
            h_tok[st] = turn_read[st % 2] = (t, t_p)

        def observe(st):
            q, kk = st % 4, st // 4
            rows = slice(32 * q, 32 * q + 32)
            wr, wi = ws[st % 2]
            rc_, is_ = xs[st % 2]
            out = PB[YB][rows, :]
            p.mm(out, cre[:, st, :], rc_, True, False, tcr, *h_tok[st], *(self.fr[YB] if q == 0 else ()), loose=True)
            p.mm(out, nre[:, st, :], is_, False, False, loose=True)
            p.mm(out, cim[:, st, :], wr, False, False, tci, loose=True)
            m = p.mm(out, cim[:, st, :], wi, False, True, sig=True, loose=True)
            h_read[st % 2] = (m,)
            if q == 3:
                t = p.stt(H[:, 4 + kk, :], u[kk], self.col("s5_d", kk), PB[YB][:, :], M, A, m)
                self.fr[YB] = (t,)
                t_y.append(t)

        t_y = []

        def nothing(*_):
            pass

        make(0)
        for st in range(2):
            angle(st)
        sines(0)
        for i in range(4):
            score(0, i)
        bound(0)
        m = drive(0)
        for h in range(8):
            st = 2 * h
            if h > 0:
                observe(st - 2)
            prob(h, 0)
            prob(h, 1)
            value(h, 0)
            prob(h, 2)
            value(h, 1)
            if h < 7:
                make(h + 1)
            states(st, m)
            prob(h, 3)
            m = drive(st + 1)
            value(h, 2)
            m_v = value(h, 3)
            angle(st + 2)
            sines(st + 1)
            st += 1
            if h > 0:
                observe(st - 2)
            if h < 7:
                for i in range(4):
                    score(h + 1, i)
            states(st, m)
            divide(h, m_v)
            if h < 7:
                bound(h + 1)
                m = drive(st + 1)
            angle(st + 2)
            sines(st + 1)
        observe(14)
        observe(15)
        return t_y

    def turn_of(self, name):
        sem, n = self.named.get(name) or (self.sem(name), 0)
        self.named[name] = (sem, n + 16)
        return sem, n + 16

    def moe_weights(self, layer):
        p = self.p
        gu = [self.flat(8 * i, 8 * i + 8, 4096) for i in range(3)]
        dn = [self.flat(24 + 4 * i, 28 + 4 * i, 2048) for i in range(3)]
        t_gu, t_dn = {}, {}
        now = [p.last[k] for k in ("pe", "act", "dve", "pool")]
        for b in range(3):
            t_gu[b] = p.dma("sp", gu[b], self.ins[f"moe_up{layer}"][128 * b:128 * b + 128, :], *self.turn_of(f"u{b}"), now)
            t_dn[b] = p.dma("sp", dn[b], self.ins[f"moe_down{layer}"][128 * b:128 * b + 128, :], *self.turn_of(f"d{b}"), now)
        return gu, dn, t_gu, t_dn

    def moe(self, layer, weights=None):
        p, X, T, PB, sm = self.p, self.X, self.T, self.PB, self.small
        NE, NB = 16, 23
        nc = self.nc
        gu, dn, t_gu, t_dn = weights or self.moe_weights(layer)
        xs = [X[:, i, :] for i in range(KT)]
        M, A, SB, MX = ALU.mult, ALU.add, ALU.subtract, ALU.max
        rows_d = nc.dram_tensor(f"moe_x{layer}", (S, D), F32, kind="Internal").ap()
        out_d = nc.dram_tensor(f"moe_y{layer}", (NB * 128, D), F32, kind="Internal").ap()

        xg = [self.flat(36 + 2 * i, 38 + 2 * i, 1024) for i in range(2)]
        xT = [self.flat(40 + 2 * i, 42 + 2 * i, 1024) for i in range(2)]
        hid = [T[:, 44, 256 * i:256 * i + 256] for i in range(2)]
        sl = [T[:, 45, 256 * i:256 * i + 256] for i in range(2)]
        hT = [T[:, 46, 256 * i:256 * i + 256] for i in range(2)]
        wr = T[:, 47, 0:160].rearrange("p (k e) -> p k e", k=8)
        slot = T[:, 48, :]
        xrow = self.AS[:, :, :].rearrange("p a b -> p (a b)").bitcast(F32).rearrange("p (q d) -> p q d", q=4)
        xflat = X[:, :, :].rearrange("p a b -> p (a b)")
        onehot = xflat[:, 0:2048].bitcast(F16).rearrange("p (k s) -> p k s", k=8)
        yst = [xflat[:, 2048 + 1024 * i:3072 + 1024 * i] for i in range(2)]

        tw = self.side(f"w_route{layer}", T[:, 47, 0:160])
        for k in range(KT):
            for q in range(4):
                m = p.mm(PB[7][:, 20 * q:20 * q + 20], xs[k][:, 128 * q:128 * q + 128], wr[:, k, :], k == 0 and q == 0,
                         k == 7 and q == 3, tw, *self.x_tok[k], *(self.fr[7] if k == 0 else ()), sig=k == 7 and q == 3,
                         loose=True)
        t_lg = m
        self.x_tok = [()] * KT
        t_row = []
        for q in range(4):
            got = []
            for half in range(2):
                b = 2 * (q % 2) + half
                for i in range(4):
                    m = p.tr(PB[b][:, 128 * i:128 * i + 128], xs[4 * half + i][:, 128 * q:128 * q + 128], self.cst("ident"),
                             *(self.fr[b] if i == 0 else ()), sig=i == 3)
                t = p.act(xrow[:, q, 512 * half:512 * half + 512], PB[b][:, :], ACT.Copy, m)
                self.fr[b] = (t,)
                got.append(t)
            t_row.append(p.dma("sp", rows_d[128 * q:128 * q + 128, :], xrow[:, q, :],
                               *self.turn_of(f"r{q}"), got))
        x_read = m
        off = [0, 0]

        def tile(*shape, wide=False):
            n = int(np.prod(shape))
            a = (T[:, 49, :] if wide else sm)[:, off[wide]:off[wide] + n]
            off[wide] += n
            if len(shape) == 2:
                return a.rearrange("p (a b) -> p a b", a=shape[0])
            if len(shape) == 3:
                return a.rearrange("p (a b c) -> p a b c", a=shape[0], b=shape[1])
            return a

        ni = tile(64, wide=True)
        nint = ni.bitcast(I32)
        si = sl[0].bitcast(I32)
        t = p.put("pool", lambda e: e.iota(slot.bitcast(I32), [[1, S]], base=0, channel_multiplier=0), ())
        t_slot = p.cp(slot, slot.bitcast(I32), t, eng="pool")
        t = p.put("pool", lambda e: e.iota(nint[:, 0:NE], [[1, NE]], base=0, channel_multiplier=0), ())
        t = p.put("pool", lambda e: e.iota(nint[:, 32:36], [[128, 4]], base=0, channel_multiplier=1), ())
        num, tok = ni[:, 0:NE], ni[:, 32:36]
        t = p.cp(num, nint[:, 0:NE], eng="pool")
        t = p.cp(tok, nint[:, 32:36], eng="pool")
        tok16 = tile(2, wide=True).bitcast(F16)
        t_num = p.cp(tok16, tok, eng="pool")

        lg = tile(4, 20)
        t = p.tt(lg, PB[7][:, 0:80].rearrange("p (a b) -> p a b", a=4),
                 self.col(f"mb{layer}", n=20).unsqueeze(1).to_broadcast([128, 4, 20]), A, t_lg)
        self.fr[7] = (t,)

        def wide(a, n=4):
            return a.unsqueeze(2).to_broadcast([128, 4, n])

        def softmax(src):
            mx, ex, sn = tile(4), tile(4, 4), tile(4)
            p.rmax(mx, src)
            t = p.tt(ex, src, wide(mx), SB)
            t = p.act(ex, ex, ACT.Exp, t)
            p.rsum(sn, ex, t)
            p.recip(sn, sn)
            p.tt(ex, ex, wide(sn), M)
            return ex

        def top(prob):
            mx, eq = tile(4), tile(4, 4)
            p.rmax(mx, prob)
            p.tt(eq, prob, wide(mx), ALU.is_equal)
            f = lambda a: a.rearrange("p a b -> p (a b)")
            p.scan(f(cum), f(fresh), f(eq), 0.0, M, A)
            p.stt(f(eq), f(cum), 1.0, f(eq), ALU.is_equal, M)
            return mx, eq

        fresh, cum = (T[:, 47, 400 + 16 * i:416 + 16 * i].rearrange("p (a b) -> p a b", a=4) for i in range(2))
        p.memset(fresh, 1.0, eng="dve")
        p.memset(fresh[:, :, 0:1], 0.0, eng="dve")
        gp = softmax(lg[:, :, 0:4])
        gv, goh = top(gp)
        pick, el = tile(4, 4), tile(4, 4)
        for g in range(4):
            dst = el if g == 0 else pick
            p.tt(dst, lg[:, :, 4 + 4 * g:8 + 4 * g], wide(goh[:, :, g]), M)
            if g:
                p.tt(el, el, pick, A)
        ep = softmax(el)
        v1, oh1 = top(ep)
        rest = tile(4, 4)
        p.stt(rest, oh1, -2.0, ep, M, A)
        v2, oh2 = top(rest)
        one = [tile(4, 4, 4, wide=True) for _ in range(2)]
        both = tile(4, 16, wide=True)
        before = T[:, 47, 320:384].rearrange("p (q e) -> p q e", q=4)
        for a, oh in zip(one, (oh1, oh2)):
            for g in range(4):
                t = p.tt(a[:, :, g, :], oh, wide(goh[:, :, g]), M)
        pairs = [a.rearrange("p q g e -> p q (g e)") for a in one]
        t = p.tt(both, pairs[0], pairs[1], A, t)
        r3 = lambda a: a.rearrange("p (q e) -> p q e", q=4)
        flat = both.rearrange("p q e -> p (q e)")
        upto, all_ = PB[6][:, 0:64], PB[6][:, 64:80]
        p.mm(upto, self.cst("causal"), flat, True, False, t, *self.fr[6], loose=True)
        p.tt(before[:, 1, :], both[:, 0, :], both[:, 1, :], A)
        p.cp(before[:, 0, :], both[:, 0, :])
        p.tt(before[:, 2, :], before[:, 1, :], both[:, 2, :], A)
        t = p.tt(before[:, 3, :], before[:, 2, :], both[:, 3, :], A)
        p.mm(upto[:, 16:64], self.cst("ones"), before[:, 0:3, :].rearrange("p q e -> p (q e)"), False, True, t, loose=True)
        m = p.mm(all_, self.cst("ones"), before[:, 3, :], True, True, loose=True, sig=True)
        den = tile(4)
        p.tt(den, v1, v2, A)
        p.recip(den, den)
        p.tt(den, den, gv, M)
        p.tt(v1, v1, den, M)
        t_v = p.tt(v2, v2, den, M)
        more, end, far, one16 = (tile(16, wide=True) for _ in range(4))
        own = T[:, 47, 432:448]
        p.memset(one16, 1.0, eng="dve")
        p.ts(own, num, 128.0, -1.0, M, A, t_num)
        p.ts(end, all_, -1.0, 0.0, A, MX, m)
        p.cp(far.bitcast(I32), end)
        p.ts(end.bitcast(I32), far.bitcast(I32), 7, None, ALU.logical_shift_right, None)
        p.cp(more, end.bitcast(I32))
        p.scan(end, one16, more, 0.0, M, A)
        p.tt(far, end, more, SB)
        p.tt(far, far, num, SB, t_num)
        p.ts(far, far, float(NE - 1), 128.0, A, M)
        at, over = tile(4, 16, wide=True), tile(4, 16, wide=True)
        q16 = lambda a: a.unsqueeze(1).to_broadcast([128, 4, 16])
        p.ts(over, r3(upto), 128.5, None, ALU.is_gt, None)
        p.tt(over, over, q16(far), M)
        t = p.tt(at, r3(upto), q16(own), A)
        self.fr[6] = (t,)
        p.tt(at, at, over, A)
        pos, rel = tile(2, 4, wide=True), tile(8, wide=True)
        for a, ps in zip(pairs, (pos[:, 0, :], pos[:, 1, :])):
            p.tt(a, a, at, M)
            p.rsum(ps, a)
        pos = pos.rearrange("p k q -> p (k q)")
        pos_i, w_i, x_i = (sm[:, o:o + n].bitcast(U32) for o, n in ((256, 8), (264, NB - NE), (288, NB)))
        t_pos = p.cp(pos_i, pos)
        one_read, t_ids, t_one = [x_read], {}, {}

        def match(r, k0, k1, c0=0, c1=S):
            for k in range(k0, k1):
                if k == 0 and r > 0:
                    p.ts(rel, pos, float(512 * r), None, SB, None)
                t_one[r] = p.ts(onehot[:, k, c0:c1], slot[:, c0:c1], (rel if r else pos)[:, k:k + 1], None, ALU.is_equal,
                                None, t_slot, *one_read)

        def ids(r, b0, b1):
            for b in range(b0, b1):
                c = 128 * (b - 4 * r)
                for k in range(8):
                    m = p.mm(PB[7][:, b:b + 1], onehot[:, k, c:c + 128], tok16[:, k % 4:k % 4 + 1], k == 0, k == 7,
                             t_one[r], t_num, *self.fr[7], loose=True, sig=k == 7)
            one_read[0] = m
            t = p.cp(x_i[:, b0:b1], PB[7][:, b0:b1], m)
            for b in range(b0, b1):
                t_ids[b] = t

        t_x, gu_read, dn_read, xg_read, y_done = {}, {}, {}, {}, {}

        def load(b, to, table, name, read):
            if b < NE:
                return p.dma("sp", to[b % 3], self.ins[table][128 * b:128 * b + 128, :], *self.turn_of(f"{name}{b % 3}"),
                             [read[b - 3]])
            return p.gather(to[b % 3], self.ins[table], w_i[:, b - NE:b - NE + 1], *self.turn_of(f"more_{name}{b % 3}"),
                            t_w, read[b - 3])

        def load_gu(b):
            if b < NB:
                t_gu[b] = load(b, gu, f"moe_up{layer}", "u", gu_read)

        def load_dn(b):
            if b < NB:
                t_dn[b] = load(b, dn, f"moe_down{layer}", "d", dn_read)

        def load_x(b):
            if b < NB:
                t_x[b] = p.gather(xg[b % 2], rows_d, x_i[:, b:b + 1], *self.turn_of(f"x{b % 2}"), t_ids[b],
                                  xg_read.get(b - 2), *t_row)

        xT_tok, xT_read, hid_tok, h_read, hT_tok, hT_read, sl_tok = {}, {}, {}, {}, {}, {}, {}

        def turn(b):
            got = []
            for half in range(2):
                for i in range(4):
                    m = p.tr(PB[half][:, 128 * i:128 * i + 128], xg[b % 2][:, 512 * half + 128 * i:512 * half + 128 * i + 128],
                             self.cst("ident"), t_x[b], *(self.fr[half] if i == 0 else ()), sig=i == 3)
                dst = xT[b % 2][:, 512 * half:512 * half + 512]
                t = (p.act(dst, PB[0][:, :], ACT.Copy, m, xT_read.get(b - 2)) if half == 0
                     else p.cp(dst, PB[1][:, :], m, xT_read.get(b - 2)))
                self.fr[half] = (t,)
                got.append(t)
            xg_read[b] = m
            xT_tok[b] = tuple(got)

        def up(b):
            bank = 2 + b % 2
            m = p.group(PB[bank][:, :], [(xT[b % 2][:, 128 * k:128 * k + 128], gu[b % 3][:, 512 * k:512 * k + 512])
                                         for k in range(KT)], t_gu[b], xT_tok[b], *self.fr[bank])
            gu_read[b] = xT_read[b] = m
            s = p.act(sl[b % 2], PB[bank][:, 0:256], ACT.Silu, m, hid_tok.get(b - 2))
            hid_tok[b] = p.tt(hid[b % 2], sl[b % 2], PB[bank][:, 256:512], M, s, m, h_read.get(b - 2))
            self.fr[bank] = (hid_tok[b],)

        def turn_hid(b):
            for c in range(2):
                m = p.tr(PB[4][:, 128 * c:128 * c + 128], hid[b % 2][:, 128 * c:128 * c + 128], self.cst("ident"),
                         hid_tok[b], *(self.fr[4] if c == 0 else ()), sig=c == 1)
            h_read[b] = m
            hT_tok[b] = p.cp(hT[b % 2], PB[4][:, 0:256], m, hT_read.get(b - 2))
            self.fr[4] = (hT_tok[b],)

        def down(b):
            got = []
            for half in range(2):
                bank = 5 + half
                m = p.group(PB[bank][:, :], [(hT[b % 2][:, 128 * c:128 * c + 128],
                                              dn[b % 3][:, 1024 * c + 512 * half:1024 * c + 512 * half + 512])
                                             for c in range(2)], hT_tok[b], t_dn[b], *self.fr[bank])
                dst = yst[b % 2][:, 512 * half:512 * half + 512]
                t = (p.act(dst, PB[bank][:, :], ACT.Copy, m, x_read, y_done.get(b - 2)) if half == 0
                     else p.cp(dst, PB[bank][:, :], m, x_read, y_done.get(b - 2)))
                self.fr[bank] = (t,)
                got.append(t)
            hT_read[b] = dn_read[b] = m
            y_done[b] = p.dma("sp", out_d[128 * b:128 * b + 128, :], yst[b % 2], *self.turn_of(f"y{b % 2}"), got)

        match(0, 0, 8, 0, 128)
        ids(0, 0, 1)
        load_x(0)
        match(0, 0, 8, 128)
        ids(0, 1, 4)
        load_x(1)
        w_f = tile(NB - NE, wide=True)
        cmp_ = T[:, 47, 192:192 + 16 * (NB - NE)].rearrange("p (b e) -> p b e", b=NB - NE)
        for b in range(NB - NE):
            p.ts(cmp_[:, b, :], end, float(b), None, ALU.is_le, None)
        p.rsum(w_f, cmp_)
        p.ts(w_f, w_f, 15.0, 128.0, ALU.min, M)
        p.ts(w_f, w_f, tok[:, 0:1], None, A, None)
        t_w = p.cp(w_i, w_f)
        turn(0)
        for b in range(NB):
            up(b)
            load_gu(b + 3)
            r = (b + 2) // 4
            if b % 4 == 2 and 4 * r < NB:
                ids(r, 4 * r, min(4 * r + 4, NB))
            if b + 1 < NB:
                turn(b + 1)
            if b + 2 < NB:
                load_x(b + 2)
            if b > 0:
                down(b - 1)
                load_dn(b + 2)
            turn_hid(b)
            if b < 2:
                match(1, 4 * b, 4 * b + 4)
            elif 4 * (r + 1) < NB:
                k = 2 * ((b + 2) % 4)
                match(r + 1, k, k + 2)
        down(NB - 1)

        y = [self.flat(2 * i, 2 * i + 2, 1024) for i in range(8)]
        z = [self.flat(16 + 2 * q, 18 + 2 * q, 1024) for q in range(4)]
        st = [sm[:, 312 + i:313 + i] for i in range(4)]
        junk = self.flat(24, 26, 1024)
        row = 2 * layer + 1
        lastm = p.last["pe"]
        first, sums = {}, []
        for q in range(4):
            for k in range(2):
                n = 2 * q + k
                first[n] = p.gather(y[n], out_d, pos_i[:, 4 * k + q:4 * k + q + 1], *self.turn_of(f"g{n}"), t_pos, lastm,
                                    y_done[NB - 1], y_done[NB - 2])
        mu, var, rs, neg = (sm[:, o:o + 4] for o in (80, 84, 88, 92))
        def weigh(q):
            a, c = y[2 * q], y[2 * q + 1]
            t = p.act(a, a, ACT.Identity, first[2 * q], t_v, scale=v1[:, q:q + 1])
            t = p.stt(a, c, v2[:, q:q + 1], a, M, A, first[2 * q + 1], t)
            sums.append(p.stt(z[q], xrow[:, q, :], ALPHA, a, M, A, t))

        weigh(0)
        for q in range(4):
            if q < 3:
                weigh(q + 1)
            t = p.act(junk, z[q], ACT.Identity, sums[q], total=mu[:, q:q + 1])
            t = p.act(neg[:, q:q + 1], mu[:, q:q + 1], ACT.Copy, t, scale=-1.0 / D)
            t = p.act(junk, z[q], ACT.Square, t, bias=neg[:, q:q + 1], total=var[:, q:q + 1])
        t_rs = self.rstd(rs, var, D, self.col("eps5"), 128, t)
        for q in range(4):
            t = p.ts(z[q], z[q], neg[:, q:q + 1], rs[:, q:q + 1], A, M, t_rs)
            for i in range(KT):
                m = p.tr(PB[i][:, 128 * q:128 * q + 128], z[q][:, 128 * i:128 * i + 128], self.cst("ident"), t,
                         *(self.fr[i] if q == 0 else ()), sig=q == 3)
                if q == 3:
                    self.fr[i] = (m,)
        s, inv = self.sc[:, 68 + row:69 + row], self.sc[:, 76 + row:77 + row]
        hi = [self.AS[:, i, :] for i in range(KT)]
        lo = [self.AS[:, KT + i, :] for i in range(KT)]
        got = []
        for i in range(KT):
            w = (*self.fr[i], y_done[NB - 1], y_done[NB - 2])
            g, o = self.col("lng", 8 * row + i), self.col("lnb", 8 * row + i)
            t = (p.act(X[:, i, :], PB[i][:, :], ACT.Identity, *w, scale=g, bias=o) if i % 2 == 0
                 else p.ts(X[:, i, :], PB[i][:, :], g, o, M, A, *w))
            self.fr[i] = (t,)
            if row == 3:
                self.x_tok[i] = (t,)
            if row < 3:
                a = p.act(hi[i], X[:, i, :], ACT.Identity, t, self.t_gain, scale=s)
                got.append(p.stt(lo[i], X[:, i, :], s, hi[i], M, SB, a, t))
        if row == 3:
            return None
        self.settle()
        return Split(hi, lo, got, inv, self.t_gain)

    def odd1(self, act):
        p, X, H, WK, PB, sm = self.p, self.X, self.H, self.WK, self.PB, self.small
        xs = [X[:, i, :] for i in range(KT)]
        M, A, SB, MX = ALU.mult, ALU.add, ALU.subtract, ALU.max
        qk = [WK[:, i, :] for i in range(16)]
        vv = WK[:, 16:24, :].rearrange("p (q a) b -> p q (a b)", q=4)
        og = [WK[:, i, :] for i in range(24, 32)]

        wg = self.flat(41, 42, 512).rearrange("p (k e) -> p k e", k=8)
        tw = self.side("w_mgate", self.flat(41, 42, 512))
        tap = [sm[:, 32 + 16 * i:48 + 16 * i].rearrange("p (j t) -> p j t", j=4) for i in range(2)]

        def begin(t0, t1, sc, t_sc):
            w = tap[(t0 // 4) % 2]
            c = COL["mcw"][0]
            src = self.cols[:, c:c + 64].rearrange("p (j t) -> p j t", j=4)[:, :, t0:t0 + 4]
            return w, p.ts(w, src, sc, None, M, None, t_sc, *self.evac.get(self.at - 3, ()))

        gates = []

        def conv(i, b, m, sc, extra):
            ps, c = PB[b], qk[i]
            w = [extra[0][:, j, i % 4:i % 4 + 1] for j in range(4)]
            if i == 2:
                gates.append(p.group(PB[4][0:64, :], [(wg[:, k, :], xs[k]) for k in range(KT)], tw, *self.fr[4]))
            if 5 <= i < 13:
                self.grow(i - 5, gates[0], *act.ready)
            a = p.act(c, ps[:, :], ACT.Identity, m, extra[1], scale=w[3], bias=self.col("mcb", i))
            for j in range(3):
                s = 3 - j
                a = p.stt(c[:, s:S], ps[:, 0:S - s], w[j], c[:, s:S], M, A, a)
            p.act(c, c, ACT.Silu, a)
            return (a,)

        self.project("w_in_odd_2", 0, 16, KT, act, (0, 1, 2, 3), conv, begin)
        m = m_g = gates[0]
        ig, z, t1, t2, F_, a_, mx, en = (WK[0:8, 32 + i, :] for i in range(8))
        one = WK[0:8, 40, :]
        t_one = p.memset(one, 1.0)
        t_i = p.ts(ig, PB[4][0:8, :], self.col("ib", 0, 0, 8), None, A, None, m)
        t = p.act(z, PB[4][32:40, :], ACT.Identity, m, bias=self.col("fb", 0, 32, 40))
        self.fr[4] = (t, t_i)
        t = self.log_sigmoid(z, z, t1, t2, (t,))
        p.scan(F_, one, z, 0.0, M, A, t, t_one)
        p.tt(a_, ig, F_, SB)
        t_mx = p.scan(mx, a_, a_, 0.0, MX, MX)
        t = p.tt(t1, F_, mx, A)
        t_fm = t
        sel = self.flat(40, 42, 1024, 8)
        t_sel = []

        def use_v(n, q, b, m, s_):
            return (p.act(vv[:, q, 512 * n:512 * n + 512], PB[b][:, :], ACT.Identity, m, scale=s_),)

        self.project_rows("w_in_odd_2", 16, 8, act, (0, 1, 2, 3), use_v)
        t_en = p.act(en, t1, ACT.Exp, t_fm, scale=-1.0)

        def use_o(i, b, m, s_, x):
            if i == 28:
                t_sel.append(self.side("sel8", sel, t_en, m_g))
            return (p.act(og[i - 24], PB[b][:, :], ACT.Sigmoid, m, scale=s_),)

        self.project("w_in_odd_2", 24, 8, KT, act, (0, 1, 2, 3), use_o)
        ac = sm[:, 0:32].rearrange("p (j h) -> p j h", j=4)
        for j in range(4):
            m = p.tr(PB[5][:, 8 * j:8 * j + 8], a_[:, 128 * j:128 * j + 128], self.cst("ident", 8, 0, 8), t_mx,
                     *self.fr[5], sig=j == 3)
        t_ac = p.cp(ac, PB[5][:, 0:32].rearrange("p (j h) -> p j h", j=4), m)
        self.fr[5] = (t_ac,)
        self.barrier()
        wide = self.AS[:, :, :].rearrange("p a b -> p (a b)").bitcast(F32).rearrange("p (t s) -> p t s", t=8)
        dd = [wide[:, i, :] for i in range(3)]
        stt_ = [WK[:, i, :] for i in (34, 35, 36)]
        sc = 128.0 ** -0.5
        dread, sread = [()] * 3, [()] * 3
        t_d, t_s, m_b, last = {}, {}, {}, {}
        mbank, nbank = (6, 7), (3, 4)

        def bound(h):
            mb = mbank[h % 2]
            m_b[h] = p.mm(PB[mb][:, :], sel[:, 128 * h:128 * h + 128], mx, True, True, *t_sel, *self.fr[mb], sig=True)

        def decay(n):
            h, j = n // 4, n % 4
            lo, d, mb = 128 * j, dd[n % 3], mbank[h % 2]
            t = p.ts(d[:, lo:S], PB[mb][:, lo:S], ac[:, j, h:h + 1], 0.0, SB, MX, m_b[h], *dread[n % 3])
            self.fr[mb] = (t,)
            t = p.act(d[:, lo:S], d[:, lo:S], ACT.Exp, t, scale=-1.0)
            t_d[n] = p.tt(d[:, lo:lo + 128], d[:, lo:lo + 128], self.cst("causal"), M, t, eng="pool")

        def score(n):
            h, j = n // 4, n % 4
            lo, d, st, b = 128 * j, dd[n % 3], stt_[n % 3], n % 3
            m = p.mm(PB[b][:, lo:S], qk[8 + h][:, lo:lo + 128], qk[h][:, lo:S], True, True, *self.fr[b], sig=True)
            t = p.stt(st[:, lo:S], PB[b][:, lo:S], sc, d[:, lo:S], M, M, m, t_d[n], *sread[n % 3])
            self.fr[b] = dread[n % 3] = (t,)
            t_s[n] = t

        def value(n):
            h, j = n // 4, n % 4
            lo, st, nb = 128 * j, stt_[n % 3], nbank[h % 2]
            p.mm(PB[nb][:, lo:S], vv[:, j, 128 * h:128 * h + 128], st[:, lo:S], j == 0, j == 3, t_s[n],
                 *(self.fr[nb] if j == 0 else ()), loose=True)
            last[n] = m = p.mm(PB[5][0:8, lo:S], self.cst("oh", 128, 8 * h, 8), st[:, lo:S], h == 0 and j == 0,
                               h == 7 and j == 3, sig=True, loose=True)
            sread[n % 3] = (m,)

        bound(0)
        for n in range(35):
            if n < 32:
                if n % 4 == 2 and n < 28:
                    bound(n // 4 + 1)
                decay(n)
            if 1 <= n <= 32:
                score(n - 1)
            if 2 <= n <= 33:
                value(n - 2)
            if n >= 6 and n % 4 == 2:
                h = (n - 6) // 4
                t = p.tt(H[:, h, :], PB[nbank[h % 2]][:, :], og[h], M, last[4 * h + 3])
                self.fr[nbank[h % 2]] = (t,)
        den = WK[0:8, 37, :]
        t = p.act(den, PB[5][0:8, :], ACT.Abs, last[31])
        p.tt(den, den, en, MX, p.last["act"], t_en)
        t = p.recip(den, den)
        for h in range(8):
            mb = 6 + h % 2
            m = p.mm(PB[mb][:, :], sel[:, 128 * h:128 * h + 128], den, True, True, t, *self.fr[mb], sig=True)
            x = p.tt(H[:, h, :], H[:, h, :], PB[mb][:, :], M, m)
            self.fr[mb] = (x,)
            t_q = self.square_sum(h, H[:, h, :], x)
        weights = self.moe_weights(1)
        self.add_out("w_out_odd_2", self.parts([H[:, i, :] for i in range(KT)], measured=t_q), then="mean")
        self.barrier()
        self.layernorm(2)
        return weights

    PHASES = ("even0", "ffn0", "odd0", "ffn1", "even1", "moe0", "odd1", "moe1")

    def finish(self):
        p = self.p
        now = [] if all(self.x_tok) else [p.last[k] for k in ("pe", "act", "dve", "pool") if p.last[k] is not None]
        out = self.out.rearrange("(t p) s -> p t s", p=128)
        done = []
        for i in range(0, KT, 2):
            after = [x for tok in self.x_tok[i:i + 2] for x in tok]
            done.append(p.dma("sp", out[:, i:i + 2, :], self.X[:, i:i + 2, :], self.sem(f"dout{i}"), 16, now + after))
        p.wait_all("sp", done)
        with self.nc.Block() as block:
            @block.sync
            def _(e):
                p.run("sp", e)

            @block.tensor
            def _(e):
                p.run("pe", e)

            @block.scalar
            def _(e):
                p.run("act", e)

            @block.vector
            def _(e):
                p.run("dve", e)

            @block.gpsimd
            def _(e):
                p.run("pool", e)


def build(nc, ins, out, phases=Build.PHASES):
    b = Build(nc, ins, out)
    with b.ctx:
        b.setup(phases)
        act = weights = None
        for name in phases:
            if name in ("ffn0", "ffn1"):
                b.ffn(int(name[3]))
            elif name == "even0":
                b.even0()
            elif name == "odd0":
                b.odd0()
            elif name == "even1":
                weights = b.even1()
            elif name == "odd1":
                weights = b.odd1(act or b.given())
            else:
                act = b.moe(int(name[3]), weights)
                weights = None
        b.finish()


def tiles_of(w, order=None):
    k, n = w.shape
    nt = -(-n // 128)
    out = np.zeros((k, nt * 128), w.dtype)
    out[:, :n] = w
    out = out.reshape(k // 128, 128, nt, 128).transpose(2, 1, 0, 3)
    return np.ascontiguousarray(out if order is None else out[order])


def pair_up(a, b):
    ta, tb = tiles_of(a), tiles_of(b)
    return np.ascontiguousarray(np.stack([ta, tb], 1).reshape(-1, *ta.shape[1:]))


def rows_of(w):
    k, n = w.shape
    return np.ascontiguousarray(w.reshape(k // 128, 128, n).transpose(1, 0, 2))


def constants():
    c = np.zeros((128, NCST), np.float32)

    def at(name):
        a, w = CST[name]
        return c[:, a:a + w]

    i = np.arange(128)
    at("ident")[:] = np.eye(128)
    at("nident")[:] = -np.eye(128)
    at("ones")[:] = 1
    at("bd64")[:] = i[:, None] // 64 == i[None] // 64
    for name, lo, hi, size, half in (("rot64", 0, 128, 64, 32), ("rot96", 64, 96, 32, 16)):
        m = at(name)
        for o in range(lo, hi):
            if (o - lo) % size < half:
                m[o + half, o] = -1
            else:
                m[o - half, o] = 1
    at("maskn")[:] = np.where(i[None] > i[:, None], np.float32(-1e30), 0)
    at("maskt")[:] = np.where(i[:, None] > i[None], np.float32(-1e30), 0)
    same = i[:, None] // 64 == i[None] // 64
    at("mf")[:] = same & (i[:, None] <= i[None])
    at("mb")[:] = same & (i[:, None] > i[None])
    at("causal")[:] = i[:, None] <= i[None]
    for h in range(8):
        at("oh")[:, 8 * h + h] = 1
    return c


def selectors():
    sel = np.zeros((8, 8 * 128), np.float32)
    fox = np.zeros((8, 8 * 128), np.float32)
    for h in range(8):
        sel[h, 128 * h:128 * h + 128] = 1
        fox[h, 128 * h + 64] = 1
        fox[h, 128 * h + 96] = -1
    return sel, fox


def layout(**a):
    f32 = np.float32
    a = {k: np.asarray(v) for k, v in a.items()}
    out = {}
    out["xT"] = np.ascontiguousarray(a["x"][0].T)
    out["posb"] = np.ascontiguousarray(np.broadcast_to(a["positions"].reshape(1, S), (128, S)))
    out["csts"] = constants()
    out["sel8"], out["foxsel"] = selectors()
    cols = np.zeros((128, NCOL), f32)

    def put(name, v, i=0):
        v = np.asarray(v).reshape(-1)
        n = -(-v.size // 128)
        full = np.zeros(n * 128, f32)
        full[:v.size] = v
        c = COL[name][0] + i
        cols[:, c:c + n] = full.reshape(n, 128).T

    put("mix_even", a["mix_norm_even"])
    put("q_norm", a["mla_q_norm"])
    put("kv_norm", a["mla_kv_norm"])
    put("qhn", a["mla_q_head_norm"])
    put("khn", a["mla_k_head_norm"])
    put("ret_norm", a["ret_out_norm"])
    for name, v, n in (("th_f", a["ret_theta_fwd"][0], 8), ("th_b", a["ret_theta_bwd"][0], 8)):
        cols[:, COL[name][0]:COL[name][0] + n] = v[None]
    put("mix_odd", a["mix_norm_odd"])
    put("gb_f", a["gla_b_gate_fwd"])
    put("gb_b", a["gla_b_gate_bwd"])
    put("gla_norm", a["gla_out_norm"])
    for l in range(2):
        put(f"ffn{l}", a["ffn_norm"][l])
        put(f"cw{l}", a["ffn_conv_w"][l])
        put(f"cb{l}", a["ffn_conv_b"][l])
        c = COL[f"mb{l}"][0]
        cols[:, c:c + 4] = a["moe_b_group_2"][l][None]
        cols[:, c + 4:c + 20] = a["moe_b_expert_2"][l].reshape(1, 16)
    put("lng", a["ln_g_2"])
    put("lnb", a["ln_b_2"])
    put("fox_fb", a["fox_f_bias_2"])
    put("a_re", a["s5_a_re_2"])
    put("a_im", a["s5_a_im_2"])
    put("log_dt", np.repeat(a["s5_log_dt_2"].reshape(32), 64))
    put("s5_d", a["s5_d_2"])
    put("b_glu", a["s5_b_glu_2"])
    put("mcw", a["mlstm_conv_w_2"])
    put("mcb", a["mlstm_conv_b_2"])
    put("ib", a["mlstm_i_bias_2"])
    cols[32:40, COL["fb"][0]] = a["mlstm_f_bias_2"][0]
    inv32 = (f32(10000.0) ** (-np.arange(32, dtype=f32) / f32(32))).astype(f32)
    inv16 = (f32(10000.0) ** (-np.arange(16, dtype=f32) / f32(16))).astype(f32)
    cols[:, COL["inv64"][0]] = np.tile(inv32, 4)
    cols[64:96, COL["inv96"][0]] = np.tile(inv16, 2)
    cols[:, COL["eps6"][0]] = 1e-6
    cols[:, COL["eps5"][0]] = 1e-5
    cols[:, COL["halfpi"][0]] = np.pi / 2
    cols[:, COL["one"][0]] = 1
    out["cols"] = cols

    w = a["w_in_even"][0]
    cut = np.cumsum([0, 384, 256, 32, 512, 512, 512, 512])
    cq, ckv, kro, rq, rk, rv, rg = (w[:, cut[i]:cut[i + 1]] for i in range(7))
    out["w_in_even"] = np.concatenate([tiles_of(x) for x in (cq, kro, rv, rg, rq, rk, ckv)])
    out["w_uq"] = np.ascontiguousarray(a["mla_w_uq"][0].reshape(3, 128, 8, 96).transpose(1, 2, 0, 3)).reshape(128, -1)
    kv = a["mla_w_ukv"][0].reshape(2, 128, 8, 2, 64).transpose(1, 3, 0, 2, 4)
    out["w_ukv"] = np.ascontiguousarray(kv).reshape(128, -1)
    out["w_out_even"] = tiles_of(a["w_out_even"][0])
    w = a["w_in_odd"][0]
    out["w_odd_qk"] = tiles_of(np.concatenate([w[:, :1024], w[:, 3072:]], 1))
    out["w_odd_v"] = tiles_of(w[:, 1024:3072])
    g = np.zeros((32, 2, 512), f32)
    g[0:16, 0] = a["gla_w_gate_fwd"][0]
    g[16:32, 1] = a["gla_w_gate_bwd"][0]
    out["w_gate"] = g.reshape(32, -1)
    out["w_out_odd"] = tiles_of(a["w_out_odd"][0])
    for l in range(2):
        up = a["ffn_w_up"][l]
        out[f"w_up{l}"] = pair_up(up[:, :2816], up[:, 2816:])
        out[f"w_down{l}"] = tiles_of(a["ffn_w_down"][l])
        wr = np.concatenate([a["moe_w_group_2"][l], a["moe_w_expert_2"][l].transpose(1, 0, 2).reshape(D, 16)], 1)
        out[f"w_route{l}"] = rows_of(wr).reshape(128, -1)
        up = np.concatenate([a["moe_w_gate_2"][l], a["moe_w_up_2"][l]], 2).reshape(16, 8, 128, 512)
        out[f"moe_up{l}"] = np.ascontiguousarray(up.transpose(0, 2, 1, 3)).reshape(16 * 128, 4096)
        down = a["moe_w_down_2"][l].reshape(16, 2, 128, 1024)
        out[f"moe_down{l}"] = np.ascontiguousarray(down.transpose(0, 2, 1, 3)).reshape(16 * 128, 2048)
    w = a["even_w_in_2"][0]
    out["w_in_even_2"] = tiles_of(np.concatenate([w[:, 0:1536], w[:, 1544:2056]], 1))
    out["w_fox_f"] = rows_of(w[:, 1536:1544]).reshape(128, -1)
    for name, v in (("s5_br", a["s5_b_re_2"][0]), ("s5_bi", a["s5_b_im_2"][0])):
        m = np.zeros((16, 2, 64, 2, 16), f32)
        for g2 in range(2):
            m[:, g2, :, g2, :] = v[g2::2]
        out[name] = np.ascontiguousarray(m.transpose(1, 2, 0, 3, 4)).reshape(128, -1)
    for name, v in (("s5_cr", a["s5_c_re_2"][0]), ("s5_ci", a["s5_c_im_2"][0])):
        m = np.zeros((2, 64, 16, 32), f32)
        for g2 in range(2):
            m[g2, :, :, 16 * g2:16 * g2 + 16] = v[g2::2].transpose(2, 0, 1)
        out[name] = m.reshape(128, -1)
    out["w_glu"] = tiles_of(a["s5_w_glu_2"][0])
    out["w_out_even_2"] = tiles_of(a["even_w_out_2"][0])
    w = a["odd_w_in_2"][0]
    out["w_in_odd_2"] = tiles_of(w[:, :4096])
    g = np.zeros((D, 64), f32)
    g[:, 0:8] = w[:, 4096:4104]
    g[:, 32:40] = w[:, 4104:4112]
    out["w_mgate"] = rows_of(g).reshape(128, -1)
    out["w_out_odd_2"] = tiles_of(a["odd_w_out_2"][0])
    return out


def kernel(**inputs):
    import concourse.bacc as bacc
    from concourse.bass_utils import run_bass_kernel_spmd

    arrays = layout(**inputs)
    nc = bacc.Bacc("TRN2", target_bir_lowering=False, num_devices=1)
    ins = {k: nc.dram_tensor(f"in_{k}", v.shape, mybir.dt.from_np(v.dtype), kind="ExternalInput").ap()
           for k, v in arrays.items()}
    out = nc.dram_tensor("outT", (D, S), F32, kind="ExternalOutput").ap()
    build(nc, ins, out)
    r = run_bass_kernel_spmd(nc, [{f"in_{k}": v for k, v in arrays.items()}], core_ids=[0])
    return np.ascontiguousarray(r.results[0]["outT"].T)[None]
```
